# Optimizing a Trainium2 kernel written in Bass

```python
import math
import jax
import jax.numpy as jnp
from jax import lax
import numpy as np

D_MODEL = 1024
BATCH = 1
SEQ = 512
DEPTH = 2

N_EVEN = (DEPTH + 1) // 2
N_ODD = DEPTH // 2
EPS = 1e-6
TINY = 1e-20
D_FF = 2816

HG_DK = 128
HG_DV = 128
HG_HEADS = D_MODEL // HG_DK
HG_WIDTH = HG_HEADS * HG_DV
HG_CHUNK = 64

SSD_INNER = D_MODEL
SSD_P = 64
SSD_HEADS = SSD_INNER // SSD_P
SSD_N = 128
SSD_G = 4
SSD_R = SSD_HEADS // SSD_G
SSD_CONV = 4
SSD_CHUNK = 128
SSD_XBC = SSD_INNER + 2 * SSD_G * SSD_N
DT_MIN = 1e-3
DT_MAX = 1e-1

HYB_SIZES = (HG_HEADS * HG_DK, HG_HEADS * HG_DK, HG_WIDTH, HG_WIDTH, SSD_INNER, SSD_XBC, SSD_HEADS)
HYB_IN = sum(HYB_SIZES)
HYB_SPLITS = tuple(sum(HYB_SIZES[:i + 1]) for i in range(len(HYB_SIZES) - 1))
HYB_OUT = HG_WIDTH + SSD_INNER

FOX_HD = 64
FOX_HEADS = D_MODEL // FOX_HD
FOX_WIDTH = FOX_HEADS * FOX_HD
FOX_SIZES = (FOX_WIDTH, FOX_WIDTH, FOX_WIDTH, FOX_HEADS)
FOX_IN = sum(FOX_SIZES)
FOX_SPLITS = tuple(sum(FOX_SIZES[:i + 1]) for i in range(len(FOX_SIZES) - 1))
Q_BLOCK = 128
NEG_INF = -1e30

kernel_name = "hybrid_hgrn2_ssd_fox_macaron"

def rmsnorm(x, g):
    xf = x.astype(jnp.float32)
    y = xf * lax.rsqrt(jnp.mean(xf * xf, axis=-1, keepdims=True) + EPS)
    return (y * g.astype(jnp.float32)).astype(x.dtype)

def swiglu(u, w_gate, w_up, w_down):
    return (jax.nn.silu(u @ w_gate) * (u @ w_up)) @ w_down

def causal_dwconv(u, w, b):
    k_w = w.shape[0]
    out = lax.conv_general_dilated(u, w.astype(u.dtype)[:, None, :], window_strides=(1,),
                                   padding=[(k_w - 1, 0)],
                                   dimension_numbers=('NWC', 'WIO', 'NWC'),
                                   feature_group_count=u.shape[-1])
    return out + b.astype(u.dtype)

def seg_decay(a):
    n = a.shape[-1]
    cs = jnp.cumsum(a, axis=-1)
    diff = cs[..., :, None] - cs[..., None, :]
    mask = jnp.tril(jnp.ones((n, n), dtype=bool))
    return jnp.where(mask, jnp.exp(jnp.where(mask, diff, 0.0)), 0.0)

def hgrn2_mixer(q, f_logit, inp, g, lb, out_gain):
    bsz, s, _ = q.shape
    nc = s // HG_CHUNK
    lb = lb.astype(jnp.float32)
    f = lb + (1.0 - lb) * jax.nn.sigmoid(f_logit)
    log_f = jnp.log(jnp.maximum(f, TINY))
    k = (1.0 - lb) * jax.nn.sigmoid(-f_logit)

    def chunks(t, d):
        return t.reshape(bsz, nc, HG_CHUNK, HG_HEADS, d).transpose(1, 0, 3, 2, 4)

    causal = jnp.tril(jnp.ones((HG_CHUNK, HG_CHUNK), dtype=bool))[:, :, None]

    def step(state, blk):
        qb, kb, lfb, vb = blk
        b = jnp.cumsum(lfb, axis=2)
        diff = b[:, :, :, None, :] - b[:, :, None, :, :]
        decay = jnp.where(causal, jnp.exp(jnp.where(causal, diff, 0.0)), 0.0)
        scores = jnp.einsum('bhtd,bhtsd,bhsd->bhts', qb, decay, kb)
        o = (jnp.einsum('bhts,bhsv->bhtv', scores, vb)
             + jnp.einsum('bhtd,bhdv->bhtv', qb * jnp.exp(b), state))
        b_last = b[:, :, -1:, :]
        state = (jnp.exp(b_last[:, :, 0, :])[..., None] * state
                 + jnp.einsum('bhsd,bhsv->bhdv', kb * jnp.exp(b_last - b), vb))
        return state, o

    state0 = jnp.zeros((bsz, HG_HEADS, HG_DK, HG_DV), jnp.float32)
    _, o = lax.scan(step, state0, (chunks(q, HG_DK), chunks(k, HG_DK), chunks(log_f, HG_DK), chunks(inp, HG_DV)))
    o = o.transpose(1, 0, 3, 2, 4).reshape(bsz, s, HG_HEADS, HG_DV)
    o = o * lax.rsqrt(jnp.mean(o * o, axis=-1, keepdims=True) + EPS)
    return o.reshape(bsz, s, HG_WIDTH) * out_gain.astype(jnp.float32) * jax.nn.silu(g)

def ssd_mixer(z, xbc, dt_raw, conv_w, conv_b, dt_bias, a_log, d_skip, out_gain):
    bsz, s, _ = z.shape
    nc = s // SSD_CHUNK
    f32 = jnp.float32
    xbc = jax.nn.silu(causal_dwconv(xbc, conv_w.astype(f32), conv_b.astype(f32)))
    xs, bm, cm = jnp.split(xbc, (SSD_INNER, SSD_INNER + SSD_G * SSD_N), axis=-1)
    dt = jax.nn.softplus(dt_raw + dt_bias.astype(f32))
    a_head = -jnp.exp(a_log.astype(f32)).reshape(SSD_G, SSD_R)

    x_c = xs.reshape(bsz, nc, SSD_CHUNK, SSD_G, SSD_R, SSD_P)
    b_c = bm.reshape(bsz, nc, SSD_CHUNK, SSD_G, SSD_N)
    c_c = cm.reshape(bsz, nc, SSD_CHUNK, SSD_G, SSD_N)
    dt_c = dt.reshape(bsz, nc, SSD_CHUNK, SSD_G, SSD_R)
    xdt = x_c * dt_c[..., None]
    a = (dt_c * a_head).transpose(0, 3, 4, 1, 2)
    a_cs = jnp.cumsum(a, axis=-1)

    cb = jnp.einsum('bclgn,bcsgn->bgcls', c_c, b_c)
    m = cb[:, :, None] * seg_decay(a)
    y_diag = jnp.einsum('bgrcls,bcsgrp->bclgrp', m, xdt)

    decay_states = jnp.exp(a_cs[..., -1:] - a_cs)
    states = jnp.einsum('bclgn,bgrcl,bclgrp->bcgrpn', b_c, decay_states, xdt)
    states = jnp.concatenate([jnp.zeros_like(states[:, :1]), states], axis=1)
    chunk_tot = jnp.pad(a_cs[..., -1], ((0, 0), (0, 0), (0, 0), (1, 0)))
    decay_chunk = seg_decay(chunk_tot)
    states = jnp.einsum('bgrzc,bcgrpn->bzgrpn', decay_chunk, states)[:, :-1]
    y_off = jnp.einsum('bclgn,bcgrpn,bgrcl->bclgrp', c_c, states, jnp.exp(a_cs))

    y = (y_diag + y_off).reshape(bsz, s, SSD_HEADS, SSD_P)
    y = y + xs.reshape(bsz, s, SSD_HEADS, SSD_P) * d_skip.astype(f32)[:, None]
    y = y.reshape(bsz, s, SSD_INNER) * jax.nn.silu(z)
    y = y * lax.rsqrt(jnp.mean(y * y, axis=-1, keepdims=True) + EPS)
    return y * out_gain.astype(f32)

def hybrid_hgrn2_ssd(u, w_in, lb, hg_gain, conv_w, conv_b, dt_bias, a_log, d_skip, ssd_gain, w_out):
    proj = (u @ w_in).astype(jnp.float32)
    q, f_logit, inp, g, z, xbc, dt_raw = jnp.split(proj, HYB_SPLITS, axis=-1)
    o_a = hgrn2_mixer(q, f_logit, inp, g, lb, hg_gain)
    o_b = ssd_mixer(z, xbc, dt_raw, conv_w, conv_b, dt_bias, a_log, d_skip, ssd_gain)
    o = jnp.concatenate([o_a, o_b], axis=-1).astype(u.dtype)
    return o @ w_out

def fox_attention(u, w_in, b_f, w_out):
    bsz, s, _ = u.shape
    f32 = jnp.float32
    proj = (u @ w_in).astype(f32)
    q, k, v, f_logit = jnp.split(proj, FOX_SPLITS, axis=-1)

    def heads(t):
        return t.reshape(bsz, s, FOX_HEADS, FOX_HD).transpose(0, 2, 1, 3)

    q = heads(q) * (FOX_HD ** -0.5)
    k = heads(k)
    v = heads(v)
    log_f = jax.nn.log_sigmoid(f_logit + b_f.astype(f32))
    cum = jnp.cumsum(log_f, axis=1).transpose(0, 2, 1)
    nb = s // Q_BLOCK
    q_blocks = q.reshape(bsz, FOX_HEADS, nb, Q_BLOCK, FOX_HD).transpose(2, 0, 1, 3, 4)
    cum_blocks = cum.reshape(bsz, FOX_HEADS, nb, Q_BLOCK).transpose(2, 0, 1, 3)
    k_pos = jnp.arange(s)

    def block(args):
        qi, ci, start = args
        logits = jnp.einsum('bhqd,bhkd->bhqk', qi, k) + ci[..., None] - cum[:, :, None, :]
        q_pos = start + jnp.arange(Q_BLOCK)
        logits = jnp.where(k_pos[None, :] <= q_pos[:, None], logits, NEG_INF)
        p = jax.nn.softmax(logits, axis=-1)
        return jnp.einsum('bhqk,bhkd->bhqd', p, v)

    o = lax.map(block, (q_blocks, cum_blocks, jnp.arange(nb) * Q_BLOCK))
    o = o.transpose(1, 0, 3, 2, 4).reshape(bsz, s, FOX_WIDTH).astype(u.dtype)
    return o @ w_out

def setup_inputs(seed: int = 0) -> dict:
    key = jax.random.key(seed)
    ks = jax.random.split(key, 24)
    f32 = jnp.float32

    def nrm(k, shape, fan_in):
        return jax.random.normal(k, shape, f32) * (fan_in ** -0.5)

    def gain(k, shape):
        return 1.0 + 0.02 * jax.random.normal(k, shape, f32)

    dt = jnp.exp(jax.random.uniform(ks[11], (N_EVEN, SSD_HEADS), f32, math.log(DT_MIN), math.log(DT_MAX)))
    return {
        "x": jax.random.normal(ks[0], (BATCH, SEQ, D_MODEL), f32),
        "ffn1_norm": gain(ks[1], (DEPTH, D_MODEL)),
        "ffn1_w_gate": nrm(ks[2], (DEPTH, D_MODEL, D_FF), D_MODEL),
        "ffn1_w_up": nrm(ks[3], (DEPTH, D_MODEL, D_FF), D_MODEL),
        "ffn1_w_down": nrm(ks[4], (DEPTH, D_FF, D_MODEL), D_FF),
        "mix_norm": gain(ks[5], (DEPTH, D_MODEL)),
        "hyb_w_in": nrm(ks[6], (N_EVEN, D_MODEL, HYB_IN), D_MODEL),
        "hgrn_lb_logits": 0.5 * jax.random.normal(ks[7], (N_EVEN, HG_HEADS * HG_DK), f32),
        "hgrn_out_gain": gain(ks[8], (N_EVEN, HG_WIDTH)),
        "ssd_conv_w": nrm(ks[9], (N_EVEN, SSD_CONV, SSD_XBC), SSD_CONV),
        "ssd_conv_b": 0.02 * jax.random.normal(ks[10], (N_EVEN, SSD_XBC), f32),
        "ssd_dt_bias": dt + jnp.log(-jnp.expm1(-dt)),
        "ssd_A_log": jnp.log(jax.random.uniform(ks[12], (N_EVEN, SSD_HEADS), f32, 1.0, 16.0)),
        "ssd_D": gain(ks[13], (N_EVEN, SSD_HEADS)),
        "ssd_out_gain": gain(ks[14], (N_EVEN, SSD_INNER)),
        "hyb_w_out": nrm(ks[15], (N_EVEN, HYB_OUT, D_MODEL), HYB_OUT),
        "fox_w_in": nrm(ks[16], (N_ODD, D_MODEL, FOX_IN), D_MODEL),
        "fox_b_f": jax.random.uniform(ks[17], (N_ODD, FOX_HEADS), f32, 1.0, 6.0),
        "fox_w_out": nrm(ks[18], (N_ODD, FOX_WIDTH, D_MODEL), FOX_WIDTH),
        "ffn2_norm": gain(ks[19], (DEPTH, D_MODEL)),
        "ffn2_w_gate": nrm(ks[20], (DEPTH, D_MODEL, D_FF), D_MODEL),
        "ffn2_w_up": nrm(ks[21], (DEPTH, D_MODEL, D_FF), D_MODEL),
        "ffn2_w_down": nrm(ks[22], (DEPTH, D_FF, D_MODEL), D_FF),
        "final_norm": gain(ks[23], (D_MODEL,)),
    }

def reference(x, ffn1_norm, ffn1_w_gate, ffn1_w_up, ffn1_w_down, mix_norm,
              hyb_w_in, hgrn_lb_logits, hgrn_out_gain, ssd_conv_w, ssd_conv_b,
              ssd_dt_bias, ssd_A_log, ssd_D, ssd_out_gain, hyb_w_out,
              fox_w_in, fox_b_f, fox_w_out,
              ffn2_norm, ffn2_w_gate, ffn2_w_up, ffn2_w_down, final_norm):
    p = jax.nn.softmax(hgrn_lb_logits.astype(jnp.float32), axis=0)
    lower_bounds = jnp.cumsum(p, axis=0) - p[0]
    h = x
    for layer in range(DEPTH):
        j = layer // 2
        u = rmsnorm(h, ffn1_norm[layer])
        h = h + 0.5 * swiglu(u, ffn1_w_gate[layer], ffn1_w_up[layer], ffn1_w_down[layer])
        u = rmsnorm(h, mix_norm[layer])
        if layer % 2 == 0:
            mix = hybrid_hgrn2_ssd(u, hyb_w_in[j], lower_bounds[j], hgrn_out_gain[j],
                                   ssd_conv_w[j], ssd_conv_b[j], ssd_dt_bias[j], ssd_A_log[j],
                                   ssd_D[j], ssd_out_gain[j], hyb_w_out[j])
        else:
            mix = fox_attention(u, fox_w_in[j], fox_b_f[j], fox_w_out[j])
        h = h + mix.astype(h.dtype)
        u = rmsnorm(h, ffn2_norm[layer])
        h = h + 0.5 * swiglu(u, ffn2_w_gate[layer], ffn2_w_up[layer], ffn2_w_down[layer])
    return rmsnorm(h, final_norm)


_drawn_inputs = setup_inputs


def setup_inputs(seed=0):
    import zlib

    import numpy as np

    out = dict(_drawn_inputs(seed))
    spreads = {}
    factors = {'ffn1_norm': 3.436,
     'hgrn_out_gain': 81.688,
     'ssd_conv_b': 3.462,
     'ssd_D': 119.756,
     'ssd_out_gain': 46.218,
     'ffn2_norm': 6.448,
     'final_norm': 24.539,
     'fox_b_f': 33.76,
     'ssd_dt_bias': 2.932,
     'ssd_A_log': 5.01,
     'fox_w_in': 6.051,
     'fox_w_out': 6.059}
    for name, (base, spread) in spreads.items():
        noise = np.random.default_rng([zlib.crc32(name.encode()), seed]).standard_normal(out[name].shape)
        drawn = base * np.exp(spread * noise) if base else spread * noise
        out[name] = jnp.asarray(drawn.astype(out[name].dtype))
    for name, factor in factors.items():
        out[name] = (out[name] * factor).astype(out[name].dtype)
    return out
```

```python
from contextlib import ExitStack

import numpy as np

import concourse.bass as bass
from concourse import mybir
from concourse.alu_op_type import AluOpType as ALU

ACT = mybir.ActivationFunctionType
F32 = mybir.dt.float32
F32R = mybir.dt.float32r
U32 = mybir.dt.uint32
AX = mybir.AxisListType

P = 128
T = 512
D = 1024
KD = D // P
FF = 2816
CB = 256
NF = FF // CB
TC = T // P
EPS = 1e-6
HD = 64
HPB = CB // HD
NQ = D // CB
NH = D // HD
FOX_SMALL = 3 * D
BF16 = mybir.dt.bfloat16
NEG = -1e30
HEADS2 = 2
TINY = 1e-20
LOG_SPLIT = 2.0 ** -60
G4 = 4
SP_ = 64
CONV = 4
HYB_X, HYB_SMALL = 5 * D, 7 * D
SLOTS = 3


def affine(fn, i, lo, hi):
    if isinstance(i, int):
        return fn(i)
    vals = [fn(x) for x in range(lo, hi)]
    step = vals[1] - vals[0] if len(vals) > 1 else 0
    assert all(b - a == step for a, b in zip(vals, vals[1:])), vals
    base = vals[0] - lo * step
    out = i * step if step != 1 else i
    return out + base if base else out


def at_least(fn, own, i, lo, hi):
    if isinstance(i, int):
        return fn(i)
    vals = [fn(x) for x in range(lo, hi)]
    step = vals[-1] - vals[-2]
    base = max(y - step * x for x, y in zip(range(lo, hi), vals))
    assert all(base + step * x <= own(x) for x in range(lo, hi))
    return i * step + base


HG_LINKS, SSD_LINKS = 16, 12


class Links:

    def __init__(self, sem):
        self.sem, self.n, self.i, self.per = sem, 0, None, 0

    def enter(self, i, lo, per):
        self.i, self.lo, self.per, self.k = i, lo, per, 0

    def leave(self, trips):
        assert self.k == self.per, (self.k, self.per)
        self.n += trips * self.per
        self.i = None

    def step(self, eng, ins):
        ins.then_inc(self.sem, 1)
        if self.i is None:
            self.n += 1
            eng.wait_ge(self.sem, self.n)
        else:
            self.k += 1
            eng.wait_ge(self.sem, self.i * self.per + (self.n - self.lo * self.per + self.k))


class Blocks:

    def __init__(self):
        self.order, self.slot, self.nth, self.last_use = [], {}, {}, [-3, -2, -1]
        self.count = [0] * SLOTS
        self.prev = {}
        self.held = [None] * SLOTS
        self.landed, self.lands, self.next_lands = [0] * SLOTS, {}, {}

    def add(self, key, slot=None):
        if slot is None:
            slot = min(range(SLOTS), key=lambda s: self.last_use[s])
        self.slot[key], self.nth[key] = slot, self.count[slot]
        self.prev[key] = self.held[slot]
        self.held[slot] = key
        self.landed[slot] += 32 if key[0] == "sb" else 16
        self.lands[key] = self.next_lands[self.prev[key]] = self.landed[slot]
        self.last_use[slot] = len(self.order)
        self.count[slot] += 1
        self.order.append(key)

    def body(self, keys_at, lo, hi, first=None):
        for i in range(lo, hi):
            for j, key in enumerate(keys_at(i)):
                self.add(key, None if first is None else first[j])
            if first is None:
                first = [self.slot[k] for k in keys_at(i)]


def plan_blocks(parts):
    b = Blocks()
    for part in parts:
        if part[0] == "ffn":
            f = part[1]
            b.add(("g", f, 0)); b.add(("u", f, 0))
            b.body(lambda i: [("g", f, i), ("u", f, i), ("d", f, i - 1)], 1, NF)
            b.add(("d", f, NF - 1))
        if part[0] == "hyb":
            s0, s1, s2 = sorted(range(SLOTS), key=lambda s: b.last_use[s])
            for kind, at, s in (("hf", 0, s0), ("hq", 0, s1), ("hv", 0, s0), ("hg", 0, s2), ("hf", 1, s0), ("hq", 1, s1)):
                b.add((kind, 0, at), s)
            b.body(lambda i: [("hv", 0, i), ("hg", 0, i), ("hd", 0, i - 1), ("hf", 0, i + 1), ("hq", 0, i + 1)],
                   1, NQ - 1, [s0, s2, s1, s0, s1])
            for kind, at, s in (("hv", 3, s0), ("hg", 3, s2), ("hd", 2, s1), ("sx", 0, s0), ("sb", 0, s2), ("hd", 3, s1)):
                b.add((kind, 0, at), s)
            b.body(lambda i: [("sz", 0, i), ("sx", 0, i + 1), ("sb", 0, i + 1)], 0, G4 - 1)
            b.add(("sz", 0, G4 - 1))
            for j in range(NQ):
                b.add(("so", 0, j))
        if part[0] == "fox":
            for kind in ("fq", "fk", "fv"):
                b.add((kind, 0, 0))
            b.body(lambda i: [("fq", 0, i), ("fk", 0, i), ("fd", 0, i - 1), ("fv", 0, i)], 1, NQ)
            b.add(("fd", 0, NQ - 1))
    return b


FOX_STEPS = [("S", 0), ("S", 1), ("T", 0), ("S", 2), ("T", 1), ("V", 0), ("S", 3), ("T", 2), ("V", 1),
             ("T", 3), ("V", 2), ("V", 3)]
PT_AT = {0: (0, 0), 1: (1, 0), 3: (1, 384), 2: (2, 0)}


def hgrn_steps(i):
    steps = [("L", 0), ("hg", 0), ("L", 1), ("K", 0), ("L", 2), ("hd", 0), ("hd", 1), ("L", 3), ("U", 0),
             ("hg", 1), ("L", 4), ("hd", 2), ("hd", 3), ("L", 5), ("hf", 0), ("L", 6), ("hd", 4), ("L", 7),
             ("K", 1), ("L", 8), ("hd", 5), ("L", 9), ("hd", 6), ("U", 1), ("L", 10), ("hd", 7),
             ("L", 11), ("L", 12), ("hf", 1), ("L", 13), ("O", 0), ("O", 1), ("hq", 0), ("hq", 1), ("sx", 0), ("sx", 1),
             ("N", 0), ("N", 1)]
    gone = {"hd", "sx"} if i == 0 else {"hf", "hq"} if i == NQ - 1 else {"sx"}
    return [x for x in steps if x[0] not in gone]


def ssd_steps(i):
    steps = [("sz", 0), ("sz", 1), ("sX", 0), ("sX", 1), ("sB", 0), ("sC", 0), ("sR", 0), ("sR", 1), ("sU", 0), ("sU", 1),
             ("sx", 0), ("sY", 0), ("sR", 2), ("sR", 3), ("sx", 1), ("sb", 0), ("sY", 1), ("sb", 1)]
    gone = {"sx", "sb"} if i == G4 - 1 else set()
    return [x for x in steps if x[0] not in gone]


class Tiles:

    def __init__(self):
        self.n, self.bank, self.prev, self.held = {}, {}, {}, [None] * 8

    def add(self, key, bank):
        self.n[key], self.bank[key] = len(self.n), bank
        self.prev[key] = -1 if self.held[bank] is None else self.n[self.held[bank]]
        self.held[bank] = key


def plan_tiles(parts):
    t = Tiles()
    t.add(("rows",), 0)
    if ("hyb",) in parts:
        t.add(("rows2",), 1)
        t.add(("rows3",), 2)
    for m in range(KD):
        t.add(("in", m), 4 + m % 4)
    for part in parts:
        if part[0] == "ffn":
            f = part[1]
            for i in range(NF + 1):
                if i < NF:
                    for m in range(2):
                        t.add(("g", f, i, m), m)
                    for m in range(2):
                        t.add(("u", f, i, m), 2 + m)
                if i:
                    for m in range(KD):
                        t.add(("d", f, i - 1, m), 4 + m % 4)
        if part[0] == "hyb":
            two = lambda kind, i, b0: [t.add((kind, 0, i, m), b0 + m) for m in range(2)]
            two("hf", 0, 0)
            t.add(("dlog",), 4)
            t.add(("hrt",), 6)
            two("hq", 0, 2)
            for i in range(NQ):
                two("hv", i, 0)
                for what, k in hgrn_steps(i):
                    bank = {"L": 6 + k % 2, "K": k, "O": k, "U": 1, "N": k, "hd": 4 + k % 2}.get(what, 2 + k)
                    at = i + {"hf": 1, "hq": 1, "hd": -1, "sx": -i}.get(what, 0)
                    t.add(("h" + what if len(what) == 1 else what, 0, at, k), bank)
            t.add(("dlogT",), 6)
            two("sb", 0, 0)
            for m in range(KD):
                t.add(("hd", 0, NQ - 1, m), 4 + m % 4)
                if m == 3:
                    t.add(("cst",), 2)
            for i in range(G4):
                for what, k in ssd_steps(i):
                    bank = {"sz": 4 + k, "sX": k, "sB": 2, "sC": 3, "sU": k, "sR": 4 + k % 2, "sY": 6,
                            "sx": k, "sb": 2 + k}[what]
                    t.add((what, 0, i + (what in ("sx", "sb")), k), bank)
            for j in range(NQ):
                for m in range(2):
                    t.add(("so", 0, j, m), (2 * j + m) % 4)
        if part[0] == "fox":
            for i in range(NQ + 1):
                if i < NQ:
                    for m in range(2):
                        t.add(("fq", 0, i, m), m)
                    if i == 0:
                        t.add(("flog",), 4)
                        t.add(("flogT",), 5)
                        t.add(("frt",), 6)
                if i:
                    for m in range(2):
                        t.add(("fo", 0, i - 1, m), 4 + m)
                if i < NQ:
                    for m in range(2):
                        t.add(("fk", 0, i, m), 2 + m)
                if i:
                    for m in range(KD):
                        t.add(("fd", 0, i - 1, m), 4 + m % 4)
                if i < NQ:
                    for m in range(2):
                        t.add(("fv", 0, i, m), m)
                    for what, h in FOX_STEPS:
                        if what == "T":
                            for m in range(3):
                                t.add(("fT", 0, i, h, m), m)
                        if what == "V":
                            t.add(("fV", 0, i, h), 3)
    for m in range(2 * TC):
        t.add(("out", m), m % 4)
    return t


def trunk(nc, A, out, parts):
    B, TL = plan_blocks(parts), plan_tiles(parts)
    ffns = [p[1] for p in parts if p[0] == "ffn"]
    last_block_part = parts[-1]
    norms = {"final": len(parts)}
    gains = []
    for p in parts:
        if p[0] == "ffn":
            gains.append(A["ffn1_norm" if p[1] % 2 == 0 else "ffn2_norm"][p[1] // 2:p[1] // 2 + 1, :])
        else:
            gains.append(A["mix_norm"][(0 if p[0] == "hyb" else 1):(1 if p[0] == "hyb" else 2), :])
    gains.append(A["final_norm"].rearrange("(a d) -> a d", a=1))
    NN = len(gains)

    ctx = ExitStack()
    with ctx:
        def sb(name, shape, dt=F32):
            return ctx.enter_context(nc.sbuf_tensor(name, shape, dt))

        def sem(name):
            return ctx.enter_context(nc.semaphore(name))

        xT = sb("xT", [P, KD, T])
        uh = sb("uh", [P, KD, T], F32R)
        ul = sb("ul", [P, KD, T], F32R)
        sq = sb("sq", [P, KD, T])
        rstd = sb("rstd", [P, T])
        var = sb("var", [P, T])
        raw = [sb(f"raw{s}", [P, KD * CB]) for s in range(SLOTS)]
        wh = [sb(f"wh{s}", [P, KD * CB], F32R) for s in range(SLOTS)]
        wl = [sb(f"wl{s}", [P, KD * CB], F32R) for s in range(SLOTS)]
        gain = sb("gain", [P, NN, KD])
        ident = sb("ident", [P, P])
        ones = sb("ones", [P, P])
        hh = sb("hh", [P, 2, T], F32R)
        hl = sb("hl", [P, 2, T], F32R)
        rtok = sb("rtok", [P, TC])
        vtok = sb("vtok", [P, TC])
        cw = sb("cw", [P, CONV + 1, 16])
        hcols = sb("hcols", [P, 3, KD])
        scols = sb("scols", [P, 2, KD])
        lbt = sb("lbt", [P, KD])
        with (nc.sbuf_tensor("rows", [NN * KD, P], F32) as rows,
              nc.sbuf_tensor("rows2", [CONV * 16, P], F32) as rows2,
              nc.sbuf_tensor("dpair", [KD, 2], F32) as dpair,
              nc.sbuf_tensor("rows3", [48, P], F32) as rows3):
            pass
        with (nc.sbuf_tensor("gs", [P, 2, T], F32) as gs, nc.sbuf_tensor("us", [P, 2, T], F32) as us,
              nc.sbuf_tensor("hh_last", [P, 2, T], F32R) as hh_last, nc.sbuf_tensor("hl_last", [P, 2, T], F32R) as hl_last,
              nc.sbuf_tensor("xg", [P, KD, T], F32) as xg):
            pass
        fox_ctx = ExitStack()
        fb = lambda name, shape, dt=F32: fox_ctx.enter_context(nc.sbuf_tensor(name, shape, dt))
        qx = fb("qx", [P, HPB, T])
        kx = fb("kx", [P, HPB, T])
        vt = fb("vt", [P, TC, CB])
        pr = [fb(f"pr{b}", [P, TC, T]) for b in range(2)]
        pt = [fb(f"pt{b}", [P, 3, T]) for b in range(2)]
        ot = fb("ot", [P, TC, CB])
        negmax = fb("negmax", [P, HPB * TC])
        rowsum = fb("rowsum", [P, HPB * TC])
        rrow = fb("rrow", [P, HPB * TC])
        rt = fb("rt", [P, TC])
        flog = fb("flog", [P, TC * NH])
        fcum = [pr[1][0:NH, b, :] for b in range(2)]
        ftmp = [pr[0][0:NH, b, :] for b in range(4)] + [pr[1][0:NH, b, :] for b in range(2, 4)]
        bfcol = fb("bfcol", [NH, 1])
        identb = fb("identb", [P, P], BF16)
        maskb = fb("maskb", [P, P], BF16)
        fsr = fb("fsr", [P, KD * NH])
        fsh = fb("fsh", [P, KD * NH], F32R)
        fsl = fb("fsl", [P, KD * NH], F32R)
        cum_dram = nc.dram_tensor("cum_dram", (2, NH, T), F32, kind="Internal").ap()
        fox_ctx.close()
        hyb_ctx = ExitStack()
        hb = lambda name, shape, dt=F32: hyb_ctx.enter_context(nc.sbuf_tensor(name, shape, dt))
        U8 = mybir.dt.uint8
        waited = hb("waited", [P, 14])
        lmask = hb("lmask", [P, 7, P], U8)
        causal = hb("causal", [P, P])
        sel = hb("sel", [G4, G4, P])
        tok3 = hb("tok3", [P, 3, TC, NH])
        tokg = hb("tokg", [P, 3, TC, G4])
        hc = hb("hc", [P, 3, 2])
        hgain = hb("hgain", [P, 2])
        wc = hb("wc", [P, CONV + 1, 4])
        hrt = hb("hrt", [P, TC])
        dsr = hb("dsr", [P, KD * NH])
        dsh = hb("dsh", [P, KD * NH], F32R)
        dsl = hb("dsl", [P, KD * NH], F32R)
        dtb = hb("dtb", [NH, 1])
        alog = hb("alog", [NH, 1])
        dlog = hb("dlog", [P, TC * NH])
        cs_dram = nc.dram_tensor("cs_dram", (NH, T), F32, kind="Internal").ap()
        hg_ctx = ExitStack()
        gb = lambda name, shape, dt=F32: hg_ctx.enter_context(nc.sbuf_tensor(name, shape, dt))
        fz = gb("fz", [P, 2, T])
        kk = gb("kk", [P, 2, T])
        qq = gb("qq", [P, 2, T])
        bb = gb("bb", [P, 2, T])
        vv = gb("vv", [P, TC, CB])
        khT = gb("khT", [P, T])
        kh = gb("kh", [P, TC, P])
        osum = gb("osum", [P, 2 * TC])
        ovar = gb("ovar", [P, 2 * TC])
        lx2 = gb("lx2", [P, T])
        gg = gb("gg", [P, 2, T])
        qhat = gb("qhat", [P, 2, T])
        etot = gb("etot", [P, 2, TC])
        lev = gb("lev", [P, 2, T])
        lx = gb("lx", [P, 2, T])
        sc = gb("sc", [P, 2, TC, P])
        st = gb("st", [P, 2, TC - 1, P])
        hg_ctx.close()
        t1, osq, osb = (sq[:, 2 * n:2 * n + 2, :] for n in range(3))
        dtz, dta, dts, dtw, dtp, dcs, dde = (sq[0:NH, n, :] for n in range(7))
        ss_ctx = ExitStack()
        cb_ = lambda name, shape, dt=F32: ss_ctx.enter_context(nc.sbuf_tensor(name, shape, dt))
        yy = cb_("yy", [P, KD, T])
        xpad = cb_("xpad", [P, 4, T + CONV - 1])
        xc = cb_("xc", [P, 4, T])
        bt = cb_("bt", [P, TC, P])
        cbm = cb_("cbm", [P, TC, P])
        mm_ = cb_("mm", [P, 2, T])
        cx = cb_("cx", [P, 2, T])
        ecs = cb_("ecs", [P, 2, T])
        ub = cb_("ub", [P, TC - 1, CB])
        csg = var[0:G4, :]
        ss_ctx.close()
        xdt, xdd, zs, ysq = (sq[:, 2 * n:2 * n + 2, :] for n in range(4))
        xdt4, xdd4 = (x.rearrange("p a (c f) -> p (a c) f", c=2) for x in (xdt, xdd))
        hyb_ctx.close()

        banks = [ctx.enter_context(nc.psum_tensor(f"bank{n}", [P, T], F32)) for n in range(8)]
        stat_bank = banks[7]

        landed = [sem(f"landed{s}") for s in range(SLOTS)]
        hi_done = [sem(f"hi_done{s}") for s in range(SLOTS)]
        lo_done = [sem(f"lo_done{s}") for s in range(SLOTS)]
        tile_done = sem("tile_done")
        tile_read = sem("tile_read")
        x_in = [sem(f"x_in{h}") for h in range(2)]
        gains_in = sem("gains_in"); const_ready = sem("const_ready")
        u_ready = sem("u_ready")
        sq_ready = sem("sq_ready")
        stat_done = sem("stat_done")
        var_ready = sem("var_ready")
        rms_ready = sem("rms_ready")
        silu_ready = sem("silu_ready")
        hd_ready = sem("hd_ready")
        h_ready = sem("h_ready")
        stored = sem("stored")
        small_in = sem("small_in"); small_hi = sem("small_hi"); small_lo = sem("small_lo"); fsmall_hi = sem("fsmall_hi")
        fox_const = sem("fox_const")
        lse_ready = sem("lse_ready")
        exp_l_ready = sem("exp_l_ready")
        cum_ready = sem("cum_ready"); cum_stored = sem("cum_stored"); aug_in = sem("aug_in")
        params_in = sem("params_in"); dpair_in = sem("dpair_in"); d_spread = sem("d_spread")
        lb_asked = sem("lb_asked"); lb_exp = sem("lb_exp")
        hyb_const = sem("hyb_const"); dt_asked = sem("dt_asked"); dt_exp = sem("dt_exp")
        dec_asked = sem("dec_asked"); dec_exp = sem("dec_exp"); cs_ready = sem("cs_ready")
        cs_stored = sem("cs_stored"); csg_in = sem("csg_in"); d_in = sem("d_in")
        fz_ready = sem("fz_ready")
        sig_ready = sem("sig_ready")
        ln_asked = sem("ln_asked"); ln_ready = sem("ln_ready")
        b_ready = sem("b_ready")
        eb_ready = sem("eb_ready")
        qk_ready = sem("qk_ready")
        lev_ready = sem("lev_ready")
        dec_ready = sem("dec_ready")
        lx_ready = sem("lx_ready")
        osq_ready = sem("osq_ready")
        on_ready = sem("on_ready"); ovar_ready = sem("ovar_ready"); oroot_ready = sem("oroot_ready"); gsilu_ready = sem("gsilu_ready")
        cols_ready = sem("cols_ready")
        tap_ready = sem("tap_ready")
        conv_ready = sem("conv_ready")
        xc_ready = sem("xc_ready")
        zsilu_ready = sem("zsilu_ready")
        xdd_ready = sem("xdd_ready"); ecs_ready = sem("ecs_ready"); dl_ready = sem("dl_ready")
        dexp_ready = sem("dexp_ready"); mc_ready = sem("mc_ready"); st_ready = sem("st_ready")
        ysq_ready = sem("ysq_ready"); y_ready = sem("y_ready")
        ystat_done = sem("ystat_done"); yvar_ready = sem("yvar_ready"); yroot_ready = sem("yroot_ready")
        yu_ready = sem("yu_ready")
        flog_ready = sem("flog_ready")
        qkv_ready = sem("qkv_ready")
        s_done = sem("s_done")
        negmax_ready = sem("negmax_ready")
        exp_done = sem("exp_done")
        o_ready = sem("o_ready")
        dve_sem = sem("dve_steps"); pool_sem = sem("pool_steps")

        def last_tile_of_x(n, m):
            if n == 0:
                return ("in", m)
            p = parts[n - 1]
            return {"ffn": ("d", p[-1], NF - 1, m), "hyb": ("so", 0, m // 2, m % 2), "fox": ("fd", 0, NQ - 1, m)}[p[0]]

        def gu_src(key_kind, f, i):
            w = A[("ffn1" if f % 2 == 0 else "ffn2") + {"g": "_w_gate", "u": "_w_up"}[key_kind]][f // 2]
            return w[:, bass.ts(i, CB)].rearrange("(k p) c -> p k c", p=P)

        def d_src(f, i):
            w = A[("ffn1" if f % 2 == 0 else "ffn2") + "_w_down"][f // 2]
            return w[bass.ts(i, CB), :].rearrange("(k p) c -> p k c", p=P)

        def source(kind, f, i, skip=0):
            if kind == "d":
                return d_src(f, i)
            if kind in ("g", "u"):
                return gu_src(kind, f, i)
            if kind == "fd":
                return A["fox_w_out"][0][bass.ts(i, CB), :].rearrange("(k p) c -> p k c", p=P)
            if kind == "hd":
                return A["hyb_w_out"][0][:D, :][bass.ts(i, CB), :].rearrange("(k p) c -> p k c", p=P)
            if kind == "so":
                return A["hyb_w_out"][0][D:, :][:, bass.ts(i, CB)].rearrange("(k p) c -> p k c", p=P)
            col = {"hq": 0, "hf": D, "hv": 2 * D, "hg": 3 * D, "sz": 4 * D, "sx": 5 * D}.get(kind)
            if col is not None:
                return A["hyb_w_in"][0][:, col + skip:col + D][:, bass.ts(i, CB)].rearrange("(k p) c -> p k c", p=P)
            col = {"fq": 0, "fk": D, "fv": 2 * D}[kind]
            return A["fox_w_in"][0][:, col:col + D][:, bass.ts(i, CB)].rearrange("(k p) c -> p k c", p=P)

        def slot_of(kind, f, i, lo, hi):
            return B.slot[(kind, f, i if isinstance(i, int) else lo)]

        def nth(kind, f, i, lo, hi, shift=0):
            return affine(lambda x: B.nth[(kind, f, x - shift)], i, lo, hi)

        block = ctx.enter_context(nc.Block())

        @block.sync
        def _(sp):
            def load(kind, f, i, lo, hi, shift=0):
                s = B.slot[(kind, f, (i if isinstance(i, int) else lo) - shift)]
                at, skip = i - shift if shift else i, 0
                if kind == "hq" and not isinstance(i, int):
                    at, skip = i, -shift * CB
                if not (isinstance(i, int) and B.nth[(kind, f, i - shift)] == 0):
                    sp.wait_ge(lo_done[s], affine(lambda x: B.nth[(kind, f, x - shift)], i, lo, hi))
                dst = raw[s].rearrange("p (k c) -> p k c", k=2 if kind in ("d", "fd", "hd") else KD)
                if kind == "sb":
                    for h in range(2):
                        c0 = 6 * D + h * G4 * P
                        src = A["hyb_w_in"][0][:, c0:c0 + G4 * P][:, bass.ts(at, P)].rearrange("(k p) c -> p k c", p=P)
                        sp.dma_start(dst[:, :, h * P:(h + 1) * P], src).then_inc(landed[s], 16)
                    return
                sp.dma_start(dst, source(kind, f, at, skip)).then_inc(landed[s], 16)

            for h in range(2):
                sp.dma_start(sq.rearrange("p (c h) t -> p c h t", h=2)[:, :, h, :],
                             A["x"][0][:, h * T:(h + 1) * T].rearrange("(c p) d -> p c d", p=P)).then_inc(x_in[h], 16)
            for part in parts:
                if part[0] == "ffn":
                    f = part[1]
                    load("g", f, 0, 0, 1)
                    load("u", f, 0, 0, 1)
                    with sp.Fori(1, NF) as i:
                        load("g", f, i, 1, NF)
                        load("u", f, i, 1, NF)
                        load("d", f, i, 1, NF, 1)
                    load("d", f, NF - 1, NF - 1, NF)
                if part[0] == "hyb":
                    for kind, at in (("hf", 0), ("hq", 0), ("hv", 0), ("hg", 0), ("hf", 1), ("hq", 1)):
                        load(kind, 0, at, at, at + 1)
                    with sp.Fori(1, NQ - 1) as i:
                        for kind, shift in (("hv", 0), ("hg", 0), ("hd", 1), ("hf", -1), ("hq", -1)):
                            load(kind, 0, i, 1, NQ - 1, shift)
                    for kind, at in (("hv", 3), ("hg", 3), ("hd", 2), ("sx", 0), ("sb", 0), ("hd", 3)):
                        load(kind, 0, at, at, at + 1)
                    with sp.Fori(0, G4 - 1) as i:
                        for kind, shift in (("sz", 0), ("sx", -1), ("sb", -1)):
                            load(kind, 0, i, 0, G4 - 1, shift)
                    load("sz", 0, G4 - 1, G4 - 1, G4)
                    for j in range(NQ):
                        load("so", 0, j, j, j + 1)
                if part[0] == "fox":
                    for kind in ("fq", "fk", "fv"):
                        load(kind, 0, 0, 0, 1)
                    with sp.Fori(1, NQ) as i:
                        load("fq", 0, i, 1, NQ)
                        load("fk", 0, i, 1, NQ)
                        load("fd", 0, i, 1, NQ, 1)
                        load("fv", 0, i, 1, NQ)
                    load("fd", 0, NQ - 1, NQ - 1, NQ)
            for c in range(TC):
                sp.wait_ge(tile_read, TL.n[("out", 2 * c + 1)] + 1)
                sp.dma_start(out[0, c * P:(c + 1) * P, :], sq[:, 2 * c:2 * c + 2, :].rearrange("p h t -> p (h t)")).then_inc(stored, 16)
            sp.wait_ge(stored, 16 * TC)

        @block.gpsimd
        def _(pool):
            pl = Links(pool_sem)
            nc.gpsimd.memset(ones[:], 1.0).then_inc(const_ready, 1)
            pl.step(pool, nc.gpsimd.memset(ident[:], 0.0))
            nc.gpsimd.affine_select(out=ident[:], in_=ident[:], compare_op=ALU.not_equal, fill=1.0, base=0,
                                    pattern=[[-1, P]], channel_multiplier=1).then_inc(const_ready, 1)
            for n, part in enumerate(parts):
                if part[0] == "hyb":
                    pool.wait_ge(dpair_in, 16)
                    nc.gpsimd.tensor_copy(rows3[0:KD, :].rearrange("k (e c) -> k e c", e=2),
                                          dpair[:].unsqueeze(2).to_broadcast([KD, 2, SP_])).then_inc(d_spread, 1)
                    pool.wait_ge(tile_read, TL.n[last_tile_of_x(n, KD - 1) if n else ("rows3",)] + 1)
                    nc.gpsimd.dma_start(dtb[:], A["ssd_dt_bias"].rearrange("a h -> h a")).then_inc(d_in, 16)
                    nc.gpsimd.dma_start(alog[:], A["ssd_A_log"].rearrange("a h -> h a")).then_inc(d_in, 16)
                    nc.gpsimd.dma_start(dsr.rearrange("p (k c) -> p k c", k=KD),
                                        A["hyb_w_in"][0][:, HYB_SMALL:HYB_SMALL + NH].rearrange("(k p) c -> p k c", p=P)
                                        ).then_inc(d_in, 16)
                    pl.step(pool, nc.gpsimd.memset(causal[:], 1.0))
                    pl.step(pool, nc.gpsimd.affine_select(out=causal[:], in_=causal[:], compare_op=ALU.is_ge, fill=0.0,
                                                          base=0, pattern=[[1, P]], channel_multiplier=-1))
                    pl.step(pool, nc.gpsimd.memset(sel[:], 1.0))
                    pl.step(pool, nc.gpsimd.affine_select(out=sel[:], in_=sel[:], compare_op=ALU.is_equal, fill=0.0,
                                                          base=0, pattern=[[-1, G4], [0, P]], channel_multiplier=1))
                    for l in range(7):
                        m = 64 >> l
                        mk = lev[:, 0, 0:P].rearrange("p (n h j) -> p n h j", h=2, j=m)
                        pl.step(pool, nc.gpsimd.memset(lev[:, 0, 0:P], 0.0 if l < 6 else 1.0))
                        if l < 6:
                            a = mk[:, :, 1, :]
                            pl.step(pool, nc.gpsimd.memset(a, 1.0))
                            pl.step(pool, nc.gpsimd.affine_select(out=a, in_=a, compare_op=ALU.is_ge, fill=0.0, base=0,
                                                                  pattern=[[-2 * m, P // (2 * m)], [0, m]], channel_multiplier=1))
                            pl.step(pool, nc.gpsimd.affine_select(out=a, in_=a, compare_op=ALU.is_ge, fill=0.0, base=m - 1,
                                                                  pattern=[[2 * m, P // (2 * m)], [0, m]], channel_multiplier=-1))
                        else:
                            a = lev[:, 0, 0:P].rearrange("p (n j) -> p n j", j=2)
                            pl.step(pool, nc.gpsimd.affine_select(out=a, in_=a, compare_op=ALU.is_ge, fill=0.0, base=0,
                                                                  pattern=[[-2, P // 2], [0, 2]], channel_multiplier=1))
                            pl.step(pool, nc.gpsimd.affine_select(out=a, in_=a, compare_op=ALU.is_ge, fill=0.0, base=0,
                                                                  pattern=[[2, P // 2], [1, 2]], channel_multiplier=-1))
                        pl.step(pool, nc.gpsimd.tensor_copy(lmask[:, l, :], lev[:, 0, 0:P]))
                    pl.step(pool, nc.gpsimd.memset(lx[:], 0.0))
                    nc.gpsimd.memset(sc[:], 0.0).then_inc(hyb_const, 1)
                if part[0] == "fox":
                    if n:
                        pool.wait_ge(tile_read, TL.n[last_tile_of_x(n, KD - 1)] + 1)
                    nc.gpsimd.dma_start(bfcol[:], A["fox_b_f"].rearrange("a h -> h a")).then_inc(small_in, 16)
                    nc.gpsimd.dma_start(fsr.rearrange("p (k c) -> p k c", k=KD),
                                        A["fox_w_in"][0][:, FOX_SMALL:FOX_SMALL + NH].rearrange("(k p) c -> p k c", p=P)
                                        ).then_inc(small_in, 16)
                    pl.step(pool, nc.gpsimd.memset(qx[:], 0.0))
                    pl.step(pool, nc.gpsimd.memset(kx[:], 0.0))
                    pl.step(pool, nc.gpsimd.memset(maskb[:], 0.0))
                    for x in (qx, kx):
                        pl.step(pool, nc.gpsimd.memset(x[HD:HD + 2, 0:HPB:2, :], 1.0))
                        pl.step(pool, nc.gpsimd.memset(x[0:2, 1:HPB:2, :], 1.0))
                    pool.wait_ge(const_ready, 2)
                    pl.step(pool, nc.gpsimd.tensor_copy(identb[:], ident[:]))
                    nc.gpsimd.affine_select(out=maskb[:], in_=maskb[:], compare_op=ALU.is_ge, fill=NEG, base=0,
                                            pattern=[[-1, P]], channel_multiplier=1).then_inc(fox_const, 1)

        @block.scalar
        def _(act):
            def split(kind, f, i, lo, hi, shift=0, after=None):
                s = B.slot[(kind, f, (i if isinstance(i, int) else lo) - shift)]
                act.wait_ge(landed[s], affine(lambda x: B.lands[(kind, f, x - shift)], i, lo, hi))
                nc.scalar.activation(wh[s][:], raw[s][:], ACT.Copy).then_inc(hi_done[s], 1)

            def split_next(kind, f, i, lo, hi, last_tile, shift=0):
                key = (kind, f, (i if isinstance(i, int) else lo) - shift)
                s = B.slot[key]
                if isinstance(i, int) and B.nth[key] + 1 == B.count[s]:
                    return
                act.wait_ge(tile_done, affine(lambda x: TL.n[(kind, f, x - shift, last_tile)] + 1, i, lo, hi))
                act.wait_ge(landed[s], affine(lambda x: B.next_lands.get((kind, f, x - shift), 0), i, lo, hi))
                nc.scalar.activation(wh[s][:], raw[s][:], ACT.Copy).then_inc(hi_done[s], 1)

            def squares(n):
                for m in range(KD):
                    act.wait_ge(tile_read, TL.n[last_tile_of_x(n, m)] + 1)
                    nc.scalar.activation(sq[:, m, :], xT[:, m, :], ACT.Square).then_inc(sq_ready, 1)

            def root(n):
                act.wait_ge(var_ready, n + 1)
                nc.scalar.activation(rstd[:], var[:], ACT.Sqrt).then_inc(rms_ready, 1)

            def silu(f, i, lo, hi):
                for m in range(2):
                    act.wait_ge(tile_read, affine(lambda x: TL.n[("g", f, x, m)] + 1, i, lo, hi))
                    nc.scalar.activation(gs[:, m, :], gs[:, m, :], ACT.Silu).then_inc(silu_ready, 1)

            for n, g in enumerate(gains):
                act.dma_start(rows[n * KD:(n + 1) * KD, :], g.rearrange("a (k p) -> (a k) p", p=P)).then_inc(gains_in, 16)
            if ("hyb",) in parts:
                act.dma_start(dpair[:], A["ssd_D"].rearrange("a (k e) -> (a k) e", e=2)).then_inc(dpair_in, 16)
                act.dma_start(rows2[:], A["ssd_conv_w"][0].rearrange("k (c p) -> (k c) p", p=P)).then_inc(params_in, 16)
                for at, name in ((8, "ssd_conv_b"), (24, "hgrn_lb_logits"), (32, "hgrn_out_gain"), (40, "ssd_out_gain")):
                    src = A[name].rearrange("a (k p) -> (a k) p", p=P)
                    act.dma_start(rows3[at:at + src.shape[0], :], src).then_inc(params_in, 16)
            for key in B.order[:SLOTS]:
                s = B.slot[key]
                act.wait_ge(landed[s], B.lands[key])
                nc.scalar.activation(wh[s][:], raw[s][:], ACT.Copy).then_inc(hi_done[s], 1)
            if ("hyb",) in parts:
                act.wait_ge(lb_asked, 1)
                nc.scalar.activation(lbt[:], lbt[:], ACT.Exp).then_inc(lb_exp, 1)
            act.wait_ge(tile_done, TL.n[("in", KD - 1)] + 1)
            for n, part in enumerate(parts):
                squares(n)
                if n and parts[n - 1][0] == "ffn":
                    split_next("d", parts[n - 1][1], NF - 1, NF - 1, NF, KD - 1)
                if n and parts[n - 1][0] == "fox":
                    split_next("fd", 0, NQ - 1, NQ - 1, NQ, KD - 1)
                root(n)
                if part[0] == "ffn":
                    f = part[1]

                    def ffn_step(i, lo, hi):
                        silu(f, i, lo, hi)
                        split_next("g", f, i, lo, hi, 1)
                        split_next("u", f, i, lo, hi, 1)
                        if not isinstance(i, int) or i:
                            split_next("d", f, i, lo, hi, KD - 1, 1)
                    ffn_step(0, 0, 1)
                    with act.Fori(1, NF - 1) as i:
                        ffn_step(i, 1, NF - 1)
                    ffn_step(NF - 1, NF - 1, NF)
                if part[0] == "hyb":
                    A_ = nc.scalar.activation

                    def hgrn_gates(i, lo, hi, shift=0):
                        for e in range(2):
                            act.wait_ge(tile_read, affine(lambda x: TL.n[("hf", 0, x - shift, e)] + 1, i, lo, hi))
                            A_(t1[:, e, :], fz[:, e, :], ACT.Sigmoid).then_inc(sig_ready, 1)
                            if shift and e == 0:
                                act.wait_ge(lx_ready, affine(lambda x: 14 * x + 14, i, lo, hi))
                            A_(kk[:, e, :], fz[:, e, :], ACT.Sigmoid, scale=-1.0).then_inc(sig_ready, 1)

                    def hgrn_logs(i, lo, hi):
                        for e in range(2):
                            act.wait_ge(ln_asked, affine(lambda x: 2 * x + e + 1, i, lo, hi))
                            A_(t1[:, e, :], t1[:, e, :], ACT.Ln).then_inc(ln_ready, 1)
                            A_(fz[:, e, :], fz[:, e, :], ACT.Ln, scale=1.0 / LOG_SPLIT).then_inc(ln_ready, 1)

                    def hgrn_step(i, lo, hi, steps):
                        hgrn_logs(i, lo, hi)

                        def decays(j):
                            act.wait_ge(lev_ready, affine(lambda x: 14 * x + j + 1, i, lo, hi))
                            if j % 7 == 6:
                                if not (isinstance(i, int) and i == 0 and j == 6):
                                    act.wait_ge(tile_read, affine(lambda x: TL.n[("hL", 0, x if j > 6 else x - 1, 6 if j > 6 else 13)] + 1, i, lo, hi))
                                A_(lx2[:], lev[:, j % 2, :], ACT.Exp, scale=-1.0)
                            A_(lev[:, j % 2, :], lev[:, j % 2, :], ACT.Exp).then_inc(dec_ready, 1)

                        def chunk_decays(e):
                            act.wait_ge(b_ready, affine(lambda x: 2 * x + e + 1, i, lo, hi))
                            A_(khT[:], khT[:], ACT.Exp)
                            A_(qhat[:, e, :], bb[:, e, :], ACT.Exp).then_inc(eb_ready, 1)
                        decays(0)
                        decays(1)
                        chunk_decays(0)
                        decays(2)
                        decays(3)
                        split_next("hq", 0, i, lo, hi, 1)
                        for what, k in steps:
                            if what == "L":
                                if k + 4 < 14:
                                    decays(k + 4)
                                if k == 4:
                                    chunk_decays(1)
                                if k == 13 and ("hq", 0) in steps:
                                    hgrn_gates(i, lo, hi, -1)
                            if what == "hg" and k == 0:
                                split_next("hv", 0, i, lo, hi, 1)
                            if what == "hg" and k == 1:
                                split_next("hg", 0, i, lo, hi, 1)
                            if what == "hd" and k == KD - 1:
                                split_next("hd", 0, i, lo, hi, KD - 1, 1)
                            if what == "hf" and k == 1:
                                split_next("hf", 0, i, lo, hi, 1, -1)
                            if what == "O":
                                act.wait_ge(tile_done, affine(lambda x: TL.n[("hO", 0, x, k)] + 1, i, lo, hi))
                                for c in range(TC):
                                    r = slice(c * P, (c + 1) * P)
                                    ins = A_(osq[:, k, r], banks[k][:, r], ACT.Square, accum_out=osum[:, k * TC + c:k * TC + c + 1])
                                ins.then_inc(osq_ready, 1)
                                if k == 1:
                                    for e in range(2):
                                        A_(gg[:, e, :], gg[:, e, :], ACT.Silu).then_inc(gsilu_ready, 1)
                                    act.wait_ge(ovar_ready, affine(lambda x: x + 1, i, lo, hi))
                                    A_(ovar[:], ovar[:], ACT.Sqrt).then_inc(oroot_ready, 1)
                            if what == "N" and k == 1 and ("sx", 0) in steps:
                                split_next("sx", 0, 0, 0, 1, 1)

                    act.wait_ge(d_in, 48)
                    A_(dsh[:], dsr[:], ACT.Copy).then_inc(small_hi, 1)
                    A_(alog[:], alog[:], ACT.Exp).then_inc(lb_exp, 1)
                    hgrn_gates(0, 0, 1)
                    split_next("hf", 0, 0, 0, 1, 1)
                    hgrn_step(0, 0, 1, hgrn_steps(0))
                    with act.Fori(1, NQ - 1) as i:
                        hgrn_step(i, 1, NQ - 1, hgrn_steps(1))
                    hgrn_step(NQ - 1, NQ - 1, NQ, hgrn_steps(NQ - 1))
                    act.wait_ge(dt_asked, 1)
                    A_(dta, dta, ACT.Exp, scale=-1.0).then_inc(dt_exp, 1)
                    act.wait_ge(dec_asked, 1)
                    A_(dde, dde, ACT.Exp).then_inc(dec_exp, 1)
                    act.wait_ge(cs_ready, TC)
                    act.dma_start(cs_dram, dcs).then_inc(cs_stored, 16)
                    act.wait_ge(cs_stored, 16)
                    split_next("sb", 0, 0, 0, 1, 1)
                    split_next("hd", 0, NQ - 1, NQ - 1, NQ, KD - 1)

                    def ssd_step(i, lo, hi, steps):
                        act.wait_ge(cols_ready, affine(lambda x: x + 1, i, lo, hi))
                        act.dma_start(csg[:], cs_dram[bass.ts(i, G4), :]).then_inc(csg_in, 16)
                        for m in range(4):
                            A_(xc[:, m, :], xpad[:, m, CONV - 1:], ACT.Identity, scale=wc[:, CONV - 1, m:m + 1],
                               bias=wc[:, CONV, m:m + 1]).then_inc(tap_ready, 1)
                        for m in range(4):
                            act.wait_ge(conv_ready, affine(lambda x: 4 * x + m + 1, i, lo, hi))
                            A_(xc[:, m, :], xc[:, m, :], ACT.Silu).then_inc(xc_ready, 1)
                        for m in range(2):
                            act.wait_ge(tile_read, affine(lambda x: TL.n[("sz", 0, x, m)] + 1, i, lo, hi))
                            A_(zs[:, m, :], zs[:, m, :], ACT.Silu).then_inc(zsilu_ready, 1)
                        split_next("sz", 0, i, lo, hi, 1)
                        for what, k in steps:
                            if what == "sR":
                                act.wait_ge(tile_done, affine(lambda x: TL.n[("sR", 0, x, k)] + 1, i, lo, hi))
                                if k > 1:
                                    act.wait_ge(st_ready, affine(lambda x: 2 * x + 1, i, lo, hi))
                                A_(ecs[:, k % 2, :], banks[4 + k % 2][:], ACT.Exp).then_inc(ecs_ready, 1)
                                act.wait_ge(dl_ready, affine(lambda x: 4 * x + k + 1, i, lo, hi))
                                A_(mm_[:, k % 2, :], mm_[:, k % 2, :], ACT.Exp).then_inc(dexp_ready, 1)
                            if what == "sY":
                                act.wait_ge(y_ready, affine(lambda x: 2 * x + k + 1, i, lo, hi))
                                if not (isinstance(i, int) and i == 0):
                                    act.wait_ge(ystat_done, affine(lambda x: 2 * x + k - 1, i, lo, hi))
                                else:
                                    pass
                                A_(ysq[:, k, :], yy[:, bass.ds(2 * i + k, 1), :].rearrange("p a t -> p (a t)"),
                                   ACT.Square).then_inc(ysq_ready, 1)
                            if what in ("sx", "sb") and k == 1:
                                split_next(what, 0, i, lo, hi, 1, -1)
                    ssd_step(0, 0, 1, ssd_steps(0))
                    with act.Fori(1, G4 - 1) as i:
                        ssd_step(i, 1, G4 - 1, ssd_steps(1))
                    ssd_step(G4 - 1, G4 - 1, G4, ssd_steps(G4 - 1))
                    act.wait_ge(yvar_ready, 1)
                    A_(var[:], var[:], ACT.Sqrt).then_inc(yroot_ready, 1)
                    for j in range(NQ):
                        split_next("so", 0, j, j, j + 1, 1)
                if part[0] == "fox":
                    def fox_step(i, lo, hi):
                        for kind, last, shift in (("fq", 1, 0), ("fk", 1, 0), ("fd", KD - 1, 1), ("fv", 1, 0)):
                            if kind == "fq" and not isinstance(i, int):
                                bias_rows(i)
                            if kind == "fd" and isinstance(i, int) and i == 0:
                                continue
                            split_next(kind, 0, i, lo, hi, last, shift)
                            if kind == "fq" and isinstance(i, int) and i == 0:
                                act.wait_ge(lse_ready, 1)
                                nc.scalar.activation(ftmp[1], ftmp[1], ACT.Exp, scale=-1.0).then_inc(exp_l_ready, 1)
                                act.wait_ge(cum_ready, 2)
                                act.dma_start(cum_dram[0], fcum[0]).then_inc(cum_stored, 16)
                                act.dma_start(cum_dram[1], fcum[1]).then_inc(cum_stored, 16)
                                act.wait_ge(cum_stored, 32)
                                act.wait_ge(fox_const, 1)
                                bias_rows(0)
                        for h in range(HPB):
                            for c in range(TC):
                                j = h * TC + c
                                act.wait_ge(negmax_ready, affine(lambda x: x * HPB * TC + j + 1, i, lo, hi))
                                if c == 0 and h >= 2:
                                    act.wait_ge(tile_done, affine(lambda x: TL.n[("fT", 0, x, h - 2, 2)] + 1, i, lo, hi))
                                w = (c + 1) * P
                                nc.scalar.activation(pr[h % 2][:, c, 0:w], banks[4 + c][:, 0:w], ACT.Exp,
                                                     bias=negmax[:, j:j + 1], accum_out=rowsum[:, j:j + 1]
                                                     ).then_inc(exp_done, 1)

                    def bias_rows(i):
                        c0 = cum_dram[0][bass.ts(i, HPB), :].rearrange("(a b) t -> b a t", b=2)
                        c1 = cum_dram[1][bass.ts(i, HPB), :].rearrange("(a b) t -> b a t", b=2)
                        act.dma_start(qx[HD:HD + 1, 0:HPB:2, :], c0[0:1]).then_inc(aug_in, 16)
                        act.dma_start(qx[0:1, 1:HPB:2, :], c0[1:2]).then_inc(aug_in, 16)
                        act.dma_start(kx[HD + 1:HD + 2, 0:HPB:2, :], c1[0:1]).then_inc(aug_in, 16)
                        act.dma_start(kx[1:2, 1:HPB:2, :], c1[1:2]).then_inc(aug_in, 16)
                    act.wait_ge(small_in, 32)
                    nc.scalar.activation(fsh[:], fsr[:], ACT.Copy).then_inc(fsmall_hi, 1)
                    fox_step(0, 0, 1)
                    with act.Fori(1, NQ) as i:
                        fox_step(i, 1, NQ)
            squares(len(parts))
            act.wait_ge(var_ready, len(parts) + 1)
            nc.scalar.activation(rtok[:], vtok[:], ACT.Sqrt).then_inc(rms_ready, 1)

        @block.vector
        def _(dve):
            links = Links(dve_sem)
            v = nc.vector

            def split(s, n):
                dve.wait_ge(hi_done[s], n)
                v.tensor_tensor(wl[s][:], raw[s][:], wh[s][:].bitcast(F32), ALU.subtract).then_inc(lo_done[s], 1)

            def split_next(kind, f, i, lo, hi, shift=0):
                key = (kind, f, (i if isinstance(i, int) else lo) - shift)
                s = B.slot[key]
                if isinstance(i, int) and B.nth[key] + 1 == B.count[s]:
                    return
                split(s, affine(lambda x: B.nth[(kind, f, x - shift)] + 2, i, lo, hi))

            def tile(key, i, lo, hi):
                dve.wait_ge(tile_done, affine(lambda x: TL.n[key(x)] + 1, i, lo, hi))
                return banks[TL.bank[key(i if isinstance(i, int) else lo)]]

            def prepare(n, m):
                g = gain[:, n, m:m + 1]
                if n == len(parts):
                    v.tensor_scalar(xg[:, m, :], xT[:, m, :], g, None, ALU.mult).then_inc(u_ready, 1)
                    return
                links.step(dve, v.tensor_scalar(uh[:, m, :], xT[:, m, :], g, None, ALU.mult))
                v.scalar_tensor_tensor(out=ul[:, m, :], in0=xT[:, m, :], scalar=g, in1=uh[:, m, :].bitcast(F32),
                                       op0=ALU.mult, op1=ALU.subtract).then_inc(u_ready, 1)

            def norm_scale(n):
                dve.wait_ge(stat_done, n + 1)
                v.tensor_scalar(var[:], stat_bank[:], 1.0 / D, EPS, ALU.mult, ALU.add).then_inc(var_ready, 1)
                dve.wait_ge(rms_ready, n + 1)
                links.step(dve, v.reciprocal(rstd[:], rstd[:]))

            def residual(key, i, lo, hi, m, scale, final):
                b = tile(key, i, lo, hi)
                ins = v.scalar_tensor_tensor(out=xT[:, m, :], in0=b[:], scalar=scale, in1=xT[:, m, :],
                                             op0=ALU.mult, op1=ALU.add)
                ins.then_inc(tile_read, 1)
                return ins

            def log1p_exp(z, a, out, w, p, asked, answered, n):
                v.scalar_tensor_tensor(out=a, in0=z, scalar=-1.0, in1=z, op0=ALU.mult, op1=ALU.max).then_inc(asked, 1)
                dve.wait_ge(answered, n)
                links.step(dve, v.tensor_scalar(w, a, 2.0, None, ALU.add))
                links.step(dve, v.reciprocal(w, w))
                links.step(dve, v.tensor_tensor(a, a, w, ALU.mult))
                links.step(dve, v.tensor_tensor(w, a, a, ALU.mult))
                links.step(dve, v.tensor_scalar(p, w, 1.0 / 15, None, ALU.mult))
                for k in (13, 11, 9, 7, 5, 3):
                    links.step(dve, v.scalar_tensor_tensor(out=p, in0=p, scalar=1.0 / k, in1=w, op0=ALU.add, op1=ALU.mult))
                links.step(dve, v.scalar_tensor_tensor(out=p, in0=p, scalar=1.0, in1=a, op0=ALU.add, op1=ALU.mult))
                links.step(dve, v.tensor_scalar(out, p, 2.0, None, ALU.mult))

            TT, TS, STT = v.tensor_tensor, v.tensor_scalar, v.scalar_tensor_tensor

            def head_params():
                b = tile(lambda x: ("rows2",), 0, 0, 1)
                v.tensor_copy(cw[:, 0:CONV, :], b[:, 0:CONV * 16].rearrange("p (k c) -> p k c", k=CONV)).then_inc(tile_read, 1)
                b = tile(lambda x: ("rows3",), 0, 0, 1)
                v.tensor_copy(cw[:, CONV, :], b[:, 8:24])
                v.tensor_copy(lbt[:], b[:, 24:32])
                v.tensor_copy(hcols[:, 2, :], b[:, 32:40])
                v.tensor_copy(scols[:, 1, :], b[:, 40:48])
                v.tensor_copy(scols[:, 0, :], b[:, 0:8]).then_inc(tile_read, 1)
                dve.wait_ge(tile_read, TL.n[("rows3",)] + 1)
                TT(lbt[:], lbt[:], lbt[:], ALU.subtract).then_inc(lb_asked, 1)
                dve.wait_ge(lb_exp, 1)
                links.step(dve, v.reciprocal(hcols[:, 1, :], lbt[:]))
                links.step(dve, TT(lbt[:], lbt[:], hcols[:, 1, :], ALU.mult))
                links.step(dve, TT(hcols[:, 0, :], lbt[:], lbt[:], ALU.subtract))
                links.step(dve, TS(hcols[:, 1, :], hcols[:, 0, :], -1.0, 1.0, ALU.mult, ALU.add))

            split(B.slot[B.order[0]], 1)
            b = tile(lambda x: ("rows",), 0, 0, 1)
            v.tensor_copy(gain.rearrange("p n k -> p (n k)"), b[:, 0:NN * KD]).then_inc(tile_read, 1)
            dve.wait_ge(tile_read, TL.n[("rows",)] + 1)
            if ("hyb",) in parts:
                head_params()
            for m in range(KD):
                b = tile(lambda x: ("in", m), 0, 0, 1)
                v.tensor_copy(xT[:, m, :], b[:]).then_inc(tile_read, 1)
                dve.wait_ge(tile_read, TL.n[("in", m)] + 1)
                prepare(0, m)
            for key in B.order[1:SLOTS]:
                split(B.slot[key], 1)

            for n, part in enumerate(parts):
                norm_scale(n)
                if part[0] == "ffn":
                    f = part[1]
                    first = ffns.index(f) * NF

                    def ffn_hidden(i, lo, hi):
                        for m in range(2):
                            dve.wait_ge(silu_ready, affine(lambda x: 2 * (first + x) + m + 1, i, lo, hi))
                            links.step(dve, v.tensor_tensor(us[:, m, :], gs[:, m, :], us[:, m, :], ALU.mult))
                            h_, l_ = (hh_last, hl_last) if isinstance(i, int) and i == NF - 1 else (hh, hl)
                            links.step(dve, v.tensor_copy(h_[:, m, :], us[:, m, :]))
                            v.tensor_tensor(l_[:, m, :], us[:, m, :], h_[:, m, :].bitcast(F32),
                                            ALU.subtract).then_inc(h_ready, 1)

                    def ffn_step(i, lo, hi):
                        for m in range(2):
                            b = tile(lambda x: ("g", f, x, m), i, lo, hi)
                            v.tensor_tensor(gs[:, m, :], b[:], rstd[:], ALU.mult).then_inc(tile_read, 1)
                        split_next("g", f, i, lo, hi)
                        for m in range(2):
                            b = tile(lambda x: ("u", f, x, m), i, lo, hi)
                            v.tensor_tensor(us[:, m, :], b[:], rstd[:], ALU.mult).then_inc(tile_read, 1)
                            dve.wait_ge(tile_read, affine(lambda x: TL.n[("u", f, x, m)] + 1, i, lo, hi))
                        if isinstance(i, int):
                            ffn_hidden(i, lo, hi)
                        if not isinstance(i, int) or i:
                            for m in range(KD):
                                residual(lambda x: ("d", f, x - 1, m), i, lo, hi, m, 0.5, False)
                        if not isinstance(i, int):
                            ffn_hidden(i, lo, hi)
                        split_next("u", f, i, lo, hi)
                        if not isinstance(i, int) or i:
                            split_next("d", f, i, lo, hi, 1)
                    ffn_step(0, 0, 1)
                    with dve.Fori(1, NF - 1) as i:
                        links.enter(i, 1, 4)
                        ffn_step(i, 1, NF - 1)
                    links.leave(NF - 2)
                    ffn_step(NF - 1, NF - 1, NF)
                    for m in range(KD):
                        residual(lambda x: ("d", f, x, m), NF - 1, NF - 1, NF, m, 0.5, True)
                        dve.wait_ge(tile_read, TL.n[("d", f, NF - 1, m)] + 1)
                        prepare(n + 1, m)
                    split_next("d", f, NF - 1, NF - 1, NF)
                if part[0] == "hyb":
                    def scaled_in(kind, i, lo, hi, m, dst, shift=0):
                        b = tile(lambda x: (kind, 0, x - shift, m), i, lo, hi)
                        return TT(dst, b[:], rstd[:], ALU.mult).then_inc(tile_read, 1)

                    def tokens_in(i, lo, hi):
                        for m in range(2):
                            b = tile(lambda x: ("hv", 0, x, m), i, lo, hi)
                            TS(vv[:, 2 * m, :], b[:, 0:CB], hrt[:, 2 * m:2 * m + 1], None, ALU.mult).then_inc(qkv_ready, 1)
                            TS(vv[:, 2 * m + 1, :], b[:, CB:2 * CB], hrt[:, 2 * m + 1:2 * m + 2], None,
                               ALU.mult).then_inc(tile_read, 1)

                    def time_steps():
                        z, a, dt_, w_, p_, cs_, de_ = dtz, dta, dts, dtw, dtp, dcs, dde
                        b = tile(lambda x: ("dlogT",), 0, 0, 1)
                        TT(z, b[0:NH, :], rstd[0:NH, :], ALU.mult).then_inc(tile_read, 1)
                        dve.wait_ge(tile_read, TL.n[("dlogT",)] + 1)
                        links.step(dve, TS(z, z, dtb[:, 0:1], None, ALU.add))
                        log1p_exp(z, a, dt_, w_, p_, dt_asked, dt_exp, 1)
                        links.step(dve, STT(out=dt_, in0=z, scalar=0.0, in1=dt_, op0=ALU.max, op1=ALU.add))
                        dve.wait_ge(lb_exp, 2)
                        links.step(dve, TS(z, dt_, alog[:, 0:1], -1.0, ALU.mult, ALU.mult))
                        links.step(dve, v.memset(a, 0.0))
                        for c in range(TC):
                            r = slice(c * P, (c + 1) * P)
                            v.tensor_tensor_scan(cs_[:, r], z[:, r], a[:, r], 0.0, ALU.add, ALU.add).then_inc(cs_ready, 1)
                        dve.wait_ge(cs_ready, TC)
                        c4 = cs_.rearrange("p (c t) -> p c t", c=TC)
                        TT(de_.rearrange("p (c t) -> p c t", c=TC), c4[:, :, P - 1:P].to_broadcast([NH, TC, P]), c4,
                           ALU.subtract).then_inc(dec_asked, 1)

                    def gates(i, lo, hi, shift=0):
                        links.step(dve, v.tensor_copy(hc[:], hcols[:, :, bass.ts(i - shift if shift else i, 2)]))
                        for e in range(2):
                            dve.wait_ge(sig_ready, affine(lambda x: 4 * (x - shift) + 2 * e + 2, i, lo, hi))
                            TS(kk[:, e, :], kk[:, e, :], hc[:, 1, e:e + 1], None, ALU.mult)
                            links.step(dve, TS(t1[:, e, :], t1[:, e, :], hc[:, 1, e:e + 1], hc[:, 0, e:e + 1], ALU.mult, ALU.add))
                            links.step(dve, TS(fz[:, e, :], t1[:, e, :], LOG_SPLIT, TINY, ALU.min, ALU.max))
                            TS(t1[:, e, :], t1[:, e, :], LOG_SPLIT, None, ALU.max).then_inc(ln_asked, 1)

                    def log_decay(i, lo, hi, e):
                        dve.wait_ge(ln_ready, affine(lambda x: 4 * x + 2 * e + 2, i, lo, hi))
                        for c in range(TC):
                            r = slice(c * P, (c + 1) * P)
                            ins = v.tensor_tensor_scan(bb[:, e, r], t1[:, e, r], fz[:, e, r], 0.0, ALU.add, ALU.add)
                        links.step(dve, ins)

                    def hgrn_step(i, lo, hi, steps):
                        v.tensor_copy(hgain[:], hcols[:, 2, bass.ts(i, 2)])

                        def chunk_diff(e):
                            b4 = bb[:, e, :].rearrange("p (c t) -> p c t", c=TC)
                            TT(khT.rearrange("p (c t) -> p c t", c=TC), b4[:, :, P - 1:P].to_broadcast([P, TC, P]), b4,
                               ALU.subtract).then_inc(b_ready, 1)

                        def chunk_scaled(e):
                            dve.wait_ge(eb_ready, affine(lambda x: 2 * x + e + 1, i, lo, hi))
                            links.step(dve, v.tensor_copy(etot[:, e, :], qhat[:, e, :].rearrange("p (c t) -> p c t", c=TC)[:, :, P - 1:P].rearrange("p c t -> p (c t)")))
                            TT(khT[:], khT[:], kk[:, e, :], ALU.mult)
                            TT(qhat[:, e, :], qhat[:, e, :], qq[:, e, :], ALU.mult).then_inc(qk_ready, 1)

                        def diff(j):
                            e, l = divmod(j, 7)
                            m = 64 >> l
                            if j > 1:
                                dve.wait_ge(lx_ready, affine(lambda x: 14 * x + j - 1, i, lo, hi))
                            src = bb[:, e, :].rearrange("p (n h j) -> p n h j", h=2, j=m)
                            dst = lev[:, j % 2, :].rearrange("p (n h j) -> p n h j", h=2, j=m)
                            nb = T // (2 * m)
                            if l < 6:
                                ref = src[:, :, 0, m - 1:m].to_broadcast([P, nb, m])
                                TT(dst[:, :, 0, :], ref, src[:, :, 0, :], ALU.subtract)
                                TT(dst[:, :, 1, :], src[:, :, 1, :], ref, ALU.subtract).then_inc(lev_ready, 1)
                            else:
                                s2 = bb[:, e, :].rearrange("p (n j) -> p n j", j=2)
                                TT(lev[:, j % 2, :].rearrange("p (n j) -> p n j", j=2), s2,
                                   s2[:, :, 0:1].to_broadcast([P, T // 2, 2]), ALU.subtract).then_inc(lev_ready, 1)

                        def mult(j):
                            e, l = divmod(j, 7)
                            m = 64 >> l
                            dve.wait_ge(dec_ready, affine(lambda x: 14 * x + j + 1, i, lo, hi))
                            dst = lx[:, j % 2, :]
                            if l < 6:
                                view = lambda x: x.rearrange("p (n h j) -> p n h j", h=2, j=m)
                                TT(view(dst)[:, :, 0, :], view(lev[:, j % 2, :])[:, :, 0, :], view(kk[:, e, :])[:, :, 0, :], ALU.mult)
                                TT(view(dst)[:, :, 1, :], view(lev[:, j % 2, :])[:, :, 1, :], view(qq[:, e, :])[:, :, 1, :],
                                   ALU.mult).then_inc(lx_ready, 1)
                            else:
                                TT(lx2[:], lx2[:], kk[:, e, :], ALU.mult)
                                TT(dst, lev[:, j % 2, :], qq[:, e, :], ALU.mult).then_inc(lx_ready, 1)

                        log_decay(i, lo, hi, 0)
                        diff(0)
                        diff(1)
                        chunk_diff(0)
                        log_decay(i, lo, hi, 1)
                        mult(0)
                        mult(1)
                        diff(2)
                        diff(3)
                        chunk_scaled(0)
                        tokens_in(i, lo, hi)
                        split_next("hq", 0, i, lo, hi)
                        for what, k in steps:
                            if what == "L":
                                if k == 4:
                                    dve.wait_ge(tile_read, affine(lambda x: TL.n[("hK", 0, x, 0)] + 1, i, lo, hi))
                                    chunk_diff(1)
                                if k == 5:
                                    chunk_scaled(1)
                                b = tile(lambda x: ("hL", 0, x, k), i, lo, hi)
                                if k % 7:
                                    dve.wait_ge(tile_read, affine(lambda x: TL.n[("hL", 0, x, k - 1)] + 1, i, lo, hi))
                                v.memset(waited[:, k:k + 1], 0.0)
                                v.copy_predicated(sc[:, k // 7], lmask[:, k % 7:k % 7 + 1, :].to_broadcast([P, TC, P]),
                                                  b.rearrange("p (c t) -> p c t", c=TC)).then_inc(tile_read, 1)
                                if k + 2 < 14:
                                    mult(k + 2)
                                if k + 4 < 14:
                                    diff(k + 4)
                            if what == "K":
                                b = tile(lambda x: ("hK", 0, x, k), i, lo, hi)
                                v.tensor_copy(kh.rearrange("p c d -> p (c d)"), b[:]).then_inc(tile_read, 1)
                            if what == "U":
                                b = tile(lambda x: ("hU", 0, x, k), i, lo, hi)
                                links.step(dve, v.tensor_copy(st[:, k, 0, :], b[:, 0:P]))
                                links.step(dve, STT(out=st[:, k, 1, :], in0=st[:, k, 0, :], scalar=etot[:, k, 1:2],
                                                    in1=b[:, P:2 * P], op0=ALU.mult, op1=ALU.add))
                                STT(out=st[:, k, 2, :], in0=st[:, k, 1, :], scalar=etot[:, k, 2:3],
                                    in1=b[:, 2 * P:3 * P], op0=ALU.mult, op1=ALU.add).then_inc(tile_read, 1)
                            if what == "O":
                                b = tile(lambda x: ("hO", 0, x, k), i, lo, hi)
                                dve.wait_ge(osq_ready, affine(lambda x: 2 * x + k + 1, i, lo, hi))
                                v.tensor_copy(osb[:, k, :], b[:]).then_inc(tile_read, 1)
                                if k == 1:
                                    TS(ovar[:], osum[:], 1.0 / P, EPS, ALU.mult, ALU.add).then_inc(ovar_ready, 1)
                                    if ("hq", 0) in steps:
                                        gates(i, lo, hi, -1)
                                    dve.wait_ge(oroot_ready, affine(lambda x: x + 1, i, lo, hi))
                                    links.step(dve, v.reciprocal(ovar[:], ovar[:]))
                                    for e in range(2):
                                        o3 = osb[:, e, :].rearrange("p (c d) -> p c d", c=TC)
                                        TT(o3, o3, ovar[:, e * TC:(e + 1) * TC].unsqueeze(2).to_broadcast([P, TC, P]),
                                           ALU.mult).then_inc(on_ready, 1)
                            if what == "hq":
                                if k == 0:
                                    split_next("hf", 0, i, lo, hi, -1)
                                scaled_in("hq", i, lo, hi, k, qq[:, k, :], -1)
                            if what == "sx":
                                scaled_in("sx", 0, 0, 1, k, xpad[:, k, CONV - 1:])
                            if what == "N":
                                b = tile(lambda x: ("hN", 0, x, k), i, lo, hi)
                                dve.wait_ge(gsilu_ready, affine(lambda x: 2 * x + k + 1, i, lo, hi))
                                STT(out=gg[:, k, :], in0=gg[:, k, :], scalar=hgain[:, k:k + 1], in1=b[:],
                                    op0=ALU.mult, op1=ALU.mult).then_inc(tile_read, 1)
                                dve.wait_ge(tile_read, affine(lambda x: TL.n[("hN", 0, x, k)] + 1, i, lo, hi))
                                links.step(dve, v.tensor_copy(hh[:, k, :], gg[:, k, :]))
                                TT(hl[:, k, :], gg[:, k, :], hh[:, k, :].bitcast(F32), ALU.subtract).then_inc(hd_ready, 1)
                            if what == "hg":
                                scaled_in("hg", i, lo, hi, k, gg[:, k, :])
                                if k == 0:
                                    split_next("hv", 0, i, lo, hi)
                                if k == 1:
                                    split_next("hg", 0, i, lo, hi)
                            if what == "hd":
                                residual(lambda x: ("hd", 0, x - 1, k), i, lo, hi, k, 1.0, False)
                                if k == KD - 1:
                                    split_next("hd", 0, i, lo, hi, 1)
                            if what == "hf":
                                scaled_in("hf", i, lo, hi, k, fz[:, k, :], -1)

                    dve.wait_ge(small_hi, 1)
                    TT(dsl[:], dsr[:], dsh[:].bitcast(F32), ALU.subtract).then_inc(small_lo, 1)
                    for e in range(2):
                        scaled_in("hf", 0, 0, 1, e, fz[:, e, :])
                    split_next("hf", 0, 0, 0, 1)
                    b = tile(lambda x: ("dlog",), 0, 0, 1)
                    v.tensor_copy(dlog[:], b[:, 0:TC * NH]).then_inc(tile_read, 1)
                    dve.wait_ge(hyb_const, 1)
                    b = tile(lambda x: ("hrt",), 0, 0, 1)
                    v.tensor_copy(hrt[:], b[:, 0:TC]).then_inc(tile_read, 1)
                    gates(0, 0, 1)
                    for e in range(2):
                        scaled_in("hq", 0, 0, 1, e, qq[:, e, :])
                    hgrn_step(0, 0, 1, hgrn_steps(0))
                    with dve.Fori(1, NQ - 1) as i:
                        links.enter(i, 1, HG_LINKS)
                        hgrn_step(i, 1, NQ - 1, hgrn_steps(1))
                    links.leave(NQ - 2)
                    hgrn_step(NQ - 1, NQ - 1, NQ, hgrn_steps(NQ - 1))
                    time_steps()
                    split_next("sx", 0, 0, 0, 1)
                    for m in range(2):
                        scaled_in("sb", 0, 0, 1, m, xpad[:, 2 + m, CONV - 1:])
                    split_next("sb", 0, 0, 0, 1)
                    links.step(dve, v.memset(xpad[:, :, 0:CONV - 1], 0.0))
                    v.memset(yy[:, KD - 1, :], 0.0)
                    for m in range(KD):
                        residual(lambda x: ("hd", 0, x, m), NQ - 1, NQ - 1, NQ, m, 1.0, False)
                        if m == 3:
                            b = tile(lambda x: ("cst",), 0, 0, 1)
                            v.tensor_copy(tok3.rearrange("p a c h -> p (a c h)"), b[:, 0:3 * TC * NH]).then_inc(tile_read, 1)
                    split_next("hd", 0, NQ - 1, NQ - 1, NQ)
                    dve.wait_ge(tile_read, TL.n[("hd", 0, NQ - 1, KD - 1)] + 1)

                    def ssd_step(i, lo, hi, steps):
                        v.tensor_copy(tokg.rearrange("p a c h -> p (a c) h"),
                                      tok3[:, :, :, bass.ts(i, G4)].rearrange("p a c h -> p (a c) h"))
                        v.tensor_copy(wc[:, :, 0:2], cw[:, :, bass.ts(i, 2)])
                        v.tensor_copy(wc[:, :, 2:3], cw[:, :, bass.ds(i + 8, 1)])
                        v.tensor_copy(wc[:, :, 3:4], cw[:, :, bass.ds(i + 12, 1)])
                        v.tensor_copy(hc[:, 0, :], scols[:, 0, bass.ts(i, 2)]).then_inc(cols_ready, 1)
                        dve.wait_ge(cols_ready, affine(lambda x: x + 1, i, lo, hi))
                        for t in range(CONV - 1):
                            for m in range(4):
                                dve.wait_ge(tap_ready, affine(lambda x: 4 * x + m + 1, i, lo, hi))
                                ins = STT(out=xc[:, m, :], in0=xpad[:, m, t:t + T], scalar=wc[:, t, m:m + 1],
                                          in1=xc[:, m, :], op0=ALU.mult, op1=ALU.add)
                                if t < CONV - 2:
                                    links.step(dve, ins)
                                else:
                                    ins.then_inc(conv_ready, 1)
                        for what, k in steps:
                            if what == "sz":
                                scaled_in("sz", i, lo, hi, k, zs[:, k, :])
                                if k == 1:
                                    split_next("sz", 0, i, lo, hi)
                            if what == "sX":
                                b = tile(lambda x: ("sX", 0, x, k), i, lo, hi)
                                r = slice(2 * k * G4, (2 * k + 2) * G4)
                                col = lambda a: tokg[:, a, 2 * k:2 * k + 2, :].rearrange("p c h -> p (c h)").unsqueeze(2).to_broadcast([P, 2 * G4, SP_])
                                hv = lambda x: x.rearrange("p (h d) -> p h d", d=SP_)
                                TT(hv(xdt[:, k, :]), hv(b[:]), col(1), ALU.mult).then_inc(tile_read, 1)
                                dve.wait_ge(tile_read, affine(lambda x: TL.n[("sX", 0, x, k)] + 1, i, lo, hi))
                                TT(hv(xdd[:, k, :]), hv(xdt[:, k, :]), col(2), ALU.mult).then_inc(xdd_ready, 1)
                            if what == "sB":
                                b = tile(lambda x: ("sB", 0, x, k), i, lo, hi)
                                v.tensor_copy(bt.rearrange("p c n -> p (c n)"), b[:]).then_inc(tile_read, 1)
                            if what == "sC":
                                b = tile(lambda x: ("sC", 0, x, k), i, lo, hi)
                                TT(cbm[:], b.rearrange("p (c l) -> p c l", c=TC), causal[:].unsqueeze(1).to_broadcast([P, TC, P]),
                                   ALU.mult).then_inc(tile_read, 1)
                                dve.wait_ge(tile_read, affine(lambda x: TL.n[("sC", 0, x, k)] + 1, i, lo, hi))
                            if what == "sR":
                                e = k % 2
                                b = tile(lambda x: ("sR", 0, x, k), i, lo, hi)
                                dve.wait_ge(ecs_ready, affine(lambda x: 4 * x + k + 1, i, lo, hi))
                                if k > 1:
                                    dve.wait_ge(tile_done, affine(lambda x: TL.n[("sY", 0, x, 0)] + 1, i, lo, hi))
                                for c in range(TC):
                                    r = slice(c * P, (c + 1) * P)
                                    ins = TS(mm_[:, e, r], b[:, r], tokg[:, 0, c, k:k + 1], 0.0, ALU.subtract, ALU.min)
                                    if c == TC - 2:
                                        ins.then_inc(tile_read, 1)
                                ins.then_inc(dl_ready, 1)
                                TT(cx[:, e, :], ecs[:, e, :], xc[:, 3, :], ALU.mult)
                                dve.wait_ge(dexp_ready, affine(lambda x: 4 * x + k + 1, i, lo, hi))
                                TT(mm_[:, e, :], mm_[:, e, :], cbm.rearrange("p c l -> p (c l)"), ALU.mult).then_inc(mc_ready, 1)
                            if what == "sU":
                                b = tile(lambda x: ("sU", 0, x, k), i, lo, hi)
                                if k == 0:
                                    v.tensor_copy(ub[:, 0:2, :].rearrange("p c f -> p (c f)"), b[:]).then_inc(tile_read, 1)
                                else:
                                    v.tensor_copy(ub[:, 2, :], b[:, 0:CB]).then_inc(tile_read, 1)
                            if what == "sY":
                                b = tile(lambda x: ("sY", 0, x, k), i, lo, hi)
                                y = yy[:, bass.ds(2 * i + k, 1), :].rearrange("p a t -> p (a t)")
                                STT(out=xc[:, k, :], in0=xc[:, k, :], scalar=hc[:, 0, k:k + 1], in1=b[:],
                                    op0=ALU.mult, op1=ALU.add).then_inc(tile_read, 1)
                                dve.wait_ge(tile_read, affine(lambda x: TL.n[("sY", 0, x, k)] + 1, i, lo, hi))
                                dve.wait_ge(zsilu_ready, affine(lambda x: 2 * x + k + 1, i, lo, hi))
                                TT(y, xc[:, k, :], zs[:, k, :], ALU.mult).then_inc(y_ready, 1)
                            if what in ("sR", "sU") and (what, k) in (("sU", 1), ("sR", 3)):
                                dve.wait_ge(tile_read, affine(lambda x: TL.n[(what, 0, x, k)] + 1, i, lo, hi))
                                h0 = 0 if what == "sU" else 2
                                for c in (1, 2):
                                    for h in (h0, h0 + 1):
                                        f = slice(h * SP_, (h + 1) * SP_)
                                        ins = STT(out=ub[:, c, f], in0=ub[:, c - 1, f], scalar=ecs[:, h % 2, c * P + P - 1:c * P + P],
                                                  in1=ub[:, c, f], op0=ALU.mult, op1=ALU.add)
                                        if c == 1:
                                            links.step(dve, ins)
                                ins.then_inc(st_ready, 1)
                            if what == "sx":
                                scaled_in("sx", i, lo, hi, k, xpad[:, k, CONV - 1:], -1)
                                if k == 1:
                                    split_next("sx", 0, i, lo, hi, -1)
                            if what == "sb":
                                scaled_in("sb", i, lo, hi, k, xpad[:, 2 + k, CONV - 1:], -1)
                                if k == 1:
                                    split_next("sb", 0, i, lo, hi, -1)

                    ssd_step(0, 0, 1, ssd_steps(0))
                    with dve.Fori(1, G4 - 1) as i:
                        links.enter(i, 1, SSD_LINKS)
                        ssd_step(i, 1, G4 - 1, ssd_steps(1))
                    links.leave(G4 - 2)
                    ssd_step(G4 - 1, G4 - 1, G4, ssd_steps(G4 - 1))
                    dve.wait_ge(y_ready, 2 * G4)
                    for m in range(KD):
                        g_ = scols[:, 1, m:m + 1]
                        links.step(dve, TS(uh[:, m, :], yy[:, m, :], g_, None, ALU.mult))
                        STT(out=ul[:, m, :], in0=yy[:, m, :], scalar=g_, in1=uh[:, m, :].bitcast(F32), op0=ALU.mult,
                            op1=ALU.subtract).then_inc(yu_ready, 1)
                    dve.wait_ge(ystat_done, 2 * G4)
                    TS(var[:], banks[7][:], 1.0 / D, EPS, ALU.mult, ALU.add).then_inc(yvar_ready, 1)
                    dve.wait_ge(yroot_ready, 1)
                    links.step(dve, v.reciprocal(var[:], var[:]))
                    for j in range(NQ):
                        for m in range(2):
                            f = 2 * j + m
                            b = tile(lambda x: ("so", 0, j, m), 0, 0, 1)
                            links.step(dve, TT(ecs[:, 0, :], b[:], var[:], ALU.mult))
                            TT(xT[:, f, :], xT[:, f, :], ecs[:, 0, :], ALU.add).then_inc(tile_read, 1)
                            dve.wait_ge(tile_read, TL.n[("so", 0, j, m)] + 1)
                        if j < NQ - 1:
                            split_next("so", 0, j, j, j + 1)
                    for m in range(KD):
                        prepare(n + 1, m)
                    split_next("so", 0, NQ - 1, NQ - 1, NQ)
                if part[0] == "fox":
                    def heads_in(kind, dst, scale, i, lo, hi):
                        for m in range(2):
                            b = tile(lambda x: (kind, 0, x, m), i, lo, hi)
                            for e in range(2):
                                r = slice(e * HD, (e + 1) * HD)
                                ins = v.scalar_tensor_tensor(out=dst[r, 2 * m + e, :], in0=b[r, :], scalar=scale,
                                                             in1=rstd[r, :], op0=ALU.mult, op1=ALU.mult)
                                if e == 0:
                                    ins.then_inc(qkv_ready, 1)
                            ins.then_inc(tile_read, 1)

                    def fox_step(i, lo, hi):
                        peeled = isinstance(i, int)
                        heads_in("fq", qx, HD ** -0.5, i, lo, hi)
                        if peeled and i == 0:
                            b = tile(lambda x: ("flog",), 0, 0, 1)
                            v.tensor_copy(flog[:], b[:, 0:TC * NH]).then_inc(tile_read, 1)
                            forget_gates()
                        split_next("fq", 0, i, lo, hi)
                        if not peeled or i:
                            outputs(i, lo, hi)
                        heads_in("fk", kx, 1.0, i, lo, hi)
                        split_next("fk", 0, i, lo, hi)
                        if not peeled or i:
                            for m in range(KD):
                                residual(lambda x: ("fd", 0, x - 1, m), i, lo, hi, m, 1.0, False)
                            split_next("fd", 0, i, lo, hi, 1)
                        for m in range(2):
                            b = tile(lambda x: ("fv", 0, x, m), i, lo, hi)
                            v.tensor_scalar(vt[:, 2 * m, :], b[:, 0:CB], rt[:, 2 * m:2 * m + 1], None,
                                            ALU.mult).then_inc(qkv_ready, 1)
                            v.tensor_scalar(vt[:, 2 * m + 1, :], b[:, CB:2 * CB], rt[:, 2 * m + 1:2 * m + 2], None,
                                            ALU.mult).then_inc(tile_read, 1)
                        split_next("fv", 0, i, lo, hi)
                        for what, h in FOX_STEPS:
                            if what == "S":
                                for c in range(TC):
                                    j = h * TC + c
                                    dve.wait_ge(s_done, affine(lambda x: x * HPB * TC + j + 1, i, lo, hi))
                                    v.tensor_reduce(negmax[:, j:j + 1], banks[4 + c][:, 0:(c + 1) * P], AX.X, ALU.max,
                                                    negate=True).then_inc(negmax_ready, 1)
                            if what == "T":
                                for m in range(3):
                                    b = tile(lambda x: ("fT", 0, x, h, m), i, lo, hi)
                                    w = T if m < 2 else T // 2
                                    v.tensor_copy(pt[h % 2][:, m, 0:w], b[:, 0:w]).then_inc(tile_read, 1)
                            if what == "V":
                                dve.wait_ge(exp_done, affine(lambda x: x * HPB * TC + (h + 1) * TC, i, lo, hi))
                                r = slice(h * TC, (h + 1) * TC)
                                links.step(dve, v.reciprocal(rrow[:, r], rowsum[:, r]))
                                b = tile(lambda x: ("fV", 0, x, h), i, lo, hi)
                                v.tensor_tensor(ot[:, :, h * HD:(h + 1) * HD],
                                                b[:, 0:TC * HD].rearrange("p (c d) -> p c d", c=TC),
                                                rrow[:, r].unsqueeze(2).to_broadcast([P, TC, HD]),
                                                ALU.mult).then_inc(tile_read, 1)

                    def outputs(i, lo, hi):
                        for m in range(2):
                            b = tile(lambda x: ("fo", 0, x - 1, m), i, lo, hi)
                            links.step(dve, v.tensor_copy(hh[:, m, :], b[:]))
                            v.tensor_tensor(hl[:, m, :], b[:], hh[:, m, :].bitcast(F32),
                                            ALU.subtract).then_inc(tile_read, 1)

                    def forget_gates():
                        b = tile(lambda x: ("flogT",), 0, 0, 1)
                        z, a = ftmp[0], ftmp[1]
                        dve.wait_ge(small_in, 32)
                        v.tensor_tensor(z, b[0:NH, :], rstd[0:NH, :], ALU.mult).then_inc(tile_read, 1)
                        dve.wait_ge(tile_read, TL.n[("flogT",)] + 1)
                        links.step(dve, v.tensor_scalar(z, z, bfcol[:, 0:1], None, ALU.add))
                        log1p_exp(z, a, ftmp[2], ftmp[3], ftmp[4], lse_ready, exp_l_ready, 1)
                        links.step(dve, v.scalar_tensor_tensor(out=z, in0=z, scalar=0.0, in1=ftmp[2], op0=ALU.min,
                                                               op1=ALU.subtract))
                        links.step(dve, v.memset(a, 0.0))
                        v.tensor_tensor_scan(fcum[0], z, a, 0.0, ALU.add, ALU.add).then_inc(cum_ready, 1)
                        dve.wait_ge(cum_ready, 1)
                        v.tensor_scalar(fcum[1], fcum[0], -1.0, None, ALU.mult).then_inc(cum_ready, 1)
                        b = tile(lambda x: ("frt",), 0, 0, 1)
                        v.tensor_copy(rt[:], b[:, 0:TC]).then_inc(tile_read, 1)
                        dve.wait_ge(tile_read, TL.n[("frt",)] + 1)

                    dve.wait_ge(fsmall_hi, 1)
                    v.tensor_tensor(fsl[:], fsr[:], fsh[:].bitcast(F32), ALU.subtract).then_inc(small_lo, 1)
                    dve.wait_ge(fox_const, 1)
                    fox_step(0, 0, 1)
                    with dve.Fori(1, NQ) as i:
                        links.enter(i, 1, 6)
                        fox_step(i, 1, NQ)
                    links.leave(NQ - 1)
                    outputs(NQ, NQ, NQ + 1)
                    for m in range(KD):
                        residual(lambda x: ("fd", 0, x, m), NQ - 1, NQ - 1, NQ, m, 1.0, True)
                        dve.wait_ge(tile_read, TL.n[("fd", 0, NQ - 1, m)] + 1)
                        prepare(n + 1, m)
                    split_next("fd", 0, NQ - 1, NQ - 1, NQ)
            dve.wait_ge(stat_done, len(parts) + 1)
            v.tensor_scalar(vtok[:], stat_bank[:, 0:TC], 1.0 / D, EPS, ALU.mult, ALU.add).then_inc(var_ready, 1)
            dve.wait_ge(rms_ready, len(parts) + 1)
            links.step(dve, v.reciprocal(rtok[:], rtok[:]))
            for c in range(TC):
                for h in range(2):
                    b = tile(lambda x: ("out", 2 * c + h), 0, 0, 1)
                    v.tensor_scalar(sq[:, 2 * c + h, :], b[:], rtok[:, c:c + 1], None, ALU.mult).then_inc(tile_read, 1)

        @block.tensor
        def _(pe):
            def free(key, i, lo, hi):
                k = key(i if isinstance(i, int) else lo)
                if TL.prev[k] >= 0:
                    pe.wait_ge(tile_read, at_least(lambda x: TL.prev[key(x)] + 1, lambda x: TL.n[key(x)], i, lo, hi))
                return banks[TL.bank[k]]

            def block_in(kind, f, i, lo, hi, shift=0):
                s = B.slot[(kind, f, (i if isinstance(i, int) else lo) - shift)]
                pe.wait_ge(lo_done[s], affine(lambda x: B.nth[(kind, f, x - shift)] + 1, i, lo, hi))
                return s

            def product(dst, lh, ll, rh, rl, first, last):
                nc.tensor.matmul(dst, lh, rh, start=first, stop=False)
                nc.tensor.matmul(dst, lh, rl, start=False, stop=False)
                return nc.tensor.matmul(dst, ll, rh, start=False, stop=last)

            def columns(kind, f, i, lo, hi, m, n=None, shift=0):
                s = B.slot[(kind, f, (i if isinstance(i, int) else lo) - shift)]
                b = free(lambda x: (kind, f, x - shift, m), i, lo, hi)
                for k in range(KD):
                    if n is not None:
                        pe.wait_ge(u_ready, n * KD + k + 1)
                    c = slice(k * CB + m * P, k * CB + (m + 1) * P)
                    mm = product(b[:], wh[s][:, c], wl[s][:, c], uh[:, k, :], ul[:, k, :], k == 0, k == KD - 1)
                mm.then_inc(tile_done, 1)

            def stat(n):
                for k in range(KD):
                    pe.wait_ge(sq_ready, n * KD + k + 1)
                    mm = nc.tensor.matmul(stat_bank[:], ones[:], sq[:, k, :], start=k == 0, stop=k == KD - 1)
                mm.then_inc(stat_done, 1)

            def down(f, i, lo, hi, shift=0, kind="d", only=None):
                s = B.slot[(kind, f, (i if isinstance(i, int) else lo) - shift)]
                if only in (None, 0):
                    block_in(kind, f, i, lo, hi, shift)
                if kind == "d":
                    pe.wait_ge(h_ready, affine(lambda x: 2 * (ffns.index(f) * NF + x - shift) + 2, i, lo, hi))
                if kind == "hd":
                    pe.wait_ge(hd_ready, affine(lambda x: 2 * (x - shift) + 2, i, lo, hi))
                if kind == "fd":
                    pe.wait_ge(tile_read, affine(lambda x: TL.n[("fo", 0, x - shift, 1)] + 1, i, lo, hi))
                h_, l_ = (hh_last, hl_last) if kind == "d" and not shift else (hh, hl)
                for m in range(KD) if only is None else [only]:
                    b = free(lambda x: (kind, f, x - shift, m), i, lo, hi)
                    for k in range(2):
                        c = slice(k * D + m * P, k * D + (m + 1) * P)
                        mm = product(b[:], wh[s][:, c], wl[s][:, c], h_[:, k, :], l_[:, k, :], k == 0, k == 1)
                    mm.then_inc(tile_done, 1)

            def tokens(kind, i, lo, hi):
                s = block_in(kind, 0, i, lo, hi)
                for m in range(2):
                    b = free(lambda x: (kind, 0, x, m), i, lo, hi)
                    for c in range(2):
                        r = slice((2 * m + c) * P, (2 * m + c + 1) * P)
                        for k in range(KD):
                            w = slice(k * CB, (k + 1) * CB)
                            mm = product(b[:, c * CB:(c + 1) * CB], uh[:, k, r], ul[:, k, r],
                                         wh[s][:, w], wl[s][:, w], k == 0, k == KD - 1)
                    mm.then_inc(tile_done, 1)

            def small_logits(key, hi_, lo_):
                pe.wait_ge(small_lo, 1 + (key == "flog" and ("hyb",) in parts))
                b = free(lambda x: (key,), 0, 0, 1)
                for c in range(TC):
                    for k in range(KD):
                        r, w = slice(c * P, (c + 1) * P), slice(k * NH, (k + 1) * NH)
                        mm = product(b[:, c * NH:(c + 1) * NH], uh[:, k, r], ul[:, k, r], hi_[:, w], lo_[:, w],
                                     k == 0, k == KD - 1)
                mm.then_inc(tile_done, 1)

            def rms_by_token(key):
                b = free(lambda x: (key,), 0, 0, 1)
                for c in range(TC):
                    mm = nc.tensor.matmul(b[:, c:c + 1], rstd[0:1, c * P:(c + 1) * P], ones[0:1, 0:1], start=True, stop=True)
                mm.then_inc(tile_done, 1)

            def heads_first(key, src):
                b = free(lambda x: (key,), 0, 0, 1)
                for c in range(TC):
                    mm = nc.tensor.transpose(b[0:NH, c * P:(c + 1) * P], src[:, c * NH:(c + 1) * NH], ident[:])
                mm.then_inc(tile_done, 1)

            pe.wait_ge(const_ready, 2)
            pe.wait_ge(gains_in, 16 * NN)
            nc.tensor.transpose(banks[0][:, 0:NN * KD], rows[:], ident[0:NN * KD, 0:NN * KD]).then_inc(tile_done, 1)
            if ("hyb",) in parts:
                pe.wait_ge(params_in, 80)
                pe.wait_ge(d_spread, 1)
                nc.tensor.transpose(banks[1][:, 0:CONV * 16], rows2[:], ident[0:CONV * 16, 0:CONV * 16]).then_inc(tile_done, 1)
                nc.tensor.transpose(banks[2][:, 0:48], rows3[:], ident[0:48, 0:48]).then_inc(tile_done, 1)
            for m in range(KD):
                pe.wait_ge(x_in[m // (KD // 2)], 16)
                b = free(lambda x: ("in", m), 0, 0, 1)
                for c in range(TC):
                    xt = sq[:, 2 * c + m // 4, (m % 4) * P:(m % 4 + 1) * P]
                    mm = nc.tensor.transpose(b[:, c * P:(c + 1) * P], xt, ident[:])
                mm.then_inc(tile_done, 1)
            for n, part in enumerate(parts):
                if part[0] == "ffn":
                    f = part[1]
                    block_in("g", f, 0, 0, 1)
                    columns("g", f, 0, 0, 1, 0, n)
                    stat(n)
                    columns("g", f, 0, 0, 1, 1)
                    block_in("u", f, 0, 0, 1)
                    columns("u", f, 0, 0, 1, 0)
                    columns("u", f, 0, 0, 1, 1)
                    with pe.Fori(1, NF) as i:
                        block_in("g", f, i, 1, NF)
                        columns("g", f, i, 1, NF, 0)
                        columns("g", f, i, 1, NF, 1)
                        block_in("u", f, i, 1, NF)
                        columns("u", f, i, 1, NF, 0)
                        columns("u", f, i, 1, NF, 1)
                        down(f, i, 1, NF, 1)
                    down(f, NF - 1, NF - 1, NF)
                if part[0] == "hyb":
                    mm_f = nc.tensor.matmul

                    def hgrn_step(i, lo, hi, steps):
                        tokens("hv", i, lo, hi)
                        for what, k in steps:
                            if what == "L":
                                b = free(lambda x: ("hL", 0, x, k), i, lo, hi)
                                pe.wait_ge(lx_ready, affine(lambda x: 14 * x + k + 1, i, lo, hi))
                                for c in range(TC):
                                    r = slice(c * P, (c + 1) * P)
                                    x = lx[:, k % 2, r]
                                    mm = mm_f(b[:, r], lx2[:, r] if k % 7 == 6 else x, x, start=True, stop=True)
                                mm.then_inc(tile_done, 1)
                            if what == "K":
                                b = free(lambda x: ("hK", 0, x, k), i, lo, hi)
                                pe.wait_ge(qk_ready, affine(lambda x: 2 * x + k + 1, i, lo, hi))
                                for c in range(TC):
                                    r = slice(c * P, (c + 1) * P)
                                    mm = nc.tensor.transpose(b[:, r], khT[:, r], ident[:])
                                mm.then_inc(tile_done, 1)
                            if what == "U":
                                b = free(lambda x: ("hU", 0, x, k), i, lo, hi)
                                pe.wait_ge(tile_read, affine(lambda x: TL.n[("hK", 0, x, k)] + 1, i, lo, hi))
                                for c in range(TC - 1):
                                    mm = mm_f(b[:, c * P:(c + 1) * P], kh[:, c, :], vv[:, c, k * P:(k + 1) * P], start=True, stop=True)
                                mm.then_inc(tile_done, 1)
                            if what == "O":
                                b = free(lambda x: ("hO", 0, x, k), i, lo, hi)
                                pe.wait_ge(tile_read, affine(lambda x: TL.n[("hL", 0, x, 7 * k + 6)] + 1, i, lo, hi))
                                for c in range(TC):
                                    r = slice(c * P, (c + 1) * P)
                                    mm = mm_f(b[:, r], sc[:, k, c, :], vv[:, c, k * P:(k + 1) * P], start=True, stop=c == 0)
                                    if c:
                                        mm = mm_f(b[:, r], qhat[:, k, r], st[:, k, c - 1, :], start=False, stop=True)
                                mm.then_inc(tile_done, 1)
                            if what == "N":
                                b = free(lambda x: ("hN", 0, x, k), i, lo, hi)
                                pe.wait_ge(on_ready, affine(lambda x: 2 * x + k + 1, i, lo, hi))
                                for c in range(TC):
                                    r = slice(c * P, (c + 1) * P)
                                    mm = nc.tensor.transpose(b[:, r], osb[:, k, r], ident[:])
                                mm.then_inc(tile_done, 1)
                            if what == "hg":
                                if k == 0:
                                    block_in("hg", 0, i, lo, hi)
                                columns("hg", 0, i, lo, hi, k)
                            if what == "hd":
                                down(0, i, lo, hi, 1, "hd", k)
                            if what == "hf":
                                if k == 0:
                                    block_in("hf", 0, i, lo, hi, -1)
                                columns("hf", 0, i, lo, hi, k, None, -1)
                            if what == "hq":
                                if k == 0:
                                    block_in("hq", 0, i, lo, hi, -1)
                                columns("hq", 0, i, lo, hi, k, None, -1)
                            if what == "sx":
                                if k == 0:
                                    block_in("sx", 0, 0, 0, 1)
                                columns("sx", 0, 0, 0, 1, k)

                    block_in("hf", 0, 0, 0, 1)
                    columns("hf", 0, 0, 0, 1, 0, n)
                    stat(n)
                    columns("hf", 0, 0, 0, 1, 1)
                    small_logits("dlog", dsh, dsl)
                    rms_by_token("hrt")
                    block_in("hq", 0, 0, 0, 1)
                    columns("hq", 0, 0, 0, 1, 0)
                    columns("hq", 0, 0, 0, 1, 1)
                    hgrn_step(0, 0, 1, hgrn_steps(0))
                    with pe.Fori(1, NQ - 1) as i:
                        hgrn_step(i, 1, NQ - 1, hgrn_steps(1))
                    hgrn_step(NQ - 1, NQ - 1, NQ, hgrn_steps(NQ - 1))
                    heads_first("dlogT", dlog)
                    block_in("sb", 0, 0, 0, 1)
                    columns("sb", 0, 0, 0, 1, 0)
                    columns("sb", 0, 0, 0, 1, 1)
                    for m in range(KD):
                        down(0, NQ, NQ, NQ + 1, 1, "hd", m)
                        if m == 3:
                            b = free(lambda x: ("cst",), 0, 0, 1)
                            pe.wait_ge(dec_exp, 1)
                            for a, src in enumerate((dcs, dts, dde)):
                                for c in range(TC):
                                    mm = nc.tensor.transpose(b[:, (a * TC + c) * NH:(a * TC + c + 1) * NH],
                                                             src[:, c * P:(c + 1) * P], ident[0:NH, 0:NH])
                            mm.then_inc(tile_done, 1)
                    pe.wait_ge(cols_ready, 1)
                    mm_f(banks[7][:], ones[:], yy[:, KD - 1, :], start=True, stop=False)

                    def ssd_step(i, lo, hi, steps):
                        for what, k in steps:
                            if what == "sz":
                                if k == 0:
                                    block_in("sz", 0, i, lo, hi)
                                columns("sz", 0, i, lo, hi, k)
                            if what in ("sx", "sb"):
                                if k == 0:
                                    block_in(what, 0, i, lo, hi, -1)
                                columns(what, 0, i, lo, hi, k, None, -1)
                            if what == "sX":
                                b = free(lambda x: ("sX", 0, x, k), i, lo, hi)
                                pe.wait_ge(xc_ready, affine(lambda x: 4 * x + 2, i, lo, hi))
                                for c in range(2):
                                    for m in range(2):
                                        r = slice((2 * k + c) * P, (2 * k + c + 1) * P)
                                        mm = nc.tensor.transpose(b[:, c * CB + m * P:c * CB + (m + 1) * P], xc[:, m, r], ident[:])
                                mm.then_inc(tile_done, 1)
                            if what == "sB":
                                b = free(lambda x: ("sB", 0, x, k), i, lo, hi)
                                pe.wait_ge(xc_ready, affine(lambda x: 4 * x + 4, i, lo, hi))
                                for c in range(TC):
                                    r = slice(c * P, (c + 1) * P)
                                    mm = nc.tensor.transpose(b[:, r], xc[:, 2, r], ident[:])
                                mm.then_inc(tile_done, 1)
                            if what == "sC":
                                b = free(lambda x: ("sC", 0, x, k), i, lo, hi)
                                for c in range(TC):
                                    r = slice(c * P, (c + 1) * P)
                                    mm = mm_f(b[:, r], xc[:, 2, r], xc[:, 3, r], start=True, stop=True)
                                mm.then_inc(tile_done, 1)
                            if what == "sR":
                                b = free(lambda x: ("sR", 0, x, k), i, lo, hi)
                                pe.wait_ge(csg_in, affine(lambda x: 16 * x + 16, i, lo, hi))
                                mm_f(b[:], sel[:, k, :], csg[:], start=True, stop=True).then_inc(tile_done, 1)
                            if what == "sU":
                                b = free(lambda x: ("sU", 0, x, k), i, lo, hi)
                                pe.wait_ge(xdd_ready, affine(lambda x: 2 * x + 2, i, lo, hi))
                                pe.wait_ge(tile_read, affine(lambda x: TL.n[("sB", 0, x, 0)] + 1, i, lo, hi))
                                for c in range(2 - k):
                                    mm = mm_f(b[:, c * CB:(c + 1) * CB], bt[:, 2 * k + c, :], xdd4[:, 2 * k + c, :], start=True, stop=True)
                                mm.then_inc(tile_done, 1)
                            if what == "sY":
                                b = free(lambda x: ("sY", 0, x, k), i, lo, hi)
                                pe.wait_ge(mc_ready, affine(lambda x: 4 * x + 2 * k + 2, i, lo, hi))
                                pe.wait_ge(st_ready, affine(lambda x: 2 * x + k + 1, i, lo, hi))
                                for e in range(2):
                                    h = 2 * k + e
                                    o = slice(e * SP_, (e + 1) * SP_)
                                    f = slice(h * SP_, (h + 1) * SP_)
                                    for c in range(TC):
                                        r = slice(c * P, (c + 1) * P)
                                        mm = mm_f(b[o, r], xdt4[:, c, f], mm_[:, e, r], start=True, stop=c == 0)
                                        if c:
                                            mm = mm_f(b[o, r], ub[:, c - 1, f], cx[:, e, r], start=False, stop=True)
                                mm.then_inc(tile_done, 1)
                        for m in range(2):
                            pe.wait_ge(ysq_ready, affine(lambda x: 2 * x + m + 1, i, lo, hi))
                            mm_f(banks[7][:], ones[:], ysq[:, m, :], start=False,
                                 stop=isinstance(i, int) and i == G4 - 1 and m == 1).then_inc(ystat_done, 1)
                    ssd_step(0, 0, 1, ssd_steps(0))
                    with pe.Fori(1, G4 - 1) as i:
                        ssd_step(i, 1, G4 - 1, ssd_steps(1))
                    ssd_step(G4 - 1, G4 - 1, G4, ssd_steps(G4 - 1))
                    for j in range(NQ):
                        s = block_in("so", 0, j, j, j + 1)
                        for m in range(2):
                            b = free(lambda x: ("so", 0, j, m), 0, 0, 1)
                            for k in range(KD):
                                if j == 0 and m == 0:
                                    pe.wait_ge(yu_ready, k + 1)
                                c = slice(k * CB + m * P, k * CB + (m + 1) * P)
                                mm = product(b[:], wh[s][:, c], wl[s][:, c], uh[:, k, :], ul[:, k, :], k == 0, k == KD - 1)
                            mm.then_inc(tile_done, 1)
                if part[0] == "fox":
                    def fox_step(i, lo, hi):
                        peeled = isinstance(i, int)
                        if not peeled:
                            block_in("fq", 0, i, lo, hi)
                            columns("fq", 0, i, lo, hi, 0)
                            columns("fq", 0, i, lo, hi, 1)
                            outputs(i, lo, hi)
                        block_in("fk", 0, i, lo, hi)
                        columns("fk", 0, i, lo, hi, 0)
                        columns("fk", 0, i, lo, hi, 1)
                        if not peeled:
                            down(0, i, lo, hi, 1, "fd")
                        tokens("fv", i, lo, hi)
                        pe.wait_ge(tile_read, affine(lambda x: TL.n[("fv", 0, x, 1)] + 1, i, lo, hi))
                        pe.wait_ge(aug_in, affine(lambda x: 64 * (x + 1), i, lo, hi))
                        for what, h in FOX_STEPS:
                            if what == "S":
                                for c in range(TC):
                                    scores(i, lo, hi, h, c)
                            if what == "T":
                                pe.wait_ge(exp_done, affine(lambda x: x * HPB * TC + (h + 1) * TC, i, lo, hi))
                                for m in range(3):
                                    b = free(lambda x: ("fT", 0, x, h, m), i, lo, hi)
                                    for k, (at, col) in PT_AT.items():
                                        for c in range(k, TC):
                                            if at == m:
                                                mm = nc.tensor.transpose(
                                                    b[:, col + (c - k) * P:col + (c - k + 1) * P],
                                                    pr[h % 2][:, c, k * P:(k + 1) * P], ident[:])
                                    mm.then_inc(tile_done, 1)
                            if what == "V":
                                pe.wait_ge(tile_read, affine(lambda x: TL.n[("fT", 0, x, h, 2)] + 1, i, lo, hi))
                                b = free(lambda x: ("fV", 0, x, h), i, lo, hi)
                                for c in range(TC):
                                    for k in range(c + 1):
                                        at, col = PT_AT[k]
                                        col += (c - k) * P
                                        mm = nc.tensor.matmul(b[:, c * HD:(c + 1) * HD], pt[h % 2][:, at, col:col + P],
                                                              vt[:, k, h * HD:(h + 1) * HD], start=k == 0, stop=k == c)
                                mm.then_inc(tile_done, 1)

                    def scores(i, lo, hi, h, c):
                        w, b = (c + 1) * P, banks[4 + c]
                        j = h * TC + c
                        if not (isinstance(i, int) and h == 0):
                            pe.wait_ge(exp_done, affine(lambda x: x * HPB * TC + j + 1 - TC, i, lo, hi))
                        nc.tensor.matmul(b[:, 0:w], qx[:, h, c * P:w], kx[:, h, 0:w], start=True, stop=False)
                        nc.tensor.matmul(b[:, c * P:w], identb[:], maskb[:], start=False, stop=True).then_inc(s_done, 1)

                    def outputs(i, lo, hi):
                        pe.wait_ge(tile_read, affine(lambda x: TL.n[("fV", 0, x - 1, HPB - 1)] + 1, i, lo, hi))
                        for m in range(2):
                            b = free(lambda x: ("fo", 0, x - 1, m), i, lo, hi)
                            for c in range(TC):
                                mm = nc.tensor.transpose(b[:, c * P:(c + 1) * P], ot[:, c, m * P:(m + 1) * P], ident[:])
                            mm.then_inc(tile_done, 1)

                    block_in("fq", 0, 0, 0, 1)
                    columns("fq", 0, 0, 0, 1, 0, n)
                    stat(n)
                    columns("fq", 0, 0, 0, 1, 1)
                    small_logits("flog", fsh, fsl)
                    pe.wait_ge(tile_read, TL.n[("flog",)] + 1)
                    heads_first("flogT", flog)
                    rms_by_token("frt")
                    fox_step(0, 0, 1)
                    with pe.Fori(1, NQ) as i:
                        fox_step(i, 1, NQ)
                    outputs(NQ, NQ, NQ + 1)
                    down(0, NQ, NQ, NQ + 1, 1, "fd")
            n = len(parts)
            pe.wait_ge(sq_ready, n * KD + KD)
            for c in range(TC):
                for k in range(KD):
                    mm = nc.tensor.matmul(stat_bank[:, c:c + 1], sq[:, k, c * P:(c + 1) * P], ones[:, 0:1],
                                          start=k == 0, stop=k == KD - 1)
            mm.then_inc(stat_done, 1)
            pe.wait_ge(u_ready, n * KD + KD)
            for c in range(TC):
                for h in range(2):
                    b = free(lambda x: ("out", 2 * c + h), 0, 0, 1)
                    for j in range(4):
                        mm = nc.tensor.transpose(b[:, j * P:(j + 1) * P], xg[:, 4 * h + j, c * P:(c + 1) * P], ident[:])
                    mm.then_inc(tile_done, 1)


_INS = ["x", "ffn1_norm", "ffn1_w_gate", "ffn1_w_up", "ffn1_w_down", "mix_norm", "hyb_w_in", "hgrn_lb_logits",
        "hgrn_out_gain", "ssd_conv_w", "ssd_conv_b", "ssd_dt_bias", "ssd_A_log", "ssd_D", "ssd_out_gain", "hyb_w_out",
        "fox_w_in", "fox_b_f", "fox_w_out", "ffn2_norm", "ffn2_w_gate", "ffn2_w_up", "ffn2_w_down", "final_norm"]


def kernel(**inputs):
    import concourse.bacc as _bacc
    from concourse.bass_utils import run_bass_kernel_spmd as _run

    nc = _bacc.Bacc("TRN2", target_bir_lowering=False, num_devices=1)
    arrays, aps = {}, {}
    for name in _INS:
        a = np.ascontiguousarray(inputs[name])
        arrays[f"in_{name}_dram"] = a
        aps[name] = nc.dram_tensor(f"in_{name}_dram", a.shape, mybir.dt.from_np(a.dtype), kind="ExternalInput").ap()
    out = nc.dram_tensor("out_0_dram", (1, T, D), F32, kind="ExternalOutput").ap()
    trunk(nc, aps, out, [("ffn", 0), ("hyb",), ("ffn", 1), ("ffn", 2), ("fox",), ("ffn", 3)])
    r = _run(nc, [arrays], core_ids=[0])
    return r.results[0]["out_0_dram"]
```

```python
from contextlib import ExitStack

import numpy as np

import concourse.bass as bass
from concourse import mybir
from concourse.alu_op_type import AluOpType as ALU

ACT = mybir.ActivationFunctionType
F32 = mybir.dt.float32
F32R = mybir.dt.float32r
U32 = mybir.dt.uint32
AX = mybir.AxisListType

P = 128
T = 512
D = 1024
KD = D // P
FF = 2816
CB = 256
NF = FF // CB
TC = T // P
EPS = 1e-6
HD = 64
HPB = CB // HD
NQ = D // CB
NH = D // HD
FOX_SMALL = 3 * D
BF16 = mybir.dt.bfloat16
NEG = -1e30
HEADS2 = 2
TINY = 1e-20
LOG_SPLIT = 2.0 ** -60
G4 = 4
SP_ = 64
CONV = 4
HYB_X, HYB_SMALL = 5 * D, 7 * D
SLOTS = 3


def affine(fn, i, lo, hi):
    if isinstance(i, int):
        return fn(i)
    vals = [fn(x) for x in range(lo, hi)]
    step = vals[1] - vals[0] if len(vals) > 1 else 0
    assert all(b - a == step for a, b in zip(vals, vals[1:])), vals
    base = vals[0] - lo * step
    out = i * step if step != 1 else i
    return out + base if base else out


def at_least(fn, own, i, lo, hi):
    if isinstance(i, int):
        return fn(i)
    vals = [fn(x) for x in range(lo, hi)]
    step = vals[-1] - vals[-2]
    base = max(y - step * x for x, y in zip(range(lo, hi), vals))
    assert all(base + step * x <= own(x) for x in range(lo, hi))
    return i * step + base


HG_LINKS, SSD_LINKS, FFN_LINKS, FOX_LINKS = 16, 13, 4, 6


class Links:

    def __init__(self, sem):
        self.sem, self.n, self.i, self.per = sem, 0, None, 0

    def enter(self, i, lo, per):
        self.i, self.lo, self.per, self.k = i, lo, per, 0

    def leave(self, trips):
        assert self.k == self.per, (self.k, self.per)
        self.n += trips * self.per
        self.i = None

    def step(self, eng, ins):
        ins.then_inc(self.sem, 1)
        if self.i is None:
            self.n += 1
            eng.wait_ge(self.sem, self.n)
        else:
            self.k += 1
            eng.wait_ge(self.sem, self.i * self.per + (self.n - self.lo * self.per + self.k))


class Blocks:

    def __init__(self):
        self.order, self.slot, self.nth, self.last_use = [], {}, {}, [-3, -2, -1]
        self.count = [0] * SLOTS
        self.prev = {}
        self.held = [None] * SLOTS
        self.landed, self.lands, self.next_lands = [0] * SLOTS, {}, {}

    def add(self, key, slot=None):
        if slot is None:
            slot = min(range(SLOTS), key=lambda s: self.last_use[s])
        self.slot[key], self.nth[key] = slot, self.count[slot]
        self.prev[key] = self.held[slot]
        self.held[slot] = key
        self.landed[slot] += 32 if key[0] == "sb" else 16
        self.lands[key] = self.next_lands[self.prev[key]] = self.landed[slot]
        self.last_use[slot] = len(self.order)
        self.count[slot] += 1
        self.order.append(key)

    def body(self, keys_at, lo, hi, first=None):
        for i in range(lo, hi):
            for j, key in enumerate(keys_at(i)):
                self.add(key, None if first is None else first[j])
            if first is None:
                first = [self.slot[k] for k in keys_at(i)]


def plan_blocks(parts):
    b = Blocks()
    for part in parts:
        if part[0] == "ffn":
            f = part[1]
            b.add(("g", f, 0)); b.add(("u", f, 0))
            b.body(lambda i: [("g", f, i), ("u", f, i), ("d", f, i - 1)], 1, NF)
            b.add(("d", f, NF - 1))
        if part[0] == "hyb":
            s0, s1, s2 = sorted(range(SLOTS), key=lambda s: b.last_use[s])
            for kind, at, s in (("hf", 0, s0), ("hq", 0, s1), ("hv", 0, s0), ("hg", 0, s2), ("hf", 1, s0), ("hq", 1, s1)):
                b.add((kind, 0, at), s)
            b.body(lambda i: [("hv", 0, i), ("hg", 0, i), ("hd", 0, i - 1), ("hf", 0, i + 1), ("hq", 0, i + 1)],
                   1, NQ - 1, [s0, s2, s1, s0, s1])
            for kind, at, s in (("hv", 3, s0), ("hg", 3, s2), ("hd", 2, s1), ("sx", 0, s0), ("sb", 0, s2), ("hd", 3, s1)):
                b.add((kind, 0, at), s)
            b.body(lambda i: [("sz", 0, i), ("sb", 0, i + 1), ("sx", 0, i + 1)], 0, G4 - 1)
            b.add(("sz", 0, G4 - 1))
            for j in range(NQ):
                b.add(("so", 0, j))
        if part[0] == "fox":
            for kind in ("fq", "fk", "fv"):
                b.add((kind, 0, 0))
            b.body(lambda i: [("fq", 0, i), ("fk", 0, i), ("fd", 0, i - 1), ("fv", 0, i)], 1, NQ)
            b.add(("fd", 0, NQ - 1))
    return b


FOX_STEPS = [("S", 0), ("S", 1), ("T", 0), ("S", 2), ("T", 1), ("V", 0), ("S", 3), ("T", 2), ("V", 1),
             ("T", 3), ("V", 2), ("V", 3)]
PT_AT = {0: (0, 0), 1: (1, 0), 3: (1, 384), 2: (2, 0)}


def hgrn_steps(i):
    steps = [("L", 0), ("hg", 0), ("L", 1), ("K", 0), ("L", 2), ("hd", 0), ("hd", 1), ("L", 3), ("U", 0),
             ("hg", 1), ("L", 4), ("hd", 2), ("hd", 3), ("L", 5), ("hf", 0), ("L", 6), ("hd", 4), ("L", 7),
             ("K", 1), ("L", 8), ("hd", 5), ("L", 9), ("hd", 6), ("U", 1), ("L", 10), ("hd", 7),
             ("L", 11), ("L", 12), ("hf", 1), ("L", 13), ("O", 0), ("O", 1), ("hq", 0), ("hq", 1), ("sx", 0), ("sx", 1),
             ("N", 0), ("N", 1)]
    gone = {"hd", "sx"} if i == 0 else {"hf", "hq"} if i == NQ - 1 else {"sx"}
    return [x for x in steps if x[0] not in gone]


CONV_AT = {2: 0, 3: 1, 0: 2, 1: 3}


def ssd_steps(i):
    steps = [("sz", 0), ("sz", 1), ("sX", 0), ("sX", 1), ("sB", 0), ("sC", 0), ("sR", 0), ("sR", 1), ("sU", 0), ("sU", 1),
             ("sb", 0), ("sY", 0), ("sR", 2), ("sR", 3), ("sb", 1), ("sx", 0), ("sY", 1), ("sx", 1)]
    return [x for x in steps if i < G4 - 1 or x[0] not in ("sx", "sb")]


class Tiles:

    def __init__(self):
        self.n, self.bank, self.prev, self.held = {}, {}, {}, [None] * 8

    def add(self, key, bank):
        self.n[key], self.bank[key] = len(self.n), bank
        self.prev[key] = -1 if self.held[bank] is None else self.n[self.held[bank]]
        self.held[bank] = key


def plan_tiles(parts):
    t = Tiles()
    for m in range(KD):
        t.add(("in", m), 4 + m % 4)
    t.add(("rows",), 0)
    if ("hyb",) in parts:
        t.add(("rows2",), 1)
        t.add(("rows3",), 2)
    for part in parts:
        if part[0] == "ffn":
            f = part[1]
            for i in range(NF + 1):
                if i < NF:
                    for m in range(2):
                        t.add(("g", f, i, m), m)
                    for m in range(2):
                        t.add(("u", f, i, m), 2 + m)
                if i:
                    for m in range(KD):
                        t.add(("d", f, i - 1, m), 4 + m % 4)
        if part[0] == "hyb":
            two = lambda kind, i, b0: [t.add((kind, 0, i, m), b0 + m) for m in range(2)]
            two("hf", 0, 0)
            two("hq", 0, 2)
            t.add(("dlog",), 4)
            t.add(("dlogT",), 5)
            t.add(("hrt",), 6)
            for i in range(NQ):
                two("hv", i, 2)
                for what, k in hgrn_steps(i):
                    bank = {"L": 6 + k % 2, "K": k, "O": k, "U": 1, "N": k, "hd": 4 + k % 2}.get(what, 2 + k)
                    at = i + {"hf": 1, "hq": 1, "hd": -1, "sx": -i}.get(what, 0)
                    t.add(("h" + what if len(what) == 1 else what, 0, at, k), bank)
            two("sb", 0, 0)
            t.add(("cst",), 2)
            t.add(("csh",), 3)
            for m in range(KD):
                t.add(("hd", 0, NQ - 1, m), 4 + m % 4)
            for i in range(G4):
                for what, k in ssd_steps(i):
                    bank = {"sz": 4 + k, "sX": k, "sB": 2, "sC": 3, "sU": k, "sR": 4 + k % 2, "sY": 6,
                            "sx": k, "sb": 2 + k}[what]
                    t.add((what, 0, i + (what in ("sx", "sb")), k), bank)
            for j in range(NQ):
                for m in range(2):
                    t.add(("so", 0, j, m), (2 * j + m) % 4)
        if part[0] == "fox":
            for i in range(NQ + 1):
                if i < NQ:
                    for m in range(2):
                        t.add(("fq", 0, i, m), m)
                if i:
                    for m in range(2):
                        t.add(("fo", 0, i - 1, m), 4 + m)
                if i < NQ:
                    for m in range(2):
                        t.add(("fk", 0, i, m), 2 + m)
                        if i == 0 and m == 0:
                            t.add(("flog",), 4)
                        elif i == 0:
                            t.add(("flogT",), 5)
                            t.add(("frt",), 6)
                if i:
                    for m in range(KD):
                        t.add(("fd", 0, i - 1, m), 4 + m % 4)
                if i < NQ:
                    for m in range(2):
                        t.add(("fv", 0, i, m), m)
                        if i == 0 and m == 0:
                            t.add(("fcum",), 4)
                    for what, h in FOX_STEPS:
                        if what == "T":
                            for m in range(3):
                                t.add(("fT", 0, i, h, m), m)
                        if what == "V":
                            t.add(("fV", 0, i, h), 3)
    for m in range(2 * TC):
        t.add(("out", m), m % 4)
    return t


def trunk(nc, A, out, parts):
    B, TL = plan_blocks(parts), plan_tiles(parts)
    ffns = [p[1] for p in parts if p[0] == "ffn"]
    gains = [A["ffn1_norm"], A["mix_norm"], A["ffn2_norm"], A["final_norm"].rearrange("(a d) -> a d", a=1)]
    gain_at = [4 * (p[1] % 2) + p[1] // 2 if p[0] == "ffn" else {"hyb": 2, "fox": 3}[p[0]] for p in parts] + [6]
    NN = 7

    ctx = ExitStack()
    with ctx:
        def sb(name, shape, dt=F32):
            return ctx.enter_context(nc.sbuf_tensor(name, shape, dt))

        def sem(name):
            return ctx.enter_context(nc.semaphore(name))

        xT = sb("xT", [P, KD, T])
        uh = sb("uh", [P, KD, T], F32R)
        ul = sb("ul", [P, KD, T], F32R)
        sq = sb("sq", [P, KD, T])
        rstd = sb("rstd", [P, T])
        var = sb("var", [P, T])
        raw = [sb(f"raw{s}", [P, KD * CB]) for s in range(SLOTS)]
        wh = [sb(f"wh{s}", [P, KD * CB], F32R) for s in range(SLOTS)]
        wl = [sb(f"wl{s}", [P, KD * CB], F32R) for s in range(SLOTS)]
        gain = sb("gain", [P, NN, KD])
        ident = sb("ident", [P, P])
        ones = sb("ones", [P, P])
        causal = sb("causal", [P, P])
        after = sb("after", [P, P])
        hh = sb("hh", [P, 2, T], F32R)
        hl = sb("hl", [P, 2, T], F32R)
        logits_h = sq[0:NH, 2, :]
        rtok = sb("rtok", [P, TC])
        vtok = sb("vtok", [P, TC])
        cw = sb("cw", [P, CONV + 1, 16])
        hcols = sb("hcols", [P, 3, KD])
        scols = sb("scols", [P, 2, KD])
        lbt = sb("lbt", [P, KD])
        with (nc.sbuf_tensor("rows", [NN * KD, P], F32) as rows,
              nc.sbuf_tensor("rows2", [CONV * 16, P], F32) as rows2,
              nc.sbuf_tensor("dpair", [KD, 2], F32) as dpair,
              nc.sbuf_tensor("rows3", [48, P], F32) as rows3):
            pass
        with (nc.sbuf_tensor("gs", [P, 2, T], F32) as gs, nc.sbuf_tensor("us", [P, 2, T], F32) as us,
              nc.sbuf_tensor("hh_last", [P, 2, T], F32R) as hh_last, nc.sbuf_tensor("hl_last", [P, 2, T], F32R) as hl_last,
              nc.sbuf_tensor("xg", [P, KD, T], F32) as xg):
            pass
        fox_ctx = ExitStack()
        fb = lambda name, shape, dt=F32: fox_ctx.enter_context(nc.sbuf_tensor(name, shape, dt))
        qx = fb("qx", [P, HPB, T])
        kx = fb("kx", [P, HPB, T])
        vt = fb("vt", [P, TC, CB])
        pr = [fb(f"pr{b}", [P, TC, T]) for b in range(2)]
        pt = [fb(f"pt{b}", [P, 3, T]) for b in range(2)]
        ot = fb("ot", [P, TC, CB])
        negmax = fb("negmax", [P, HPB * TC])
        rowsum = fb("rowsum", [P, HPB * TC])
        rrow = fb("rrow", [P, HPB * TC])
        rt = fb("rt", [P, TC])
        flog = fb("flog", [P, TC * NH])
        fcum = [pr[1][0:NH, b, :] for b in range(2)]
        ftmp = fb("ftmp", [P, 5, TC * NH])
        bfrow = fb("bfrow", [P, NH])
        identb = fb("identb", [P, P], BF16)
        maskb = fb("maskb", [P, P], BF16)
        fsr = fb("fsr", [P, KD * NH])
        fsh = fb("fsh", [P, KD * NH], F32R)
        fsl = fb("fsl", [P, KD * NH], F32R)
        cum_dram = nc.dram_tensor("cum_dram", (2, NH, T), F32, kind="Internal").ap()
        fox_ctx.close()
        hyb_ctx = ExitStack()
        hb = lambda name, shape, dt=F32: hyb_ctx.enter_context(nc.sbuf_tensor(name, shape, dt))
        U8 = mybir.dt.uint8
        waited = hb("waited", [P, 14])
        lmask = hb("lmask", [P, 7, P], U8)
        sel = hb("sel", [G4, G4, P])
        tok3 = hb("tok3", [P, 3, TC, NH])
        tokg = hb("tokg", [P, 3, TC, G4])
        hc = hb("hc", [P, 3, 2])
        hgain = hb("hgain", [P, 2])
        wc = hb("wc", [P, CONV + 1, 4])
        hrt = hb("hrt", [P, TC])
        dsr = hb("dsr", [P, KD * NH])
        dsh = hb("dsh", [P, KD * NH], F32R)
        dsl = hb("dsl", [P, KD * NH], F32R)
        dtb = hb("dtb", [P, NH])
        alog = hb("alog", [P, NH])
        dlog = hb("dlog", [P, TC * NH])
        cs_dram = nc.dram_tensor("cs_dram", (NH, T), F32, kind="Internal").ap()
        hg_ctx = ExitStack()
        gb = lambda name, shape, dt=F32: hg_ctx.enter_context(nc.sbuf_tensor(name, shape, dt))
        fz = gb("fz", [P, 2, T])
        kk = gb("kk", [P, 2, T])
        qq = gb("qq", [P, 2, T])
        bb = gb("bb", [P, 2, T])
        vv = gb("vv", [P, TC, CB])
        khT = gb("khT", [P, T])
        kh = gb("kh", [P, TC, P])
        osum = gb("osum", [P, 2 * TC])
        ovar = gb("ovar", [P, 2 * TC])
        lx2 = gb("lx2", [P, T])
        gg = gb("gg", [P, 2, T])
        qhat = gb("qhat", [P, 2, T])
        etot = gb("etot", [P, 2, TC])
        lev = gb("lev", [P, 2, T])
        lx = gb("lx", [P, 2, T])
        sc = gb("sc", [P, 2, TC, P])
        st = gb("st", [P, 2, TC - 1, P])
        hg_ctx.close()
        t1, osq, osb = (sq[:, 2 * n:2 * n + 2, :] for n in range(3))
        dcs = sq[0:NH, 0, :]
        dtt = sq[:, 1, 0:5 * TC * NH].rearrange("p (n c) -> p n c", n=5)
        ss_ctx = ExitStack()
        cb_ = lambda name, shape, dt=F32: ss_ctx.enter_context(nc.sbuf_tensor(name, shape, dt))
        yy = cb_("yy", [P, KD, T])
        xpad = cb_("xpad", [P, 4, T + CONV - 1])
        xc = cb_("xc", [P, 4, T])
        bt = cb_("bt", [P, TC, P])
        cbm = cb_("cbm", [P, TC, P])
        mm_ = cb_("mm", [P, 2, T])
        cx = cb_("cx", [P, 2, T])
        ecs = cb_("ecs", [P, 2, T])
        ub = cb_("ub", [P, TC - 1, CB])
        csg = var[0:G4, :]
        ss_ctx.close()
        xdt, xdd, zs, ysq = (sq[:, 2 * n:2 * n + 2, :] for n in range(4))
        xdt4, xdd4 = (x.rearrange("p a (c f) -> p (a c) f", c=2) for x in (xdt, xdd))
        hyb_ctx.close()

        banks = [ctx.enter_context(nc.psum_tensor(f"bank{n}", [P, T], F32)) for n in range(8)]
        stat_bank = banks[7]

        landed = [sem(f"landed{s}") for s in range(SLOTS)]
        hi_done = [sem(f"hi_done{s}") for s in range(SLOTS)]
        lo_done = [sem(f"lo_done{s}") for s in range(SLOTS)]
        tile_done = sem("tile_done")
        tile_read = sem("tile_read")
        x_in = [sem(f"x_in{h}") for h in range(2)]
        gains_in = sem("gains_in"); const_ready = sem("const_ready")
        uh_ready = sem("uh_ready")
        u_ready = sem("u_ready")
        sq_ready = sem("sq_ready")
        sum_ready = sem("sum_ready")
        stat_done = sem("stat_done")
        var_ready = sem("var_ready")
        rms_ready = sem("rms_ready")
        silu_ready = sem("silu_ready")
        h_ready = sem("h_ready")
        hd_ready = sem("hd_ready")
        stored = sem("stored")
        small_in = sem("small_in"); small_hi = sem("small_hi"); small_lo = sem("small_lo"); fsmall_hi = sem("fsmall_hi")
        fox_const = sem("fox_const")
        lse_ready = sem("lse_ready")
        exp_l_ready = sem("exp_l_ready")
        cum_ready = sem("cum_ready"); cum_stored = sem("cum_stored"); aug_in = sem("aug_in")
        params_in = sem("params_in"); dpair_in = sem("dpair_in"); d_spread = sem("d_spread")
        lb_asked = sem("lb_asked"); lb_exp = sem("lb_exp")
        hyb_const = sem("hyb_const"); dt_asked = sem("dt_asked"); dt_exp = sem("dt_exp")
        dec_asked = sem("dec_asked"); dec_exp = sem("dec_exp")
        cs_stored = sem("cs_stored"); csg_in = sem("csg_in"); d_in = sem("d_in")
        sig_ready = sem("sig_ready")
        ln_asked = sem("ln_asked"); ln_ready = sem("ln_ready")
        b_ready = sem("b_ready")
        eb_ready = sem("eb_ready")
        qk_ready = sem("qk_ready")
        lev_ready = sem("lev_ready")
        dec_ready = sem("dec_ready")
        lx_ready = sem("lx_ready")
        osq_ready = sem("osq_ready")
        on_ready = sem("on_ready"); ovar_ready = sem("ovar_ready"); oroot_ready = sem("oroot_ready"); gsilu_ready = sem("gsilu_ready")
        cols_ready = sem("cols_ready")
        tap_ready = sem("tap_ready")
        conv_ready = sem("conv_ready")
        xc_ready = sem("xc_ready")
        zsilu_ready = sem("zsilu_ready")
        xdd_ready = sem("xdd_ready"); ecs_ready = sem("ecs_ready")
        dexp_ready = sem("dexp_ready"); mc_ready = sem("mc_ready"); st_ready = sem("st_ready")
        ysq_ready = sem("ysq_ready"); y_ready = sem("y_ready")
        ystat_done = sem("ystat_done"); yvar_ready = sem("yvar_ready"); yroot_ready = sem("yroot_ready")
        yu_ready = sem("yu_ready"); yy_zero = sem("yy_zero")
        flog_ready = sem("flog_ready"); a_ready = sem("a_ready")
        qkv_ready = sem("qkv_ready")
        s_done = sem("s_done")
        negmax_ready = sem("negmax_ready")
        exp_done = sem("exp_done")
        dve_sem = sem("dve_steps"); pool_sem = sem("pool_steps")

        def last_tile_of_x(n, m):
            if n == 0:
                return ("in", m)
            p = parts[n - 1]
            return {"ffn": ("d", p[-1], NF - 1, m), "hyb": ("so", 0, m // 2, m % 2), "fox": ("fd", 0, NQ - 1, m)}[p[0]]

        def gu_src(key_kind, f, i):
            w = A[("ffn1" if f % 2 == 0 else "ffn2") + {"g": "_w_gate", "u": "_w_up"}[key_kind]][f // 2]
            return w[:, bass.ts(i, CB)].rearrange("(k p) c -> p k c", p=P)

        def d_src(f, i):
            w = A[("ffn1" if f % 2 == 0 else "ffn2") + "_w_down"][f // 2]
            return w[bass.ts(i, CB), :].rearrange("(k p) c -> p k c", p=P)

        def source(kind, f, i, skip=0):
            if kind == "d":
                return d_src(f, i)
            if kind in ("g", "u"):
                return gu_src(kind, f, i)
            if kind == "fd":
                return A["fox_w_out"][0][bass.ts(i, CB), :].rearrange("(k p) c -> p k c", p=P)
            if kind == "hd":
                return A["hyb_w_out"][0][:D, :][bass.ts(i, CB), :].rearrange("(k p) c -> p k c", p=P)
            if kind == "so":
                return A["hyb_w_out"][0][D:, :][:, bass.ts(i, CB)].rearrange("(k p) c -> p k c", p=P)
            col = {"hq": 0, "hf": D, "hv": 2 * D, "hg": 3 * D, "sz": 4 * D, "sx": 5 * D}.get(kind)
            if col is not None:
                return A["hyb_w_in"][0][:, col + skip:col + D][:, bass.ts(i, CB)].rearrange("(k p) c -> p k c", p=P)
            col = {"fq": 0, "fk": D, "fv": 2 * D}[kind]
            return A["fox_w_in"][0][:, col:col + D][:, bass.ts(i, CB)].rearrange("(k p) c -> p k c", p=P)

        block = ctx.enter_context(nc.Block())

        @block.sync
        def _(sp):
            def load(kind, f, i, lo, hi, shift=0):
                s = B.slot[(kind, f, (i if isinstance(i, int) else lo) - shift)]
                at, skip = i - shift if shift else i, 0
                if kind == "hq" and not isinstance(i, int):
                    at, skip = i, -shift * CB
                if not (isinstance(i, int) and B.nth[(kind, f, i - shift)] == 0):
                    sp.wait_ge(lo_done[s], affine(lambda x: B.nth[(kind, f, x - shift)], i, lo, hi))
                dst = raw[s].rearrange("p (k c) -> p k c", k=2 if kind in ("d", "fd", "hd") else KD)
                if kind == "sb":
                    for h in range(2):
                        c0 = 6 * D + h * G4 * P
                        src = A["hyb_w_in"][0][:, c0:c0 + G4 * P][:, bass.ts(at, P)].rearrange("(k p) c -> p k c", p=P)
                        sp.dma_start(dst[:, :, h * P:(h + 1) * P], src).then_inc(landed[s], 16)
                    return
                sp.dma_start(dst, source(kind, f, at, skip)).then_inc(landed[s], 16)

            for n, g in enumerate(gains):
                src = g.rearrange("a (k p) -> (a k) p", p=P)
                sp.dma_start(rows[2 * n * KD:2 * n * KD + src.shape[0], :], src).then_inc(gains_in, 16)
            for h in range(2):
                sp.dma_start(sq.rearrange("p (c h) t -> p c h t", h=2)[:, :, h, :],
                             A["x"][0][:, h * T:(h + 1) * T].rearrange("(c p) d -> p c d", p=P)).then_inc(x_in[h], 16)
            for part in parts:
                if part[0] == "ffn":
                    f = part[1]
                    load("g", f, 0, 0, 1)
                    load("u", f, 0, 0, 1)
                    first = 2 if B.nth[("d", f, 0)] == 0 else 1
                    for i in range(1, first):
                        load("g", f, i, i, NF)
                        load("u", f, i, i, NF)
                        load("d", f, i, i, NF, 1)
                    with sp.Fori(first, NF) as i:
                        load("g", f, i, first, NF)
                        load("u", f, i, first, NF)
                        load("d", f, i, first, NF, 1)
                    load("d", f, NF - 1, NF - 1, NF)
                if part[0] == "hyb":
                    for kind, at in (("hf", 0), ("hq", 0), ("hv", 0), ("hg", 0), ("hf", 1), ("hq", 1)):
                        load(kind, 0, at, at, at + 1)
                    with sp.Fori(1, NQ - 1) as i:
                        for kind, shift in (("hv", 0), ("hg", 0), ("hd", 1), ("hf", -1), ("hq", -1)):
                            load(kind, 0, i, 1, NQ - 1, shift)
                    for kind, at in (("hv", 3), ("hg", 3), ("hd", 2), ("sx", 0), ("sb", 0), ("hd", 3)):
                        load(kind, 0, at, at, at + 1)
                    with sp.Fori(0, G4 - 1) as i:
                        for kind, shift in (("sz", 0), ("sb", -1), ("sx", -1)):
                            load(kind, 0, i, 0, G4 - 1, shift)
                    load("sz", 0, G4 - 1, G4 - 1, G4)
                    for j in range(NQ):
                        load("so", 0, j, j, j + 1)
                if part[0] == "fox":
                    for kind in ("fq", "fk", "fv"):
                        load(kind, 0, 0, 0, 1)
                    with sp.Fori(1, NQ) as i:
                        load("fq", 0, i, 1, NQ)
                        load("fk", 0, i, 1, NQ)
                        load("fd", 0, i, 1, NQ, 1)
                        load("fv", 0, i, 1, NQ)
                    load("fd", 0, NQ - 1, NQ - 1, NQ)
            for c in range(TC):
                for h in range(2):
                    sp.wait_ge(tile_read, TL.n[("out", 2 * c + h)] + 1)
                    sp.dma_start(out[0, c * P:(c + 1) * P, h * T:(h + 1) * T], sq[:, 2 * c + h, :]).then_inc(stored, 16)
            sp.wait_ge(stored, 16 * 2 * TC)

        @block.gpsimd
        def _(pool):
            pl = Links(pool_sem)
            nc.gpsimd.memset(ones[:], 1.0).then_inc(const_ready, 1)
            pl.step(pool, nc.gpsimd.memset(ident[:], 0.0))
            nc.gpsimd.affine_select(out=ident[:], in_=ident[:], compare_op=ALU.not_equal, fill=1.0, base=0,
                                    pattern=[[-1, P]], channel_multiplier=1).then_inc(const_ready, 1)
            for tri, sign, base in ((causal, 1, 0), (after, -1, -1)):
                pl.step(pool, nc.gpsimd.memset(tri[:], 1.0))
                nc.gpsimd.affine_select(out=tri[:], in_=tri[:], compare_op=ALU.is_ge, fill=0.0, base=base,
                                        pattern=[[sign, P]], channel_multiplier=-sign).then_inc(const_ready, 1)
            for n, part in enumerate(parts):
                if part[0] == "hyb":
                    pool.wait_ge(dpair_in, 16)
                    nc.gpsimd.tensor_copy(rows3[0:KD, :].rearrange("k (e c) -> k e c", e=2),
                                          dpair[:].unsqueeze(2).to_broadcast([KD, 2, SP_])).then_inc(d_spread, 1)
                    pool.wait_ge(tile_read, TL.n[last_tile_of_x(n, KD - 1) if n else ("rows3",)] + 1)
                    nc.gpsimd.dma_start(dtb[:], A["ssd_dt_bias"].to_broadcast([P, NH])).then_inc(d_in, 16)
                    nc.gpsimd.dma_start(alog[:], A["ssd_A_log"].to_broadcast([P, NH])).then_inc(d_in, 16)
                    nc.gpsimd.dma_start(dsr.rearrange("p (k c) -> p k c", k=KD),
                                        A["hyb_w_in"][0][:, HYB_SMALL:HYB_SMALL + NH].rearrange("(k p) c -> p k c", p=P)
                                        ).then_inc(d_in, 16)
                    pl.step(pool, nc.gpsimd.memset(sel[:], 1.0))
                    pl.step(pool, nc.gpsimd.affine_select(out=sel[:], in_=sel[:], compare_op=ALU.is_equal, fill=0.0,
                                                          base=0, pattern=[[-1, G4], [0, P]], channel_multiplier=1))
                    for l in range(7):
                        m = 64 >> l
                        mk = lev[:, 0, 0:P].rearrange("p (n h j) -> p n h j", h=2, j=m)
                        pl.step(pool, nc.gpsimd.memset(lev[:, 0, 0:P], 0.0 if l < 6 else 1.0))
                        if l < 6:
                            a = mk[:, :, 1, :]
                            pl.step(pool, nc.gpsimd.memset(a, 1.0))
                            pl.step(pool, nc.gpsimd.affine_select(out=a, in_=a, compare_op=ALU.is_ge, fill=0.0, base=0,
                                                                  pattern=[[-2 * m, P // (2 * m)], [0, m]], channel_multiplier=1))
                            pl.step(pool, nc.gpsimd.affine_select(out=a, in_=a, compare_op=ALU.is_ge, fill=0.0, base=m - 1,
                                                                  pattern=[[2 * m, P // (2 * m)], [0, m]], channel_multiplier=-1))
                        else:
                            a = lev[:, 0, 0:P].rearrange("p (n j) -> p n j", j=2)
                            pl.step(pool, nc.gpsimd.affine_select(out=a, in_=a, compare_op=ALU.is_ge, fill=0.0, base=0,
                                                                  pattern=[[-2, P // 2], [0, 2]], channel_multiplier=1))
                            pl.step(pool, nc.gpsimd.affine_select(out=a, in_=a, compare_op=ALU.is_ge, fill=0.0, base=0,
                                                                  pattern=[[2, P // 2], [1, 2]], channel_multiplier=-1))
                        pl.step(pool, nc.gpsimd.tensor_copy(lmask[:, l, :], lev[:, 0, 0:P]))
                    pl.step(pool, nc.gpsimd.memset(lx[:], 0.0))
                    nc.gpsimd.memset(sc[:], 0.0).then_inc(hyb_const, 1)
                if part[0] == "fox":
                    if n:
                        pool.wait_ge(tile_read, TL.n[last_tile_of_x(n, KD - 1)] + 1)
                    nc.gpsimd.dma_start(bfrow[:], A["fox_b_f"].to_broadcast([P, NH])).then_inc(small_in, 16)
                    nc.gpsimd.dma_start(fsr.rearrange("p (k c) -> p k c", k=KD),
                                        A["fox_w_in"][0][:, FOX_SMALL:FOX_SMALL + NH].rearrange("(k p) c -> p k c", p=P)
                                        ).then_inc(small_in, 16)
                    pl.step(pool, nc.gpsimd.memset(qx[:], 0.0))
                    pl.step(pool, nc.gpsimd.memset(kx[:], 0.0))
                    pl.step(pool, nc.gpsimd.memset(maskb[:], 0.0))
                    for x in (qx, kx):
                        pl.step(pool, nc.gpsimd.memset(x[HD:HD + 2, 0:HPB:2, :], 1.0))
                        pl.step(pool, nc.gpsimd.memset(x[0:2, 1:HPB:2, :], 1.0))
                    pool.wait_ge(const_ready, 2)
                    pl.step(pool, nc.gpsimd.tensor_copy(identb[:], ident[:]))
                    nc.gpsimd.affine_select(out=maskb[:], in_=maskb[:], compare_op=ALU.is_ge, fill=NEG, base=0,
                                            pattern=[[-1, P]], channel_multiplier=1).then_inc(fox_const, 1)

        @block.scalar
        def _(act):
            def split(kind, f, i, lo, hi, shift=0, after=None):
                s = B.slot[(kind, f, (i if isinstance(i, int) else lo) - shift)]
                act.wait_ge(landed[s], affine(lambda x: B.lands[(kind, f, x - shift)], i, lo, hi))
                nc.scalar.activation(wh[s][:], raw[s][:], ACT.Copy).then_inc(hi_done[s], 1)

            def split_next(kind, f, i, lo, hi, last_tile, shift=0):
                key = (kind, f, (i if isinstance(i, int) else lo) - shift)
                s = B.slot[key]
                if isinstance(i, int) and B.nth[key] + 1 == B.count[s]:
                    return
                act.wait_ge(tile_done, affine(lambda x: TL.n[(kind, f, x - shift, last_tile)] + 1, i, lo, hi))
                act.wait_ge(landed[s], affine(lambda x: B.next_lands.get((kind, f, x - shift), 0), i, lo, hi))
                nc.scalar.activation(wh[s][:], raw[s][:], ACT.Copy).then_inc(hi_done[s], 1)

            def high(n, m):
                nc.scalar.activation(uh[:, m, :], xT[:, m, :], ACT.Copy, scale=gain[:, gain_at[n], m:m + 1]).then_inc(uh_ready, 1)

            def squares(n):
                kind = parts[n - 1][0] if n else "in"
                if kind == "in":
                    for m in range(KD):
                        act.wait_ge(tile_read, max(TL.n[("in", m)], TL.n[("rows",)]) + 1)
                        high(n, m)
                    for key in B.order[1:SLOTS]:
                        first_split(key)
                    act.wait_ge(tile_done, TL.n[("in", KD - 1)] + 1)
                for m in range(KD):
                    if kind == "hyb" and m == KD - 2:
                        act.wait_ge(tile_done, TL.n[("so", 0, NQ - 1, 1)] + 1)
                        for k in range(m):
                            high(n, k)
                    act.wait_ge(tile_read, TL.n[last_tile_of_x(n, m)] + 1)
                    if n < len(parts) and kind in ("ffn", "fox") or kind == "hyb" and m >= KD - 2:
                        high(n, m)
                    nc.scalar.activation(sq[:, m, :], xT[:, m, :], ACT.Square).then_inc(sq_ready, 1)

            def root(n):
                act.wait_ge(var_ready, n + 1)
                nc.scalar.activation(rstd[:], var[:], ACT.Sqrt).then_inc(rms_ready, 1)

            def silu(f, i, lo, hi):
                for m in range(2):
                    act.wait_ge(tile_read, affine(lambda x: TL.n[("g", f, x, m)] + 1, i, lo, hi))
                    nc.scalar.activation(gs[:, m, :], gs[:, m, :], ACT.Silu).then_inc(silu_ready, 1)

            if ("hyb",) in parts:
                act.dma_start(dpair[:], A["ssd_D"].rearrange("a (k e) -> (a k) e", e=2)).then_inc(dpair_in, 16)
                act.dma_start(rows2[:], A["ssd_conv_w"][0].rearrange("k (c p) -> (k c) p", p=P)).then_inc(params_in, 16)
                for at, name in ((8, "ssd_conv_b"), (24, "hgrn_lb_logits"), (32, "hgrn_out_gain"), (40, "ssd_out_gain")):
                    src = A[name].rearrange("a (k p) -> (a k) p", p=P)
                    act.dma_start(rows3[at:at + src.shape[0], :], src).then_inc(params_in, 16)
            def first_split(key):
                s = B.slot[key]
                act.wait_ge(landed[s], B.lands[key])
                nc.scalar.activation(wh[s][:], raw[s][:], ACT.Copy).then_inc(hi_done[s], 1)
            first_split(B.order[0])
            for n, part in enumerate(parts):
                squares(n)
                if n == 0 and ("hyb",) in parts:
                    act.wait_ge(lb_asked, 1)
                    nc.scalar.activation(lbt[:], lbt[:], ACT.Exp).then_inc(lb_exp, 1)
                if n and parts[n - 1][0] == "ffn":
                    split_next("d", parts[n - 1][1], NF - 1, NF - 1, NF, KD - 1)
                if n and parts[n - 1][0] == "hyb":
                    split_next("so", 0, NQ - 1, NQ - 1, NQ, 1)
                if n and parts[n - 1][0] == "fox":
                    split_next("fd", 0, NQ - 1, NQ - 1, NQ, KD - 1)
                root(n)
                if part[0] == "ffn":
                    f = part[1]

                    def ffn_step(i, lo, hi):
                        silu(f, i, lo, hi)
                        split_next("g", f, i, lo, hi, 1)
                        split_next("u", f, i, lo, hi, 1)
                        if not isinstance(i, int) or i:
                            split_next("d", f, i, lo, hi, KD - 1, 1)
                    ffn_step(0, 0, 1)
                    with act.Fori(1, NF - 1) as i:
                        ffn_step(i, 1, NF - 1)
                    ffn_step(NF - 1, NF - 1, NF)
                if part[0] == "hyb":
                    A_ = nc.scalar.activation

                    def hgrn_gates(i, lo, hi, shift=0):
                        for e in range(2):
                            act.wait_ge(tile_read, affine(lambda x: TL.n[("hf", 0, x - shift, e)] + 1, i, lo, hi))
                            A_(t1[:, e, :], fz[:, e, :], ACT.Sigmoid).then_inc(sig_ready, 1)
                            if shift and e == 0:
                                act.wait_ge(lx_ready, affine(lambda x: 14 * x + 14, i, lo, hi))
                            A_(kk[:, e, :], fz[:, e, :], ACT.Sigmoid, scale=-1.0).then_inc(sig_ready, 1)

                    def hgrn_logs(i, lo, hi):
                        for e in range(2):
                            act.wait_ge(ln_asked, affine(lambda x: 2 * x + e + 1, i, lo, hi))
                            A_(t1[:, e, :], t1[:, e, :], ACT.Ln).then_inc(ln_ready, 1)
                            A_(fz[:, e, :], fz[:, e, :], ACT.Ln, scale=1.0 / LOG_SPLIT).then_inc(ln_ready, 1)

                    def hgrn_step(i, lo, hi, steps):
                        hgrn_logs(i, lo, hi)

                        def decays(j):
                            act.wait_ge(lev_ready, affine(lambda x: 14 * x + j + 1, i, lo, hi))
                            if j % 7 == 6:
                                if not (isinstance(i, int) and i == 0 and j == 6):
                                    act.wait_ge(tile_read, affine(lambda x: TL.n[("hL", 0, x if j > 6 else x - 1, 6 if j > 6 else 13)] + 1, i, lo, hi))
                                A_(lx2[:], lev[:, j % 2, :], ACT.Exp, scale=-1.0)
                            A_(lev[:, j % 2, :], lev[:, j % 2, :], ACT.Exp).then_inc(dec_ready, 1)

                        def chunk_decays(e):
                            act.wait_ge(b_ready, affine(lambda x: 2 * x + e + 1, i, lo, hi))
                            A_(khT[:], khT[:], ACT.Exp)
                            A_(qhat[:, e, :], bb[:, e, :], ACT.Exp).then_inc(eb_ready, 1)
                        decays(0)
                        decays(1)
                        chunk_decays(0)
                        decays(2)
                        decays(3)
                        split_next("hq", 0, i, lo, hi, 1)
                        for what, k in steps:
                            if what == "L":
                                if k + 4 < 14:
                                    decays(k + 4)
                                if k == 4:
                                    chunk_decays(1)
                                if k == 13 and ("hq", 0) in steps:
                                    hgrn_gates(i, lo, hi, -1)
                            if what == "hg" and k == 0:
                                split_next("hv", 0, i, lo, hi, 1)
                            if what == "hg" and k == 1:
                                split_next("hg", 0, i, lo, hi, 1)
                            if what == "hd" and k == KD - 1:
                                split_next("hd", 0, i, lo, hi, KD - 1, 1)
                            if what == "hf" and k == 1:
                                split_next("hf", 0, i, lo, hi, 1, -1)
                            if what == "O":
                                act.wait_ge(tile_done, affine(lambda x: TL.n[("hO", 0, x, k)] + 1, i, lo, hi))
                                for c in range(TC):
                                    r = slice(c * P, (c + 1) * P)
                                    ins = A_(osq[:, k, r], banks[k][:, r], ACT.Square, accum_out=osum[:, k * TC + c:k * TC + c + 1])
                                ins.then_inc(osq_ready, 1)
                                if k == 1:
                                    for e in range(2):
                                        A_(gg[:, e, :], gg[:, e, :], ACT.Silu).then_inc(gsilu_ready, 1)
                                    act.wait_ge(ovar_ready, affine(lambda x: x + 1, i, lo, hi))
                                    A_(ovar[:], ovar[:], ACT.Sqrt).then_inc(oroot_ready, 1)
                            if what == "N" and k == 1 and ("sx", 0) in steps:
                                split_next("sx", 0, 0, 0, 1, 1)

                    act.wait_ge(d_in, 48)
                    A_(dsh[:], dsr[:], ACT.Copy).then_inc(small_hi, 1)
                    A_(alog[:], alog[:], ACT.Exp).then_inc(lb_exp, 1)
                    hgrn_gates(0, 0, 1)
                    split_next("hf", 0, 0, 0, 1, 1)
                    hgrn_step(0, 0, 1, hgrn_steps(0))
                    with act.Fori(1, NQ - 1) as i:
                        hgrn_step(i, 1, NQ - 1, hgrn_steps(1))
                    hgrn_step(NQ - 1, NQ - 1, NQ, hgrn_steps(NQ - 1))
                    act.wait_ge(dt_asked, 1)
                    A_(dtt[:, 1, :], dtt[:, 1, :], ACT.Exp, scale=-1.0).then_inc(dt_exp, 1)
                    act.wait_ge(dec_asked, 1)
                    A_(tok3[:, 2], tok3[:, 2], ACT.Exp).then_inc(dec_exp, 1)
                    act.wait_ge(tile_read, TL.n[("csh",)] + 1)
                    act.dma_start(cs_dram, dcs).then_inc(cs_stored, 16)

                    def conv_act(ms, i, lo, hi, shift=0):
                        kind = "sb" if ms[0] == 2 else "sx"
                        if shift:
                            if kind == "sb":
                                act.wait_ge(mc_ready, affine(lambda x: 4 * x + 4, i, lo, hi))
                            else:
                                act.wait_ge(y_ready, affine(lambda x: 2 * x + 2, i, lo, hi))
                        act.wait_ge(cols_ready, affine(lambda x: x - shift + 1, i, lo, hi))
                        for m in ms:
                            act.wait_ge(tile_read, affine(lambda x: TL.n[(kind, 0, x - shift, m % 2)] + 1, i, lo, hi))
                            A_(xc[:, m, :], xpad[:, m, CONV - 1:], ACT.Identity, scale=wc[:, CONV - 1, m:m + 1],
                               bias=wc[:, CONV, m:m + 1]).then_inc(tap_ready, 1)
                        for m in ms:
                            act.wait_ge(conv_ready, affine(lambda x: 4 * (x - shift) + CONV_AT[m] + 1, i, lo, hi))
                            A_(xc[:, m, :], xc[:, m, :], ACT.Silu).then_inc(xc_ready, 1)
                    conv_act((2, 3), 0, 0, 1)
                    conv_act((0, 1), 0, 0, 1)
                    act.wait_ge(cs_stored, 16)
                    split_next("sb", 0, 0, 0, 1, 1)
                    split_next("hd", 0, NQ - 1, NQ - 1, NQ, KD - 1)

                    def ssd_step(i, lo, hi, steps):
                        act.dma_start(csg[:], cs_dram[bass.ts(i, G4), :]).then_inc(csg_in, 16)
                        for what, k in steps:
                            if what == "sz":
                                act.wait_ge(tile_read, affine(lambda x: TL.n[("sz", 0, x, k)] + 1, i, lo, hi))
                                A_(zs[:, k, :], zs[:, k, :], ACT.Silu).then_inc(zsilu_ready, 1)
                            if what == "sR":
                                act.wait_ge(tile_done, affine(lambda x: TL.n[("sR", 0, x, k)] + 1, i, lo, hi))
                                if k > 1:
                                    act.wait_ge(st_ready, affine(lambda x: 2 * x + 1, i, lo, hi))
                                A_(ecs[:, k % 2, :], banks[4 + k % 2][:], ACT.Exp).then_inc(ecs_ready, 1)
                                act.wait_ge(tile_read, affine(lambda x: TL.n[("sR", 0, x, k)] + 1, i, lo, hi))
                                A_(mm_[:, k % 2, :], mm_[:, k % 2, :], ACT.Exp).then_inc(dexp_ready, 1)
                            if what == "sR" and k == 2:
                                split_next("sz", 0, i, lo, hi, 1)
                            if what == "sY":
                                act.wait_ge(y_ready, affine(lambda x: 2 * x + k + 1, i, lo, hi))
                                if not (isinstance(i, int) and i == 0):
                                    act.wait_ge(ystat_done, affine(lambda x: 2 * x + k - 1, i, lo, hi))
                                A_(ysq[:, k, :], yy[:, bass.ds(2 * i + k, 1), :].rearrange("p a t -> p (a t)"),
                                   ACT.Square).then_inc(ysq_ready, 1)
                            if what == "sb" and k == 1:
                                conv_act((2, 3), i, lo, hi, -1)
                                split_next("sb", 0, i, lo, hi, 1, -1)
                            if what == "sx" and k == 1:
                                conv_act((0, 1), i, lo, hi, -1)
                                split_next("sx", 0, i, lo, hi, 1, -1)
                    ssd_step(0, 0, 1, ssd_steps(0))
                    with act.Fori(1, G4 - 1) as i:
                        ssd_step(i, 1, G4 - 1, ssd_steps(1))
                    ssd_step(G4 - 1, G4 - 1, G4, ssd_steps(G4 - 1))
                    act.wait_ge(yvar_ready, 1)
                    A_(var[:], var[:], ACT.Sqrt).then_inc(yroot_ready, 1)
                    for j in range(NQ - 1):
                        split_next("so", 0, j, j, j + 1, 1)
                if part[0] == "fox":
                    def fox_step(i, lo, hi):
                        for kind, last, shift in (("fq", 1, 0), ("fk", 1, 0), ("fd", KD - 1, 1)):
                            if kind == "fq" and not isinstance(i, int):
                                bias_rows(i)
                            if kind == "fd" and isinstance(i, int) and i == 0:
                                continue
                            split_next(kind, 0, i, lo, hi, last, shift)
                            if kind == "fk" and isinstance(i, int) and i == 0:
                                act.wait_ge(lse_ready, 1)
                                nc.scalar.activation(ftmp[:, 1, :], ftmp[:, 1, :], ACT.Exp, scale=-1.0).then_inc(exp_l_ready, 1)
                                act.wait_ge(tile_read, TL.n[("fcum",)] + 1)
                                act.dma_start(cum_dram[0], fcum[0]).then_inc(cum_stored, 16)
                                act.dma_start(cum_dram[1], fcum[1]).then_inc(cum_stored, 16)
                                act.wait_ge(cum_stored, 32)
                                act.wait_ge(fox_const, 1)
                                bias_rows(0)
                        for h in range(HPB):
                            for c in range(TC):
                                j = h * TC + c
                                act.wait_ge(negmax_ready, affine(lambda x: x * HPB * TC + j + 1, i, lo, hi))
                                if c == 0 and h >= 2:
                                    act.wait_ge(tile_done, affine(lambda x: TL.n[("fT", 0, x, h - 2, 2)] + 1, i, lo, hi))
                                w = (c + 1) * P
                                nc.scalar.activation(pr[h % 2][:, c, 0:w], banks[4 + c][:, 0:w], ACT.Exp,
                                                     bias=negmax[:, j:j + 1], accum_out=rowsum[:, j:j + 1]
                                                     ).then_inc(exp_done, 1)
                            if h == 1:
                                split_next("fv", 0, i, lo, hi, 1)

                    def bias_rows(i):
                        c0 = cum_dram[0][bass.ts(i, HPB), :].rearrange("(a b) t -> b a t", b=2)
                        c1 = cum_dram[1][bass.ts(i, HPB), :].rearrange("(a b) t -> b a t", b=2)
                        act.dma_start(qx[HD:HD + 1, 0:HPB:2, :], c0[0:1]).then_inc(aug_in, 16)
                        act.dma_start(qx[0:1, 1:HPB:2, :], c0[1:2]).then_inc(aug_in, 16)
                        act.dma_start(kx[HD + 1:HD + 2, 0:HPB:2, :], c1[0:1]).then_inc(aug_in, 16)
                        act.dma_start(kx[1:2, 1:HPB:2, :], c1[1:2]).then_inc(aug_in, 16)
                    act.wait_ge(small_in, 32)
                    nc.scalar.activation(fsh[:], fsr[:], ACT.Copy).then_inc(fsmall_hi, 1)
                    fox_step(0, 0, 1)
                    with act.Fori(1, NQ) as i:
                        fox_step(i, 1, NQ)
            squares(len(parts))
            act.wait_ge(var_ready, len(parts) + 1)
            nc.scalar.activation(rtok[:], vtok[:], ACT.Sqrt).then_inc(rms_ready, 1)

        @block.vector
        def _(dve):
            links = Links(dve_sem)
            v = nc.vector

            def split(s, n):
                dve.wait_ge(hi_done[s], n)
                v.tensor_tensor(wl[s][:], raw[s][:], wh[s][:].bitcast(F32), ALU.subtract).then_inc(lo_done[s], 1)

            def split_next(kind, f, i, lo, hi, shift=0):
                key = (kind, f, (i if isinstance(i, int) else lo) - shift)
                s = B.slot[key]
                if isinstance(i, int) and B.nth[key] + 1 == B.count[s]:
                    return
                split(s, affine(lambda x: B.nth[(kind, f, x - shift)] + 2, i, lo, hi))

            def tile(key, i, lo, hi):
                dve.wait_ge(tile_done, affine(lambda x: TL.n[key(x)] + 1, i, lo, hi))
                return banks[TL.bank[key(i if isinstance(i, int) else lo)]]

            def prepare(n, m):
                g = gain[:, gain_at[n], m:m + 1]
                if n == len(parts):
                    v.tensor_scalar(xg[:, m, :], xT[:, m, :], g, None, ALU.mult).then_inc(u_ready, 1)
                    return
                dve.wait_ge(uh_ready, n * KD + m + 1)
                v.scalar_tensor_tensor(out=ul[:, m, :], in0=xT[:, m, :], scalar=g, in1=uh[:, m, :].bitcast(F32),
                                       op0=ALU.mult, op1=ALU.subtract).then_inc(u_ready, 1)

            def sum_squares(n):
                dve.wait_ge(sq_ready, n * KD + KD)
                links.step(dve, TT(sq[:, 0:4, :], sq[:, 0:4, :], sq[:, 4:8, :], ALU.add))
                links.step(dve, TT(sq[:, 0:2, :], sq[:, 0:2, :], sq[:, 2:4, :], ALU.add))
                TT(sq[:, 0, :], sq[:, 0, :], sq[:, 1, :], ALU.add).then_inc(sum_ready, 1)

            def norm_scale(n):
                sum_squares(n)
                if n and parts[n - 1][0] == "ffn":
                    split_next("d", parts[n - 1][1], NF - 1, NF - 1, NF)
                if n and parts[n - 1][0] == "hyb":
                    split_next("so", 0, NQ - 1, NQ - 1, NQ)
                if n and parts[n - 1][0] == "fox":
                    split_next("fd", 0, NQ - 1, NQ - 1, NQ)
                dve.wait_ge(stat_done, n + 1)
                v.tensor_scalar(var[:], stat_bank[:], 1.0 / D, EPS, ALU.mult, ALU.add).then_inc(var_ready, 1)
                dve.wait_ge(rms_ready, n + 1)
                links.step(dve, v.reciprocal(rstd[:], rstd[:]))

            def residual(key, i, lo, hi, m, scale):
                b = tile(key, i, lo, hi)
                ins = v.scalar_tensor_tensor(out=xT[:, m, :], in0=b[:], scalar=scale, in1=xT[:, m, :],
                                             op0=ALU.mult, op1=ALU.add)
                ins.then_inc(tile_read, 1)
                return ins

            def log1p_exp(z, a, out, w, p, asked, answered, n):
                v.scalar_tensor_tensor(out=a, in0=z, scalar=-1.0, in1=z, op0=ALU.mult, op1=ALU.max).then_inc(asked, 1)
                dve.wait_ge(answered, n)
                links.step(dve, v.tensor_scalar(w, a, 2.0, None, ALU.add))
                links.step(dve, v.reciprocal(w, w))
                links.step(dve, v.tensor_tensor(a, a, w, ALU.mult))
                links.step(dve, v.tensor_tensor(w, a, a, ALU.mult))
                links.step(dve, v.tensor_scalar(p, w, 1.0 / 15, None, ALU.mult))
                for k in (13, 11, 9, 7, 5, 3):
                    links.step(dve, v.scalar_tensor_tensor(out=p, in0=p, scalar=1.0 / k, in1=w, op0=ALU.add, op1=ALU.mult))
                links.step(dve, v.scalar_tensor_tensor(out=p, in0=p, scalar=1.0, in1=a, op0=ALU.add, op1=ALU.mult))
                links.step(dve, v.tensor_scalar(out, p, 2.0, None, ALU.mult))

            TT, TS, STT = v.tensor_tensor, v.tensor_scalar, v.scalar_tensor_tensor

            def head_params():
                b = tile(lambda x: ("rows2",), 0, 0, 1)
                v.tensor_copy(cw[:, 0:CONV, :], b[:, 0:CONV * 16].rearrange("p (k c) -> p k c", k=CONV)).then_inc(tile_read, 1)
                b = tile(lambda x: ("rows3",), 0, 0, 1)
                v.tensor_copy(cw[:, CONV, :], b[:, 8:24])
                v.tensor_copy(lbt[:], b[:, 24:32])
                v.tensor_copy(hcols[:, 2, :], b[:, 32:40])
                v.tensor_copy(scols[:, 1, :], b[:, 40:48])
                v.tensor_copy(scols[:, 0, :], b[:, 0:8]).then_inc(tile_read, 1)
                dve.wait_ge(tile_read, TL.n[("rows3",)] + 1)
                TT(lbt[:], lbt[:], lbt[:], ALU.subtract).then_inc(lb_asked, 1)
                dve.wait_ge(lb_exp, 1)
                links.step(dve, v.reciprocal(hcols[:, 1, :], lbt[:]))
                links.step(dve, TT(lbt[:], lbt[:], hcols[:, 1, :], ALU.mult))
                links.step(dve, TT(hcols[:, 0, :], lbt[:], lbt[:], ALU.subtract))
                links.step(dve, TS(hcols[:, 1, :], hcols[:, 0, :], -1.0, 1.0, ALU.mult, ALU.add))

            for m in range(KD):
                b = tile(lambda x: ("in", m), 0, 0, 1)
                v.tensor_copy(xT[:, m, :], b[:]).then_inc(tile_read, 1)
            b = tile(lambda x: ("rows",), 0, 0, 1)
            v.tensor_copy(gain.rearrange("p n k -> p (n k)"), b[:, 0:NN * KD]).then_inc(tile_read, 1)
            split(B.slot[B.order[0]], 1)
            for m in range(KD):
                prepare(0, m)
            for key in B.order[1:SLOTS]:
                split(B.slot[key], 1)
            if ("hyb",) in parts:
                head_params()

            for n, part in enumerate(parts):
                norm_scale(n)
                if part[0] == "ffn":
                    f = part[1]
                    first = ffns.index(f) * NF

                    def ffn_hidden(i, lo, hi):
                        for m in range(2):
                            dve.wait_ge(silu_ready, affine(lambda x: 2 * (first + x) + m + 1, i, lo, hi))
                            links.step(dve, v.tensor_tensor(us[:, m, :], gs[:, m, :], us[:, m, :], ALU.mult))
                            h_, l_ = (hh_last, hl_last) if isinstance(i, int) and i == NF - 1 else (hh, hl)
                            links.step(dve, v.tensor_copy(h_[:, m, :], us[:, m, :]))
                            v.tensor_tensor(l_[:, m, :], us[:, m, :], h_[:, m, :].bitcast(F32),
                                            ALU.subtract).then_inc(h_ready, 1)

                    def ffn_step(i, lo, hi):
                        for m in range(2):
                            b = tile(lambda x: ("g", f, x, m), i, lo, hi)
                            v.tensor_tensor(gs[:, m, :], b[:], rstd[:], ALU.mult).then_inc(tile_read, 1)
                        split_next("g", f, i, lo, hi)
                        for m in range(2):
                            b = tile(lambda x: ("u", f, x, m), i, lo, hi)
                            v.tensor_tensor(us[:, m, :], b[:], rstd[:], ALU.mult).then_inc(tile_read, 1)
                            dve.wait_ge(tile_read, affine(lambda x: TL.n[("u", f, x, m)] + 1, i, lo, hi))
                        if isinstance(i, int):
                            ffn_hidden(i, lo, hi)
                        if not isinstance(i, int) or i:
                            for m in range(KD):
                                residual(lambda x: ("d", f, x - 1, m), i, lo, hi, m, 0.5)
                        if not isinstance(i, int):
                            ffn_hidden(i, lo, hi)
                        split_next("u", f, i, lo, hi)
                        if not isinstance(i, int) or i:
                            split_next("d", f, i, lo, hi, 1)
                    ffn_step(0, 0, 1)
                    with dve.Fori(1, NF - 1) as i:
                        links.enter(i, 1, FFN_LINKS)
                        ffn_step(i, 1, NF - 1)
                    links.leave(NF - 2)
                    ffn_step(NF - 1, NF - 1, NF)
                    for m in range(KD + 1):
                        if m < KD:
                            residual(lambda x: ("d", f, x, m), NF - 1, NF - 1, NF, m, 0.5)
                        if m:
                            dve.wait_ge(tile_read, TL.n[("d", f, NF - 1, m - 1)] + 1)
                            prepare(n + 1, m - 1)
                if part[0] == "hyb":
                    def scaled_in(kind, i, lo, hi, m, dst, shift=0):
                        b = tile(lambda x: (kind, 0, x - shift, m), i, lo, hi)
                        return TT(dst, b[:], rstd[:], ALU.mult).then_inc(tile_read, 1)

                    def tokens_in(i, lo, hi):
                        for m in range(2):
                            b = tile(lambda x: ("hv", 0, x, m), i, lo, hi)
                            TS(vv[:, 2 * m, :], b[:, 0:CB], hrt[:, 2 * m:2 * m + 1], None, ALU.mult).then_inc(qkv_ready, 1)
                            TS(vv[:, 2 * m + 1, :], b[:, CB:2 * CB], hrt[:, 2 * m + 1:2 * m + 2], None,
                               ALU.mult).then_inc(tile_read, 1)

                    def time_steps():
                        z, a, s_, w_, p_ = (dtt[:, n, :] for n in range(5))
                        by_head = lambda x: x.rearrange("p (c h) -> p c h", c=TC)
                        links.step(dve, TT(by_head(z), by_head(dlog[:]), dtb[:].unsqueeze(1).to_broadcast([P, TC, NH]), ALU.add))
                        log1p_exp(z, a, s_, w_, p_, dt_asked, dt_exp, 1)
                        dt_ = tok3[:, 1]
                        links.step(dve, STT(out=dt_, in0=by_head(z), scalar=0.0, in1=by_head(s_), op0=ALU.max, op1=ALU.add))
                        dve.wait_ge(lb_exp, 2)
                        STT(out=by_head(z), in0=dt_, scalar=-1.0, in1=alog[:].unsqueeze(1).to_broadcast([P, TC, NH]),
                            op0=ALU.mult, op1=ALU.mult).then_inc(a_ready, 1)

                    def gates(i, lo, hi, shift=0):
                        links.step(dve, v.tensor_copy(hc[:], hcols[:, :, bass.ts(i - shift if shift else i, 2)]))
                        for e in range(2):
                            dve.wait_ge(sig_ready, affine(lambda x: 4 * (x - shift) + 2 * e + 2, i, lo, hi))
                            TS(kk[:, e, :], kk[:, e, :], hc[:, 1, e:e + 1], None, ALU.mult)
                            links.step(dve, TS(t1[:, e, :], t1[:, e, :], hc[:, 1, e:e + 1], hc[:, 0, e:e + 1], ALU.mult, ALU.add))
                            links.step(dve, TS(fz[:, e, :], t1[:, e, :], LOG_SPLIT, TINY, ALU.min, ALU.max))
                            TS(t1[:, e, :], t1[:, e, :], LOG_SPLIT, None, ALU.max).then_inc(ln_asked, 1)

                    def log_decay(i, lo, hi, e):
                        dve.wait_ge(ln_ready, affine(lambda x: 4 * x + 2 * e + 2, i, lo, hi))
                        for c in range(TC):
                            r = slice(c * P, (c + 1) * P)
                            ins = v.tensor_tensor_scan(bb[:, e, r], t1[:, e, r], fz[:, e, r], 0.0, ALU.add, ALU.add)
                        links.step(dve, ins)

                    def hgrn_step(i, lo, hi, steps):
                        v.tensor_copy(hgain[:], hcols[:, 2, bass.ts(i, 2)])

                        def chunk_diff(e):
                            b4 = bb[:, e, :].rearrange("p (c t) -> p c t", c=TC)
                            TT(khT.rearrange("p (c t) -> p c t", c=TC), b4[:, :, P - 1:P].to_broadcast([P, TC, P]), b4,
                               ALU.subtract).then_inc(b_ready, 1)

                        def chunk_scaled(e):
                            dve.wait_ge(eb_ready, affine(lambda x: 2 * x + e + 1, i, lo, hi))
                            links.step(dve, v.tensor_copy(etot[:, e, :], qhat[:, e, :].rearrange("p (c t) -> p c t", c=TC)[:, :, P - 1:P].rearrange("p c t -> p (c t)")))
                            TT(khT[:], khT[:], kk[:, e, :], ALU.mult)
                            TT(qhat[:, e, :], qhat[:, e, :], qq[:, e, :], ALU.mult).then_inc(qk_ready, 1)

                        def diff(j):
                            e, l = divmod(j, 7)
                            m = 64 >> l
                            if j > 1:
                                dve.wait_ge(lx_ready, affine(lambda x: 14 * x + j - 1, i, lo, hi))
                            src = bb[:, e, :].rearrange("p (n h j) -> p n h j", h=2, j=m)
                            dst = lev[:, j % 2, :].rearrange("p (n h j) -> p n h j", h=2, j=m)
                            nb = T // (2 * m)
                            if l < 6:
                                ref = src[:, :, 0, m - 1:m].to_broadcast([P, nb, m])
                                TT(dst[:, :, 0, :], ref, src[:, :, 0, :], ALU.subtract)
                                TT(dst[:, :, 1, :], src[:, :, 1, :], ref, ALU.subtract).then_inc(lev_ready, 1)
                            else:
                                s2 = bb[:, e, :].rearrange("p (n j) -> p n j", j=2)
                                TT(lev[:, j % 2, :].rearrange("p (n j) -> p n j", j=2), s2,
                                   s2[:, :, 0:1].to_broadcast([P, T // 2, 2]), ALU.subtract).then_inc(lev_ready, 1)

                        def mult(j):
                            e, l = divmod(j, 7)
                            m = 64 >> l
                            dve.wait_ge(dec_ready, affine(lambda x: 14 * x + j + 1, i, lo, hi))
                            dst = lx[:, j % 2, :]
                            if l < 6:
                                view = lambda x: x.rearrange("p (n h j) -> p n h j", h=2, j=m)
                                TT(view(dst)[:, :, 0, :], view(lev[:, j % 2, :])[:, :, 0, :], view(kk[:, e, :])[:, :, 0, :], ALU.mult)
                                TT(view(dst)[:, :, 1, :], view(lev[:, j % 2, :])[:, :, 1, :], view(qq[:, e, :])[:, :, 1, :],
                                   ALU.mult).then_inc(lx_ready, 1)
                            else:
                                TT(lx2[:], lx2[:], kk[:, e, :], ALU.mult)
                                TT(dst, lev[:, j % 2, :], qq[:, e, :], ALU.mult).then_inc(lx_ready, 1)

                        log_decay(i, lo, hi, 0)
                        diff(0)
                        diff(1)
                        chunk_diff(0)
                        log_decay(i, lo, hi, 1)
                        mult(0)
                        mult(1)
                        diff(2)
                        diff(3)
                        chunk_scaled(0)
                        tokens_in(i, lo, hi)
                        split_next("hq", 0, i, lo, hi)
                        for what, k in steps:
                            if what == "L":
                                if k == 4:
                                    dve.wait_ge(tile_read, affine(lambda x: TL.n[("hK", 0, x, 0)] + 1, i, lo, hi))
                                    chunk_diff(1)
                                if k == 5:
                                    chunk_scaled(1)
                                b = tile(lambda x: ("hL", 0, x, k), i, lo, hi)
                                if k % 7:
                                    dve.wait_ge(tile_read, affine(lambda x: TL.n[("hL", 0, x, k - 1)] + 1, i, lo, hi))
                                v.memset(waited[:, k:k + 1], 0.0)
                                v.copy_predicated(sc[:, k // 7], lmask[:, k % 7:k % 7 + 1, :].to_broadcast([P, TC, P]),
                                                  b.rearrange("p (c t) -> p c t", c=TC)).then_inc(tile_read, 1)
                                if k + 2 < 14:
                                    mult(k + 2)
                                if k + 4 < 14:
                                    diff(k + 4)
                            if what == "K":
                                b = tile(lambda x: ("hK", 0, x, k), i, lo, hi)
                                v.tensor_copy(kh.rearrange("p c d -> p (c d)"), b[:]).then_inc(tile_read, 1)
                            if what == "U":
                                b = tile(lambda x: ("hU", 0, x, k), i, lo, hi)
                                links.step(dve, v.tensor_copy(st[:, k, 0, :], b[:, 0:P]))
                                links.step(dve, STT(out=st[:, k, 1, :], in0=st[:, k, 0, :], scalar=etot[:, k, 1:2],
                                                    in1=b[:, P:2 * P], op0=ALU.mult, op1=ALU.add))
                                STT(out=st[:, k, 2, :], in0=st[:, k, 1, :], scalar=etot[:, k, 2:3],
                                    in1=b[:, 2 * P:3 * P], op0=ALU.mult, op1=ALU.add).then_inc(tile_read, 1)
                            if what == "O":
                                b = tile(lambda x: ("hO", 0, x, k), i, lo, hi)
                                dve.wait_ge(osq_ready, affine(lambda x: 2 * x + k + 1, i, lo, hi))
                                v.tensor_copy(osb[:, k, :], b[:]).then_inc(tile_read, 1)
                                if k == 1:
                                    TS(ovar[:], osum[:], 1.0 / P, EPS, ALU.mult, ALU.add).then_inc(ovar_ready, 1)
                                    if ("hq", 0) in steps:
                                        gates(i, lo, hi, -1)
                                    dve.wait_ge(oroot_ready, affine(lambda x: x + 1, i, lo, hi))
                                    links.step(dve, v.reciprocal(ovar[:], ovar[:]))
                                    for e in range(2):
                                        o3 = osb[:, e, :].rearrange("p (c d) -> p c d", c=TC)
                                        TT(o3, o3, ovar[:, e * TC:(e + 1) * TC].unsqueeze(2).to_broadcast([P, TC, P]),
                                           ALU.mult).then_inc(on_ready, 1)
                            if what == "hq":
                                if k == 0:
                                    split_next("hf", 0, i, lo, hi, -1)
                                scaled_in("hq", i, lo, hi, k, qq[:, k, :], -1)
                            if what == "sx":
                                scaled_in("sx", 0, 0, 1, k, xpad[:, k, CONV - 1:])
                            if what == "N":
                                b = tile(lambda x: ("hN", 0, x, k), i, lo, hi)
                                dve.wait_ge(gsilu_ready, affine(lambda x: 2 * x + k + 1, i, lo, hi))
                                STT(out=gg[:, k, :], in0=gg[:, k, :], scalar=hgain[:, k:k + 1], in1=b[:],
                                    op0=ALU.mult, op1=ALU.mult).then_inc(tile_read, 1)
                                dve.wait_ge(tile_read, affine(lambda x: TL.n[("hN", 0, x, k)] + 1, i, lo, hi))
                                links.step(dve, v.tensor_copy(hh[:, k, :], gg[:, k, :]))
                                TT(hl[:, k, :], gg[:, k, :], hh[:, k, :].bitcast(F32), ALU.subtract).then_inc(hd_ready, 1)
                            if what == "hg":
                                scaled_in("hg", i, lo, hi, k, gg[:, k, :])
                                if k == 0:
                                    split_next("hv", 0, i, lo, hi)
                                if k == 1:
                                    split_next("hg", 0, i, lo, hi)
                            if what == "hd":
                                residual(lambda x: ("hd", 0, x - 1, k), i, lo, hi, k, 1.0)
                                if k == KD - 1:
                                    split_next("hd", 0, i, lo, hi, 1)
                            if what == "hf":
                                scaled_in("hf", i, lo, hi, k, fz[:, k, :], -1)

                    dve.wait_ge(small_hi, 1)
                    TT(dsl[:], dsr[:], dsh[:].bitcast(F32), ALU.subtract).then_inc(small_lo, 1)
                    for e in range(2):
                        scaled_in("hf", 0, 0, 1, e, fz[:, e, :])
                    split_next("hf", 0, 0, 0, 1)
                    dve.wait_ge(hyb_const, 1)
                    gates(0, 0, 1)
                    for e in range(2):
                        scaled_in("hq", 0, 0, 1, e, qq[:, e, :])
                    b = tile(lambda x: ("dlog",), 0, 0, 1)
                    TT(logits_h, b[0:NH, :], rstd[0:NH, :], ALU.mult).then_inc(tile_read, 1)
                    b = tile(lambda x: ("dlogT",), 0, 0, 1)
                    v.tensor_copy(dlog[:], b[:, 0:TC * NH]).then_inc(tile_read, 1)
                    b = tile(lambda x: ("hrt",), 0, 0, 1)
                    v.tensor_copy(hrt[:], b[:, 0:TC]).then_inc(tile_read, 1)
                    hgrn_step(0, 0, 1, hgrn_steps(0))
                    with dve.Fori(1, NQ - 1) as i:
                        links.enter(i, 1, HG_LINKS)
                        hgrn_step(i, 1, NQ - 1, hgrn_steps(1))
                    links.leave(NQ - 2)
                    hgrn_step(NQ - 1, NQ - 1, NQ, hgrn_steps(NQ - 1))

                    def conv_columns(g):
                        v.tensor_copy(wc[:, :, 0:2], cw[:, :, bass.ts(g, 2)])
                        v.tensor_copy(wc[:, :, 2:3], cw[:, :, bass.ds(g + 8, 1)])
                        v.tensor_copy(wc[:, :, 3:4], cw[:, :, bass.ds(g + 12, 1)]).then_inc(cols_ready, 1)

                    def conv(ms, i, lo, hi, shift=0):
                        for t in range(CONV - 1):
                            for m in ms:
                                dve.wait_ge(tap_ready, affine(lambda x: 4 * (x - shift) + CONV_AT[m] + 1, i, lo, hi))
                                ins = STT(out=xc[:, m, :], in0=xpad[:, m, t:t + T], scalar=wc[:, t, m:m + 1],
                                          in1=xc[:, m, :], op0=ALU.mult, op1=ALU.add)
                                if t < CONV - 2:
                                    links.step(dve, ins)
                                else:
                                    ins.then_inc(conv_ready, 1)

                    time_steps()
                    conv_columns(0)
                    links.step(dve, v.memset(xpad[:, :, 0:CONV - 1], 0.0))
                    split_next("sx", 0, 0, 0, 1)
                    for m in range(2):
                        scaled_in("sb", 0, 0, 1, m, xpad[:, 2 + m, CONV - 1:])
                    b = tile(lambda x: ("cst",), 0, 0, 1)
                    v.tensor_copy(tok3[:, 2].rearrange("p c h -> p (c h)"), b[:, TC * NH:2 * TC * NH]).then_inc(dec_asked, 1)
                    v.tensor_copy(tok3[:, 0].rearrange("p c h -> p (c h)"), b[:, 0:TC * NH]).then_inc(tile_read, 1)
                    b = tile(lambda x: ("csh",), 0, 0, 1)
                    v.tensor_copy(dcs, b[0:NH, :]).then_inc(tile_read, 1)
                    v.memset(yy[:, KD - 1, :], 0.0).then_inc(yy_zero, 1)
                    for m in range(KD):
                        if m % 4 == 0:
                            conv((2, 3) if m == 0 else (0, 1), 0, 0, 1)
                        residual(lambda x: ("hd", 0, x, m), NQ - 1, NQ - 1, NQ, m, 1.0)
                    split_next("sb", 0, 0, 0, 1)
                    split_next("hd", 0, NQ - 1, NQ - 1, NQ)
                    dve.wait_ge(tile_read, TL.n[("hd", 0, NQ - 1, KD - 1)] + 1)
                    dve.wait_ge(dec_exp, 1)

                    def ssd_step(i, lo, hi, steps):
                        v.tensor_copy(tokg.rearrange("p a c h -> p (a c) h"),
                                      tok3[:, :, :, bass.ts(i, G4)].rearrange("p a c h -> p (a c) h"))
                        links.step(dve, v.tensor_copy(hc[:, 0, :], scols[:, 0, bass.ts(i, 2)]))
                        for what, k in steps:
                            if what == "sz":
                                scaled_in("sz", i, lo, hi, k, zs[:, k, :])
                            if what == "sX":
                                b = tile(lambda x: ("sX", 0, x, k), i, lo, hi)
                                r = slice(2 * k * G4, (2 * k + 2) * G4)
                                col = lambda a: tokg[:, a, 2 * k:2 * k + 2, :].rearrange("p c h -> p (c h)").unsqueeze(2).to_broadcast([P, 2 * G4, SP_])
                                hv = lambda x: x.rearrange("p (h d) -> p h d", d=SP_)
                                TT(hv(xdt[:, k, :]), hv(b[:]), col(1), ALU.mult).then_inc(tile_read, 1)
                                dve.wait_ge(tile_read, affine(lambda x: TL.n[("sX", 0, x, k)] + 1, i, lo, hi))
                                TT(hv(xdd[:, k, :]), hv(xdt[:, k, :]), col(2), ALU.mult).then_inc(xdd_ready, 1)
                            if what == "sB":
                                b = tile(lambda x: ("sB", 0, x, k), i, lo, hi)
                                v.tensor_copy(bt.rearrange("p c n -> p (c n)"), b[:]).then_inc(tile_read, 1)
                            if what == "sC":
                                b = tile(lambda x: ("sC", 0, x, k), i, lo, hi)
                                TT(cbm[:], b.rearrange("p (c l) -> p c l", c=TC), causal[:].unsqueeze(1).to_broadcast([P, TC, P]),
                                   ALU.mult).then_inc(tile_read, 1)
                                dve.wait_ge(tile_read, affine(lambda x: TL.n[("sC", 0, x, k)] + 1, i, lo, hi))
                            if what == "sR":
                                e = k % 2
                                b = tile(lambda x: ("sR", 0, x, k), i, lo, hi)
                                dve.wait_ge(ecs_ready, affine(lambda x: 4 * x + k + 1, i, lo, hi))
                                if k > 1:
                                    dve.wait_ge(tile_done, affine(lambda x: TL.n[("sY", 0, x, 0)] + 1, i, lo, hi))
                                for c in range(TC):
                                    r = slice(c * P, (c + 1) * P)
                                    ins = TS(mm_[:, e, r], b[:, r], tokg[:, 0, c, k:k + 1], 0.0, ALU.subtract, ALU.min)
                                ins.then_inc(tile_read, 1)
                                TT(cx[:, e, :], ecs[:, e, :], xc[:, 3, :], ALU.mult)
                                dve.wait_ge(dexp_ready, affine(lambda x: 4 * x + k + 1, i, lo, hi))
                                TT(mm_[:, e, :], mm_[:, e, :], cbm.rearrange("p c l -> p (c l)"), ALU.mult).then_inc(mc_ready, 1)
                            if what == "sU":
                                b = tile(lambda x: ("sU", 0, x, k), i, lo, hi)
                                if k == 0:
                                    v.tensor_copy(ub[:, 0:2, :].rearrange("p c f -> p (c f)"), b[:]).then_inc(tile_read, 1)
                                else:
                                    v.tensor_copy(ub[:, 2, :], b[:, 0:CB]).then_inc(tile_read, 1)
                            if what == "sY":
                                b = tile(lambda x: ("sY", 0, x, k), i, lo, hi)
                                y = yy[:, bass.ds(2 * i + k, 1), :].rearrange("p a t -> p (a t)")
                                STT(out=xc[:, k, :], in0=xc[:, k, :], scalar=hc[:, 0, k:k + 1], in1=b[:],
                                    op0=ALU.mult, op1=ALU.add).then_inc(tile_read, 1)
                                dve.wait_ge(tile_read, affine(lambda x: TL.n[("sY", 0, x, k)] + 1, i, lo, hi))
                                dve.wait_ge(zsilu_ready, affine(lambda x: 2 * x + k + 1, i, lo, hi))
                                TT(y, xc[:, k, :], zs[:, k, :], ALU.mult).then_inc(y_ready, 1)
                            if what in ("sR", "sU") and (what, k) in (("sU", 1), ("sR", 3)):
                                dve.wait_ge(tile_read, affine(lambda x: TL.n[(what, 0, x, k)] + 1, i, lo, hi))
                                h0 = 0 if what == "sU" else 2
                                for c in (1, 2):
                                    for h in (h0, h0 + 1):
                                        f = slice(h * SP_, (h + 1) * SP_)
                                        ins = STT(out=ub[:, c, f], in0=ub[:, c - 1, f], scalar=ecs[:, h % 2, c * P + P - 1:c * P + P],
                                                  in1=ub[:, c, f], op0=ALU.mult, op1=ALU.add)
                                        if c == 1:
                                            links.step(dve, ins)
                                ins.then_inc(st_ready, 1)
                            if (what, k) == ("sR", 3):
                                split_next("sz", 0, i, lo, hi)
                            if what == "sb":
                                if k == 1:
                                    conv_columns(i + 1)
                                scaled_in("sb", i, lo, hi, k, xpad[:, 2 + k, CONV - 1:], -1)
                                if k == 1:
                                    conv((2, 3), i, lo, hi, -1)
                            if what == "sx":
                                scaled_in("sx", i, lo, hi, k, xpad[:, k, CONV - 1:], -1)
                                if k == 1:
                                    conv((0, 1), i, lo, hi, -1)
                                    split_next("sb", 0, i, lo, hi, -1)
                                    split_next("sx", 0, i, lo, hi, -1)

                    ssd_step(0, 0, 1, ssd_steps(0))
                    with dve.Fori(1, G4 - 1) as i:
                        links.enter(i, 1, SSD_LINKS)
                        ssd_step(i, 1, G4 - 1, ssd_steps(1))
                    links.leave(G4 - 2)
                    ssd_step(G4 - 1, G4 - 1, G4, ssd_steps(G4 - 1))
                    dve.wait_ge(y_ready, 2 * G4)
                    for m in range(KD):
                        g_ = scols[:, 1, m:m + 1]
                        links.step(dve, TS(uh[:, m, :], yy[:, m, :], g_, None, ALU.mult))
                        STT(out=ul[:, m, :], in0=yy[:, m, :], scalar=g_, in1=uh[:, m, :].bitcast(F32), op0=ALU.mult,
                            op1=ALU.subtract).then_inc(yu_ready, 1)
                    dve.wait_ge(ystat_done, 2 * G4)
                    TS(var[:], banks[7][:], 1.0 / D, EPS, ALU.mult, ALU.add).then_inc(yvar_ready, 1)
                    dve.wait_ge(yroot_ready, 1)
                    links.step(dve, v.reciprocal(var[:], var[:]))
                    for j in range(NQ):
                        for m in range(2):
                            f = 2 * j + m
                            b = tile(lambda x: ("so", 0, j, m), 0, 0, 1)
                            links.step(dve, TT(ecs[:, 0, :], b[:], var[:], ALU.mult))
                            TT(xT[:, f, :], xT[:, f, :], ecs[:, 0, :], ALU.add).then_inc(tile_read, 1)
                            dve.wait_ge(tile_read, TL.n[("so", 0, j, m)] + 1)
                        if j < NQ - 1:
                            split_next("so", 0, j, j, j + 1)
                    for m in range(KD):
                        prepare(n + 1, m)
                if part[0] == "fox":
                    def heads_in(kind, dst, scale, i, lo, hi, only=None):
                        for m in range(2) if only is None else [only]:
                            b = tile(lambda x: (kind, 0, x, m), i, lo, hi)
                            for e in range(2):
                                r = slice(e * HD, (e + 1) * HD)
                                ins = v.scalar_tensor_tensor(out=dst[r, 2 * m + e, :], in0=b[r, :], scalar=scale,
                                                             in1=rstd[r, :], op0=ALU.mult, op1=ALU.mult)
                                if e == 0:
                                    ins.then_inc(qkv_ready, 1)
                            ins.then_inc(tile_read, 1)

                    def fox_step(i, lo, hi):
                        peeled = isinstance(i, int)
                        heads_in("fq", qx, HD ** -0.5, i, lo, hi)
                        split_next("fq", 0, i, lo, hi)
                        if not peeled or i:
                            outputs(i, lo, hi)
                        heads_in("fk", kx, 1.0, i, lo, hi, 0)
                        if peeled:
                            b = tile(lambda x: ("flog",), 0, 0, 1)
                            TT(logits_h, b[0:NH, :], rstd[0:NH, :], ALU.mult).then_inc(tile_read, 1)
                        heads_in("fk", kx, 1.0, i, lo, hi, 1)
                        if peeled:
                            b = tile(lambda x: ("flogT",), 0, 0, 1)
                            v.tensor_copy(flog[:], b[:, 0:TC * NH]).then_inc(tile_read, 1)
                            forget_gates()
                        split_next("fk", 0, i, lo, hi)
                        if not peeled or i:
                            for m in range(KD):
                                residual(lambda x: ("fd", 0, x - 1, m), i, lo, hi, m, 1.0)
                            split_next("fd", 0, i, lo, hi, 1)
                        for m in range(2):
                            b = tile(lambda x: ("fv", 0, x, m), i, lo, hi)
                            v.tensor_scalar(vt[:, 2 * m, :], b[:, 0:CB], rt[:, 2 * m:2 * m + 1], None,
                                            ALU.mult).then_inc(qkv_ready, 1)
                            v.tensor_scalar(vt[:, 2 * m + 1, :], b[:, CB:2 * CB], rt[:, 2 * m + 1:2 * m + 2], None,
                                            ALU.mult).then_inc(tile_read, 1)
                            if peeled and m == 0:
                                b = tile(lambda x: ("fcum",), 0, 0, 1)
                                v.tensor_copy(fcum[0], b[0:NH, :]).then_inc(cum_ready, 1)
                                TS(fcum[1], b[0:NH, :], -1.0, None, ALU.mult).then_inc(tile_read, 1)
                        for what, h in FOX_STEPS:
                            if what == "S":
                                for c in range(TC):
                                    j = h * TC + c
                                    dve.wait_ge(s_done, affine(lambda x: x * HPB * TC + j + 1, i, lo, hi))
                                    v.tensor_reduce(negmax[:, j:j + 1], banks[4 + c][:, 0:(c + 1) * P], AX.X, ALU.max,
                                                    negate=True).then_inc(negmax_ready, 1)
                            if what == "T":
                                for m in range(3):
                                    b = tile(lambda x: ("fT", 0, x, h, m), i, lo, hi)
                                    w = T if m < 2 else T // 2
                                    v.tensor_copy(pt[h % 2][:, m, 0:w], b[:, 0:w]).then_inc(tile_read, 1)
                                if h == 1:
                                    split_next("fv", 0, i, lo, hi)
                            if what == "V":
                                dve.wait_ge(exp_done, affine(lambda x: x * HPB * TC + (h + 1) * TC, i, lo, hi))
                                r = slice(h * TC, (h + 1) * TC)
                                links.step(dve, v.reciprocal(rrow[:, r], rowsum[:, r]))
                                b = tile(lambda x: ("fV", 0, x, h), i, lo, hi)
                                v.tensor_tensor(ot[:, :, h * HD:(h + 1) * HD],
                                                b[:, 0:TC * HD].rearrange("p (c d) -> p c d", c=TC),
                                                rrow[:, r].unsqueeze(2).to_broadcast([P, TC, HD]),
                                                ALU.mult).then_inc(tile_read, 1)

                    def outputs(i, lo, hi):
                        for m in range(2):
                            b = tile(lambda x: ("fo", 0, x - 1, m), i, lo, hi)
                            links.step(dve, v.tensor_copy(hh[:, m, :], b[:]))
                            v.tensor_tensor(hl[:, m, :], b[:], hh[:, m, :].bitcast(F32),
                                            ALU.subtract).then_inc(tile_read, 1)

                    def forget_gates():
                        b = tile(lambda x: ("frt",), 0, 0, 1)
                        v.tensor_copy(rt[:], b[:, 0:TC]).then_inc(tile_read, 1)
                        dve.wait_ge(tile_read, TL.n[("frt",)] + 1)
                        z, a, s_, w_, p_ = (ftmp[:, n, :] for n in range(5))
                        by_head = lambda x: x.rearrange("p (c h) -> p c h", c=TC)
                        dve.wait_ge(small_in, 32)
                        links.step(dve, TT(by_head(z), by_head(flog[:]), bfrow[:].unsqueeze(1).to_broadcast([P, TC, NH]), ALU.add))
                        log1p_exp(z, a, s_, w_, p_, lse_ready, exp_l_ready, 1)
                        STT(out=z, in0=z, scalar=0.0, in1=s_, op0=ALU.min, op1=ALU.subtract).then_inc(flog_ready, 1)

                    dve.wait_ge(fsmall_hi, 1)
                    v.tensor_tensor(fsl[:], fsr[:], fsh[:].bitcast(F32), ALU.subtract).then_inc(small_lo, 1)
                    dve.wait_ge(fox_const, 1)
                    fox_step(0, 0, 1)
                    with dve.Fori(1, NQ) as i:
                        links.enter(i, 1, FOX_LINKS)
                        fox_step(i, 1, NQ)
                    links.leave(NQ - 1)
                    outputs(NQ, NQ, NQ + 1)
                    for m in range(KD + 1):
                        if m < KD:
                            residual(lambda x: ("fd", 0, x, m), NQ - 1, NQ - 1, NQ, m, 1.0)
                        if m:
                            dve.wait_ge(tile_read, TL.n[("fd", 0, NQ - 1, m - 1)] + 1)
                            prepare(n + 1, m - 1)
            sum_squares(len(parts))
            dve.wait_ge(stat_done, len(parts) + 1)
            v.tensor_scalar(vtok[:], stat_bank[:, 0:TC], 1.0 / D, EPS, ALU.mult, ALU.add).then_inc(var_ready, 1)
            dve.wait_ge(rms_ready, len(parts) + 1)
            links.step(dve, v.reciprocal(rtok[:], rtok[:]))
            for c in range(TC):
                for h in range(2):
                    b = tile(lambda x: ("out", 2 * c + h), 0, 0, 1)
                    v.tensor_scalar(sq[:, 2 * c + h, :], b[:], rtok[:, c:c + 1], None, ALU.mult).then_inc(tile_read, 1)

        @block.tensor
        def _(pe):
            def free(key, i, lo, hi):
                k = key(i if isinstance(i, int) else lo)
                if TL.prev[k] >= 0:
                    pe.wait_ge(tile_read, at_least(lambda x: TL.prev[key(x)] + 1, lambda x: TL.n[key(x)], i, lo, hi))
                return banks[TL.bank[k]]

            def block_in(kind, f, i, lo, hi, shift=0):
                s = B.slot[(kind, f, (i if isinstance(i, int) else lo) - shift)]
                pe.wait_ge(lo_done[s], affine(lambda x: B.nth[(kind, f, x - shift)] + 1, i, lo, hi))
                return s

            def product(dst, lh, ll, rh, rl, first, last):
                nc.tensor.matmul(dst, lh, rh, start=first, stop=False)
                nc.tensor.matmul(dst, lh, rl, start=False, stop=False)
                return nc.tensor.matmul(dst, ll, rh, start=False, stop=last)

            def columns(kind, f, i, lo, hi, m, n=None, shift=0):
                s = B.slot[(kind, f, (i if isinstance(i, int) else lo) - shift)]
                b = free(lambda x: (kind, f, x - shift, m), i, lo, hi)
                for k in range(KD):
                    if n is not None:
                        pe.wait_ge(u_ready, n * KD + k + 1)
                    c = slice(k * CB + m * P, k * CB + (m + 1) * P)
                    mm = product(b[:], wh[s][:, c], wl[s][:, c], uh[:, k, :], ul[:, k, :], k == 0, k == KD - 1)
                mm.then_inc(tile_done, 1)

            def stat(n):
                pe.wait_ge(sum_ready, n + 1)
                nc.tensor.matmul(stat_bank[:], ones[:], sq[:, 0, :], start=True, stop=True).then_inc(stat_done, 1)

            def down(f, i, lo, hi, shift=0, kind="d", only=None):
                s = B.slot[(kind, f, (i if isinstance(i, int) else lo) - shift)]
                if only in (None, 0):
                    block_in(kind, f, i, lo, hi, shift)
                if kind == "d":
                    pe.wait_ge(h_ready, affine(lambda x: 2 * (ffns.index(f) * NF + x - shift) + 2, i, lo, hi))
                if kind == "hd":
                    pe.wait_ge(hd_ready, affine(lambda x: 2 * (x - shift) + 2, i, lo, hi))
                if kind == "fd":
                    pe.wait_ge(tile_read, affine(lambda x: TL.n[("fo", 0, x - shift, 1)] + 1, i, lo, hi))
                h_, l_ = (hh_last, hl_last) if kind == "d" and not shift else (hh, hl)
                for m in range(KD) if only is None else [only]:
                    b = free(lambda x: (kind, f, x - shift, m), i, lo, hi)
                    for k in range(2):
                        c = slice(k * D + m * P, k * D + (m + 1) * P)
                        mm = product(b[:], wh[s][:, c], wl[s][:, c], h_[:, k, :], l_[:, k, :], k == 0, k == 1)
                    mm.then_inc(tile_done, 1)

            def tokens(kind, i, lo, hi, only=None):
                s = block_in(kind, 0, i, lo, hi)
                for m in range(2) if only is None else [only]:
                    b = free(lambda x: (kind, 0, x, m), i, lo, hi)
                    for c in range(2):
                        r = slice((2 * m + c) * P, (2 * m + c + 1) * P)
                        for k in range(KD):
                            w = slice(k * CB, (k + 1) * CB)
                            mm = product(b[:, c * CB:(c + 1) * CB], uh[:, k, r], ul[:, k, r],
                                         wh[s][:, w], wl[s][:, w], k == 0, k == KD - 1)
                    mm.then_inc(tile_done, 1)

            def small_logits(key, hi_, lo_):
                pe.wait_ge(small_lo, 1 + (key == "flog" and ("hyb",) in parts))
                b = free(lambda x: (key,), 0, 0, 1)
                for k in range(KD):
                    w = slice(k * NH, (k + 1) * NH)
                    mm = product(b[0:NH, :], hi_[:, w], lo_[:, w], uh[:, k, :], ul[:, k, :], k == 0, k == KD - 1)
                mm.then_inc(tile_done, 1)

            def rms_by_token(key):
                b = free(lambda x: (key,), 0, 0, 1)
                for c in range(TC):
                    mm = nc.tensor.matmul(b[:, c:c + 1], rstd[0:1, c * P:(c + 1) * P], ones[0:1, 0:1], start=True, stop=True)
                mm.then_inc(tile_done, 1)

            def tokens_first(key, scaled):
                pe.wait_ge(tile_read, TL.n[(scaled,)] + 1)
                b = free(lambda x: (key,), 0, 0, 1)
                for c in range(TC):
                    mm = nc.tensor.transpose(b[:, c * NH:(c + 1) * NH], logits_h[:, c * P:(c + 1) * P], ident[0:NH, 0:NH])
                mm.then_inc(tile_done, 1)

            pe.wait_ge(const_ready, 2)
            for m in range(KD):
                pe.wait_ge(x_in[m // (KD // 2)], 16)
                b = free(lambda x: ("in", m), 0, 0, 1)
                for c in range(TC):
                    xt = sq[:, 2 * c + m // 4, (m % 4) * P:(m % 4 + 1) * P]
                    mm = nc.tensor.transpose(b[:, c * P:(c + 1) * P], xt, ident[:])
                mm.then_inc(tile_done, 1)
            pe.wait_ge(gains_in, 16 * len(gains))
            nc.tensor.transpose(banks[0][:, 0:NN * KD], rows[:], ident[0:NN * KD, 0:NN * KD]).then_inc(tile_done, 1)
            if ("hyb",) in parts:
                pe.wait_ge(params_in, 80)
                pe.wait_ge(d_spread, 1)
                nc.tensor.transpose(banks[1][:, 0:CONV * 16], rows2[:], ident[0:CONV * 16, 0:CONV * 16]).then_inc(tile_done, 1)
                nc.tensor.transpose(banks[2][:, 0:48], rows3[:], ident[0:48, 0:48]).then_inc(tile_done, 1)
            for n, part in enumerate(parts):
                if part[0] == "ffn":
                    f = part[1]
                    block_in("g", f, 0, 0, 1)
                    columns("g", f, 0, 0, 1, 0, n)
                    columns("g", f, 0, 0, 1, 1)
                    stat(n)
                    block_in("u", f, 0, 0, 1)
                    columns("u", f, 0, 0, 1, 0)
                    columns("u", f, 0, 0, 1, 1)
                    with pe.Fori(1, NF) as i:
                        block_in("g", f, i, 1, NF)
                        columns("g", f, i, 1, NF, 0)
                        columns("g", f, i, 1, NF, 1)
                        block_in("u", f, i, 1, NF)
                        columns("u", f, i, 1, NF, 0)
                        columns("u", f, i, 1, NF, 1)
                        down(f, i, 1, NF, 1)
                    down(f, NF - 1, NF - 1, NF)
                if part[0] == "hyb":
                    mm_f = nc.tensor.matmul

                    def hgrn_step(i, lo, hi, steps):
                        tokens("hv", i, lo, hi)
                        for what, k in steps:
                            if what == "L":
                                b = free(lambda x: ("hL", 0, x, k), i, lo, hi)
                                pe.wait_ge(lx_ready, affine(lambda x: 14 * x + k + 1, i, lo, hi))
                                for c in range(TC):
                                    r = slice(c * P, (c + 1) * P)
                                    x = lx[:, k % 2, r]
                                    mm = mm_f(b[:, r], lx2[:, r] if k % 7 == 6 else x, x, start=True, stop=True)
                                mm.then_inc(tile_done, 1)
                            if what == "K":
                                b = free(lambda x: ("hK", 0, x, k), i, lo, hi)
                                pe.wait_ge(qk_ready, affine(lambda x: 2 * x + k + 1, i, lo, hi))
                                for c in range(TC):
                                    r = slice(c * P, (c + 1) * P)
                                    mm = nc.tensor.transpose(b[:, r], khT[:, r], ident[:])
                                mm.then_inc(tile_done, 1)
                            if what == "U":
                                b = free(lambda x: ("hU", 0, x, k), i, lo, hi)
                                pe.wait_ge(tile_read, affine(lambda x: TL.n[("hK", 0, x, k)] + 1, i, lo, hi))
                                for c in range(TC - 1):
                                    mm = mm_f(b[:, c * P:(c + 1) * P], kh[:, c, :], vv[:, c, k * P:(k + 1) * P], start=True, stop=True)
                                mm.then_inc(tile_done, 1)
                            if what == "O":
                                b = free(lambda x: ("hO", 0, x, k), i, lo, hi)
                                pe.wait_ge(tile_read, affine(lambda x: TL.n[("hL", 0, x, 7 * k + 6)] + 1, i, lo, hi))
                                for c in range(TC):
                                    r = slice(c * P, (c + 1) * P)
                                    mm = mm_f(b[:, r], sc[:, k, c, :], vv[:, c, k * P:(k + 1) * P], start=True, stop=c == 0)
                                    if c:
                                        mm = mm_f(b[:, r], qhat[:, k, r], st[:, k, c - 1, :], start=False, stop=True)
                                mm.then_inc(tile_done, 1)
                            if what == "N":
                                b = free(lambda x: ("hN", 0, x, k), i, lo, hi)
                                pe.wait_ge(on_ready, affine(lambda x: 2 * x + k + 1, i, lo, hi))
                                for c in range(TC):
                                    r = slice(c * P, (c + 1) * P)
                                    mm = nc.tensor.transpose(b[:, r], osb[:, k, r], ident[:])
                                mm.then_inc(tile_done, 1)
                            if what == "hg":
                                if k == 0:
                                    block_in("hg", 0, i, lo, hi)
                                columns("hg", 0, i, lo, hi, k)
                            if what == "hd":
                                down(0, i, lo, hi, 1, "hd", k)
                            if what == "hf":
                                if k == 0:
                                    block_in("hf", 0, i, lo, hi, -1)
                                columns("hf", 0, i, lo, hi, k, None, -1)
                            if what == "hq":
                                if k == 0:
                                    block_in("hq", 0, i, lo, hi, -1)
                                columns("hq", 0, i, lo, hi, k, None, -1)
                            if what == "sx":
                                if k == 0:
                                    block_in("sx", 0, 0, 0, 1)
                                columns("sx", 0, 0, 0, 1, k)

                    block_in("hf", 0, 0, 0, 1)
                    columns("hf", 0, 0, 0, 1, 0, n)
                    columns("hf", 0, 0, 0, 1, 1)
                    stat(n)
                    block_in("hq", 0, 0, 0, 1)
                    columns("hq", 0, 0, 0, 1, 0)
                    columns("hq", 0, 0, 0, 1, 1)
                    small_logits("dlog", dsh, dsl)
                    tokens_first("dlogT", "dlog")
                    rms_by_token("hrt")
                    hgrn_step(0, 0, 1, hgrn_steps(0))
                    with pe.Fori(1, NQ - 1) as i:
                        hgrn_step(i, 1, NQ - 1, hgrn_steps(1))
                    hgrn_step(NQ - 1, NQ - 1, NQ, hgrn_steps(NQ - 1))
                    block_in("sb", 0, 0, 0, 1)
                    columns("sb", 0, 0, 0, 1, 0)
                    columns("sb", 0, 0, 0, 1, 1)
                    b = free(lambda x: ("cst",), 0, 0, 1)
                    pe.wait_ge(const_ready, 4)
                    pe.wait_ge(a_ready, 1)
                    mm_f(b[:, 0:TC * NH], causal[:], dtt[:, 0, :], start=True, stop=True)
                    mm_f(b[:, TC * NH:2 * TC * NH], after[:], dtt[:, 0, :], start=True, stop=True).then_inc(tile_done, 1)
                    b = free(lambda x: ("csh",), 0, 0, 1)
                    for c in range(TC):
                        mm = mm_f(b[0:NH, c * P:(c + 1) * P], dtt[:, 0, c * NH:(c + 1) * NH], causal[:], start=True, stop=True)
                    mm.then_inc(tile_done, 1)
                    down(0, NQ, NQ, NQ + 1, 1, "hd")
                    pe.wait_ge(yy_zero, 1)
                    pe.wait_ge(tile_read, TL.n[("hd", 0, NQ - 1, KD - 1)] + 1)
                    mm_f(banks[7][:], ones[:], yy[:, KD - 1, :], start=True, stop=False)

                    def ssd_step(i, lo, hi, steps):
                        for what, k in steps:
                            if what == "sz":
                                if k == 0:
                                    block_in("sz", 0, i, lo, hi)
                                elif not (isinstance(i, int) and i == 0):
                                    y_squares(1, i, lo, hi, 1)
                                columns("sz", 0, i, lo, hi, k)
                            if what in ("sx", "sb"):
                                if k == 0:
                                    block_in(what, 0, i, lo, hi, -1)
                                columns(what, 0, i, lo, hi, k, None, -1)
                            if what == "sX":
                                b = free(lambda x: ("sX", 0, x, k), i, lo, hi)
                                pe.wait_ge(xc_ready, affine(lambda x: 4 * x + 4, i, lo, hi))
                                for c in range(2):
                                    for m in range(2):
                                        r = slice((2 * k + c) * P, (2 * k + c + 1) * P)
                                        mm = nc.tensor.transpose(b[:, c * CB + m * P:c * CB + (m + 1) * P], xc[:, m, r], ident[:])
                                mm.then_inc(tile_done, 1)
                            if what == "sB":
                                b = free(lambda x: ("sB", 0, x, k), i, lo, hi)
                                pe.wait_ge(xc_ready, affine(lambda x: 4 * x + 2, i, lo, hi))
                                for c in range(TC):
                                    r = slice(c * P, (c + 1) * P)
                                    mm = nc.tensor.transpose(b[:, r], xc[:, 2, r], ident[:])
                                mm.then_inc(tile_done, 1)
                            if what == "sC":
                                b = free(lambda x: ("sC", 0, x, k), i, lo, hi)
                                for c in range(TC):
                                    r = slice(c * P, (c + 1) * P)
                                    mm = mm_f(b[:, r], xc[:, 2, r], xc[:, 3, r], start=True, stop=True)
                                mm.then_inc(tile_done, 1)
                            if what == "sR":
                                b = free(lambda x: ("sR", 0, x, k), i, lo, hi)
                                pe.wait_ge(csg_in, affine(lambda x: 16 * x + 16, i, lo, hi))
                                mm_f(b[:], sel[:, k, :], csg[:], start=True, stop=True).then_inc(tile_done, 1)
                            if what == "sU":
                                b = free(lambda x: ("sU", 0, x, k), i, lo, hi)
                                pe.wait_ge(xdd_ready, affine(lambda x: 2 * x + 2, i, lo, hi))
                                pe.wait_ge(tile_read, affine(lambda x: TL.n[("sB", 0, x, 0)] + 1, i, lo, hi))
                                for c in range(2 - k):
                                    mm = mm_f(b[:, c * CB:(c + 1) * CB], bt[:, 2 * k + c, :], xdd4[:, 2 * k + c, :], start=True, stop=True)
                                mm.then_inc(tile_done, 1)
                            if what == "sY":
                                b = free(lambda x: ("sY", 0, x, k), i, lo, hi)
                                pe.wait_ge(mc_ready, affine(lambda x: 4 * x + 2 * k + 2, i, lo, hi))
                                pe.wait_ge(st_ready, affine(lambda x: 2 * x + k + 1, i, lo, hi))
                                for e in range(2):
                                    h = 2 * k + e
                                    o = slice(e * SP_, (e + 1) * SP_)
                                    f = slice(h * SP_, (h + 1) * SP_)
                                    for c in range(TC):
                                        r = slice(c * P, (c + 1) * P)
                                        mm = mm_f(b[o, r], xdt4[:, c, f], mm_[:, e, r], start=True, stop=c == 0)
                                        if c:
                                            mm = mm_f(b[o, r], ub[:, c - 1, f], cx[:, e, r], start=False, stop=True)
                                mm.then_inc(tile_done, 1)
                                if k == 1:
                                    y_squares(0, i, lo, hi)

                    def y_squares(m, i, lo, hi, shift=0):
                        pe.wait_ge(ysq_ready, affine(lambda x: 2 * (x - shift) + m + 1, i, lo, hi))
                        mm_f(banks[7][:], ones[:], ysq[:, m, :], start=False,
                             stop=isinstance(i, int) and i - shift == G4 - 1 and m == 1).then_inc(ystat_done, 1)
                    ssd_step(0, 0, 1, ssd_steps(0))
                    with pe.Fori(1, G4 - 1) as i:
                        ssd_step(i, 1, G4 - 1, ssd_steps(1))
                    ssd_step(G4 - 1, G4 - 1, G4, ssd_steps(G4 - 1))
                    y_squares(1, G4, G4, G4 + 1, 1)
                    for j in range(NQ):
                        s = block_in("so", 0, j, j, j + 1)
                        for m in range(2):
                            b = free(lambda x: ("so", 0, j, m), 0, 0, 1)
                            for k in range(KD):
                                if j == 0 and m == 0:
                                    pe.wait_ge(yu_ready, k + 1)
                                c = slice(k * CB + m * P, k * CB + (m + 1) * P)
                                mm = product(b[:], wh[s][:, c], wl[s][:, c], uh[:, k, :], ul[:, k, :], k == 0, k == KD - 1)
                            mm.then_inc(tile_done, 1)
                if part[0] == "fox":
                    def fox_step(i, lo, hi):
                        peeled = isinstance(i, int)
                        if not peeled:
                            block_in("fq", 0, i, lo, hi)
                            columns("fq", 0, i, lo, hi, 0)
                            columns("fq", 0, i, lo, hi, 1)
                            outputs(i, lo, hi)
                        block_in("fk", 0, i, lo, hi)
                        columns("fk", 0, i, lo, hi, 0)
                        if peeled:
                            small_logits("flog", fsh, fsl)
                        columns("fk", 0, i, lo, hi, 1)
                        if peeled:
                            tokens_first("flogT", "flog")
                            rms_by_token("frt")
                        else:
                            down(0, i, lo, hi, 1, "fd")
                        tokens("fv", i, lo, hi, 0)
                        if peeled:
                            b = free(lambda x: ("fcum",), 0, 0, 1)
                            pe.wait_ge(const_ready, 4)
                            pe.wait_ge(flog_ready, 1)
                            for c in range(TC):
                                for k in range(c + 1):
                                    mm = nc.tensor.matmul(b[0:NH, c * P:(c + 1) * P], ftmp[:, 0, k * NH:(k + 1) * NH],
                                                          causal[:] if k == c else ones[:], start=k == 0, stop=k == c)
                            mm.then_inc(tile_done, 1)
                        tokens("fv", i, lo, hi, 1)
                        pe.wait_ge(tile_read, affine(lambda x: TL.n[("fv", 0, x, 1)] + 1, i, lo, hi))
                        pe.wait_ge(aug_in, affine(lambda x: 64 * (x + 1), i, lo, hi))
                        for what, h in FOX_STEPS:
                            if what == "S":
                                for c in range(TC):
                                    scores(i, lo, hi, h, c)
                            if what == "T":
                                pe.wait_ge(exp_done, affine(lambda x: x * HPB * TC + (h + 1) * TC, i, lo, hi))
                                for m in range(3):
                                    b = free(lambda x: ("fT", 0, x, h, m), i, lo, hi)
                                    for k, (at, col) in PT_AT.items():
                                        for c in range(k, TC):
                                            if at == m:
                                                mm = nc.tensor.transpose(
                                                    b[:, col + (c - k) * P:col + (c - k + 1) * P],
                                                    pr[h % 2][:, c, k * P:(k + 1) * P], ident[:])
                                    mm.then_inc(tile_done, 1)
                            if what == "V":
                                pe.wait_ge(tile_read, affine(lambda x: TL.n[("fT", 0, x, h, 2)] + 1, i, lo, hi))
                                b = free(lambda x: ("fV", 0, x, h), i, lo, hi)
                                for c in range(TC):
                                    for k in range(c + 1):
                                        at, col = PT_AT[k]
                                        col += (c - k) * P
                                        mm = nc.tensor.matmul(b[:, c * HD:(c + 1) * HD], pt[h % 2][:, at, col:col + P],
                                                              vt[:, k, h * HD:(h + 1) * HD], start=k == 0, stop=k == c)
                                mm.then_inc(tile_done, 1)

                    def scores(i, lo, hi, h, c):
                        w, b = (c + 1) * P, banks[4 + c]
                        j = h * TC + c
                        if not (isinstance(i, int) and h == 0):
                            pe.wait_ge(exp_done, affine(lambda x: x * HPB * TC + j + 1 - TC, i, lo, hi))
                        nc.tensor.matmul(b[:, 0:w], qx[:, h, c * P:w], kx[:, h, 0:w], start=True, stop=False)
                        nc.tensor.matmul(b[:, c * P:w], identb[:], maskb[:], start=False, stop=True).then_inc(s_done, 1)

                    def outputs(i, lo, hi):
                        pe.wait_ge(tile_read, affine(lambda x: TL.n[("fV", 0, x - 1, HPB - 1)] + 1, i, lo, hi))
                        for m in range(2):
                            b = free(lambda x: ("fo", 0, x - 1, m), i, lo, hi)
                            for c in range(TC):
                                mm = nc.tensor.transpose(b[:, c * P:(c + 1) * P], ot[:, c, m * P:(m + 1) * P], ident[:])
                            mm.then_inc(tile_done, 1)

                    block_in("fq", 0, 0, 0, 1)
                    columns("fq", 0, 0, 0, 1, 0, n)
                    columns("fq", 0, 0, 0, 1, 1)
                    stat(n)
                    fox_step(0, 0, 1)
                    with pe.Fori(1, NQ) as i:
                        fox_step(i, 1, NQ)
                    outputs(NQ, NQ, NQ + 1)
                    down(0, NQ, NQ, NQ + 1, 1, "fd")
            n = len(parts)
            for c in range(TC):
                for h in range(2):
                    if c == 0:
                        pe.wait_ge(u_ready, n * KD + (h + 1) * KD // 2)
                    if c == 1 and h == 0:
                        pe.wait_ge(sum_ready, n + 1)
                        for k in range(TC):
                            mm = nc.tensor.matmul(stat_bank[:, k:k + 1], sq[:, 0, k * P:(k + 1) * P], ones[:, 0:1],
                                                  start=True, stop=True)
                        mm.then_inc(stat_done, 1)
                    b = free(lambda x: ("out", 2 * c + h), 0, 0, 1)
                    for j in range(4):
                        mm = nc.tensor.transpose(b[:, j * P:(j + 1) * P], xg[:, 4 * h + j, c * P:(c + 1) * P], ident[:])
                    mm.then_inc(tile_done, 1)


_INS = ["x", "ffn1_norm", "ffn1_w_gate", "ffn1_w_up", "ffn1_w_down", "mix_norm", "hyb_w_in", "hgrn_lb_logits",
        "hgrn_out_gain", "ssd_conv_w", "ssd_conv_b", "ssd_dt_bias", "ssd_A_log", "ssd_D", "ssd_out_gain", "hyb_w_out",
        "fox_w_in", "fox_b_f", "fox_w_out", "ffn2_norm", "ffn2_w_gate", "ffn2_w_up", "ffn2_w_down", "final_norm"]


def kernel(**inputs):
    import concourse.bacc as _bacc
    from concourse.bass_utils import run_bass_kernel_spmd as _run

    nc = _bacc.Bacc("TRN2", target_bir_lowering=False, num_devices=1)
    arrays, aps = {}, {}
    for name in _INS:
        a = np.ascontiguousarray(inputs[name])
        arrays[f"in_{name}_dram"] = a
        aps[name] = nc.dram_tensor(f"in_{name}_dram", a.shape, mybir.dt.from_np(a.dtype), kind="ExternalInput").ap()
    out = nc.dram_tensor("out_0_dram", (1, T, D), F32, kind="ExternalOutput").ap()
    trunk(nc, aps, out, [("ffn", 0), ("hyb",), ("ffn", 1), ("ffn", 2), ("fox",), ("ffn", 3)])
    r = _run(nc, [arrays], core_ids=[0])
    return r.results[0]["out_0_dram"]
```
